# Optimizing a Trainium2 kernel written in Bass

```python
import math
import jax, jax.numpy as jnp
from jax import lax
import numpy as np

D_MODEL = 1024
BATCH = 1
SEQ = 256
DEPTH = 1

HEAD_DIM = 64
N_HEADS_FOX = 8
N_HEADS_DIL = 8
D_FOX = N_HEADS_FOX * HEAD_DIM
D_DIL = N_HEADS_DIL * HEAD_DIM
D_MIX = D_FOX + D_DIL
D_PROJ = 3 * D_FOX + 3 * D_DIL + N_HEADS_FOX
DIL_PATTERNS = ((128, 1), (512, 4), (2048, 16))
BLOCK = 128
ROPE_THETA = 10000.0
N_GROUPS = 4
EXPERTS_PER_GROUP = 8
N_EXPERTS = N_GROUPS * EXPERTS_PER_GROUP
TOP_K_INNER = 2
D_EXPERT = 512
EPS = 1e-6
NEG = -1e30
FORGET_BIAS_INIT = 3.0


def rmsnorm(x, g):
    xf = x.astype(jnp.float32)
    y = xf * lax.rsqrt(jnp.mean(xf * xf, axis=-1, keepdims=True) + EPS)
    return (y * g.astype(jnp.float32)).astype(x.dtype)

def rope(x, pos):
    dh = x.shape[-1]
    inv_freq = 1.0 / (ROPE_THETA ** (jnp.arange(0, dh, 2, dtype=jnp.float32) / dh))
    ang = pos[:, None] * inv_freq[None, :]
    cos, sin = jnp.cos(ang), jnp.sin(ang)
    xf = x.astype(jnp.float32)
    x1, x2 = xf[..., : dh // 2], xf[..., dh // 2:]
    out = jnp.concatenate([x1 * cos - x2 * sin, x2 * cos + x1 * sin], axis=-1)
    return out.astype(x.dtype)

def forgetting_attention(q, k, v, logf):
    B, H, S, dh = q.shape
    scale = 1.0 / math.sqrt(dh)
    c = jnp.cumsum(logf, axis=-1)
    nb = S // BLOCK
    qb = q.reshape(B, H, nb, BLOCK, dh).transpose(2, 0, 1, 3, 4)
    cb = c.reshape(B, H, nb, BLOCK).transpose(2, 0, 1, 3)
    kpos = jnp.arange(S)

    def one_block(args):
        qi, ci, i = args
        s = jnp.einsum('bhqd,bhkd->bhqk', qi, k).astype(jnp.float32) * scale
        s = s + ci[..., None] - c[:, :, None, :]
        qpos = i * BLOCK + jnp.arange(BLOCK)
        mask = kpos[None, :] <= qpos[:, None]
        s = jnp.where(mask, s, NEG)
        p = jax.nn.softmax(s, axis=-1)
        return jnp.einsum('bhqk,bhkd->bhqd', p.astype(v.dtype), v)

    out = lax.map(one_block, (qb, cb, jnp.arange(nb)))
    return out.transpose(1, 2, 0, 3, 4).reshape(B, H, S, dh)

def dilated_branch(q, k, v, window, dilation):
    B, H, S, dh = q.shape
    scale = 1.0 / math.sqrt(dh)
    wsub = window // dilation
    unit = dilation * BLOCK
    Sp = -(-S // unit) * unit
    L = Sp // dilation
    nb = L // BLOCK
    pad = ((0, 0), (0, 0), (0, Sp - S), (0, 0))

    def split(t):
        t = jnp.pad(t, pad).reshape(B, H, L, dilation, dh).transpose(0, 1, 3, 2, 4)
        return t.reshape(B, H, dilation, nb, BLOCK, dh)

    def with_prev(t):
        prev = jnp.pad(t, ((0, 0), (0, 0), (0, 0), (1, 0), (0, 0), (0, 0)))[:, :, :, :-1]
        return jnp.concatenate([prev, t], axis=4)

    qs = split(q)
    kw = with_prev(split(k))
    vw = with_prev(split(v))
    s = jnp.einsum('bhrnqd,bhrnkd->bhrnqk', qs, kw).astype(jnp.float32) * scale
    ql = jnp.arange(BLOCK)[:, None]
    kl = jnp.arange(2 * BLOCK)[None, :]
    dist = ql + BLOCK - kl
    kpos = jnp.arange(nb)[:, None, None] * BLOCK + kl[None] - BLOCK
    valid = (dist >= 0) & (dist <= wsub) & (kpos >= 0)
    s = jnp.where(valid, s, NEG)
    m = jnp.max(s, axis=-1, keepdims=True)
    p = jnp.exp(s - m)
    l = jnp.sum(p, axis=-1, keepdims=True)
    o = jnp.einsum('bhrnqk,bhrnkd->bhrnqd', (p / l).astype(v.dtype), vw)
    lse = (m + jnp.log(l))[..., 0]
    o = o.reshape(B, H, dilation, L, dh).transpose(0, 1, 3, 2, 4).reshape(B, H, Sp, dh)[:, :, :S]
    lse = lse.reshape(B, H, dilation, L).transpose(0, 1, 3, 2).reshape(B, H, Sp)[:, :, :S]
    return o, lse

def dilated_attention(q, k, v):
    outs, lses = [], []
    for window, dilation in DIL_PATTERNS:
        o, lse = dilated_branch(q, k, v, window, dilation)
        outs.append(o)
        lses.append(lse)
    w = jax.nn.softmax(jnp.stack(lses, axis=0), axis=0)
    o = jnp.sum(w[..., None] * jnp.stack(outs, axis=0).astype(jnp.float32), axis=0)
    return o.astype(q.dtype)

def token_mixer(xn, w_in, b_forget, q_norm_fox, k_norm_fox, q_norm_dil, k_norm_dil,
                out_norm_fox, out_norm_dil, w_out):
    B, S, _ = xn.shape
    proj = xn @ w_in
    o1 = 3 * D_FOX
    o2 = o1 + 3 * D_DIL
    qa, ka, va = jnp.split(proj[..., :o1], 3, axis=-1)
    qb, kb, vb = jnp.split(proj[..., o1:o2], 3, axis=-1)
    fa = proj[..., o2:]

    def heads(t, h):
        return t.reshape(B, S, h, HEAD_DIM).transpose(0, 2, 1, 3)

    qa = rmsnorm(heads(qa, N_HEADS_FOX), q_norm_fox)
    ka = rmsnorm(heads(ka, N_HEADS_FOX), k_norm_fox)
    va = heads(va, N_HEADS_FOX)
    logf = jax.nn.log_sigmoid(fa.astype(jnp.float32) + b_forget.astype(jnp.float32))
    logf = logf.transpose(0, 2, 1)
    oa = forgetting_attention(qa, ka, va, logf)

    pos = jnp.arange(S, dtype=jnp.float32)
    qb = rope(rmsnorm(heads(qb, N_HEADS_DIL), q_norm_dil), pos)
    kb = rope(rmsnorm(heads(kb, N_HEADS_DIL), k_norm_dil), pos)
    vb = heads(vb, N_HEADS_DIL)
    ob = dilated_attention(qb, kb, vb)

    oa = rmsnorm(oa.transpose(0, 2, 1, 3).reshape(B, S, D_FOX), out_norm_fox)
    ob = rmsnorm(ob.transpose(0, 2, 1, 3).reshape(B, S, D_DIL), out_norm_dil)
    return jnp.concatenate([oa, ob], axis=-1) @ w_out

def hierarchical_moe(xn, w_router_group, b_router_group, w_router_expert, b_router_expert,
                     w_gate, w_up, w_down):
    B, S, D = xn.shape
    t = xn.reshape(B * S, D)
    zg = (t @ w_router_group).astype(jnp.float32) + b_router_group.astype(jnp.float32)
    pg = jax.nn.softmax(zg, axis=-1)
    pg_top, g_sel = lax.top_k(pg, 1)
    ze = jnp.einsum('td,gde->tge', t, w_router_expert).astype(jnp.float32)
    ze = ze + b_router_expert.astype(jnp.float32)
    ze_sel = jnp.take_along_axis(ze, g_sel[:, :, None], axis=1)[:, 0]
    v2, i2 = lax.top_k(ze_sel, TOP_K_INNER)
    gates = jax.nn.softmax(v2, axis=-1) * pg_top
    eid = g_sel * EXPERTS_PER_GROUP + i2
    combine = jnp.sum(jax.nn.one_hot(eid, N_EXPERTS, dtype=jnp.float32) * gates[..., None], axis=1)
    y = jnp.zeros((B * S, D), jnp.float32)
    for e in range(N_EXPERTS):
        h = jax.nn.silu(t @ w_gate[e]) * (t @ w_up[e])
        y = y + combine[:, e:e + 1] * (h @ w_down[e]).astype(jnp.float32)
    return y.astype(xn.dtype).reshape(B, S, D)

def first_inputs(seed: int = 0) -> dict:
    key = jax.random.key(seed)
    ks = jax.random.split(key, 20)
    f32 = jnp.float32

    def nrm(k, shape, scale):
        return jax.random.normal(k, shape, f32) * scale

    def gain(k, shape):
        return 1.0 + 0.02 * jax.random.normal(k, shape, f32)

    return {
        "x": jax.random.normal(ks[0], (BATCH, SEQ, D_MODEL), f32),
        "norm_mix": gain(ks[1], (DEPTH, D_MODEL)),
        "w_in": nrm(ks[2], (DEPTH, D_MODEL, D_PROJ), D_MODEL ** -0.5),
        "b_forget": FORGET_BIAS_INIT + 0.1 * jax.random.normal(ks[3], (DEPTH, N_HEADS_FOX), f32),
        "q_norm_fox": gain(ks[4], (DEPTH, HEAD_DIM)),
        "k_norm_fox": gain(ks[5], (DEPTH, HEAD_DIM)),
        "q_norm_dil": gain(ks[6], (DEPTH, HEAD_DIM)),
        "k_norm_dil": gain(ks[7], (DEPTH, HEAD_DIM)),
        "out_norm_fox": gain(ks[8], (DEPTH, D_FOX)),
        "out_norm_dil": gain(ks[9], (DEPTH, D_DIL)),
        "w_out": nrm(ks[10], (DEPTH, D_MIX, D_MODEL), D_MIX ** -0.5),
        "norm_ffn": gain(ks[11], (DEPTH, D_MODEL)),
        "w_router_group": nrm(ks[12], (DEPTH, D_MODEL, N_GROUPS), D_MODEL ** -0.5),
        "b_router_group": nrm(ks[13], (DEPTH, N_GROUPS), 0.01),
        "w_router_expert": nrm(ks[14], (DEPTH, N_GROUPS, D_MODEL, EXPERTS_PER_GROUP), D_MODEL ** -0.5),
        "b_router_expert": nrm(ks[15], (DEPTH, N_GROUPS, EXPERTS_PER_GROUP), 0.01),
        "w_gate": nrm(ks[16], (DEPTH, N_EXPERTS, D_MODEL, D_EXPERT), D_MODEL ** -0.5),
        "w_up": nrm(ks[17], (DEPTH, N_EXPERTS, D_MODEL, D_EXPERT), D_MODEL ** -0.5),
        "w_down": nrm(ks[18], (DEPTH, N_EXPERTS, D_EXPERT, D_MODEL), D_EXPERT ** -0.5),
    }

def first_block(x, norm_mix, w_in, b_forget, q_norm_fox, k_norm_fox, q_norm_dil, k_norm_dil,
              out_norm_fox, out_norm_dil, w_out, norm_ffn, w_router_group, b_router_group,
              w_router_expert, b_router_expert, w_gate, w_up, w_down):
    h = x
    for l in range(DEPTH):
        xn = rmsnorm(h, norm_mix[l])
        h = h + token_mixer(xn, w_in[l], b_forget[l], q_norm_fox[l], k_norm_fox[l],
                            q_norm_dil[l], k_norm_dil[l], out_norm_fox[l], out_norm_dil[l],
                            w_out[l])
        hn = rmsnorm(h, norm_ffn[l])
        h = h + hierarchical_moe(hn, w_router_group[l], b_router_group[l], w_router_expert[l],
                                 b_router_expert[l], w_gate[l], w_up[l], w_down[l])
    return h


DEPTH_2 = 2

GRID_W = 64
CTX_LEN = 256
N_DIFF_HEADS = 6
DIFF_HEAD_DIM = 64
DIFF_V_DIM = 2 * DIFF_HEAD_DIM
N_FOURIER_GROUPS = 4
FOURIER_GROUP_DIM = 64
ATTN_QK_W = N_DIFF_HEADS * 2 * DIFF_HEAD_DIM
ATTN_V_W = N_DIFF_HEADS * DIFF_V_DIM
FOURIER_W = N_FOURIER_GROUPS * FOURIER_GROUP_DIM
EVEN_IN_W = 2 * ATTN_QK_W + ATTN_V_W + FOURIER_W
EVEN_MIX_W = ATTN_V_W + FOURIER_W
CONV_K = 3
N_EXPERTS_2 = 16
EC_CAPACITY_FACTOR = 2
D_EXPERT_2 = 1024
ROPE_BASE = 10000.0
Q_BLOCK = 128
N_EVEN = (DEPTH_2 + 1) // 2
N_ODD = DEPTH_2 // 2


def rmsnorm_2(x, g):
    xf = x.astype(jnp.float32)
    y = xf * lax.rsqrt(jnp.mean(xf * xf, axis=-1, keepdims=True) + EPS)
    return (y * g.astype(jnp.float32)).astype(x.dtype)

def modulate(x, g, shift, scale):
    return rmsnorm_2(x, g) * (1 + scale) + shift

def ada_params(cond, w_ada, b_ada):
    m = jax.nn.silu(cond) @ w_ada + b_ada
    return jnp.split(m[..., None, :], 6, axis=-1)

def axial_rope(n, dtype):
    rows = n // GRID_W
    r = jnp.repeat(jnp.arange(rows, dtype=jnp.float32), GRID_W)
    col = jnp.tile(jnp.arange(GRID_W, dtype=jnp.float32), rows)
    n_freq = DIFF_HEAD_DIM // 4
    inv = ROPE_BASE ** (-jnp.arange(n_freq, dtype=jnp.float32) / n_freq)
    ar = r[:, None] * inv
    ac = col[:, None] * inv
    ang = jnp.concatenate([ar, ar, ac, ac], axis=-1)
    return jnp.cos(ang).astype(dtype), jnp.sin(ang).astype(dtype)

def apply_rope(x, cos, sin):
    x1, x2, x3, x4 = jnp.split(x, 4, axis=-1)
    rot = jnp.concatenate([-x2, x1, -x4, x3], axis=-1)
    return x * cos[None, :, None, None, :] + rot * sin[None, :, None, None, :]

def qk_heads(t):
    return t.reshape(t.shape[0], t.shape[1], N_DIFF_HEADS, 2, DIFF_HEAD_DIM)

def v_heads(t):
    return t.reshape(t.shape[0], t.shape[1], N_DIFF_HEADS, DIFF_V_DIM)

def diff_attend(q, k, v, lam):
    s = jnp.einsum('bqhmd,bkhmd->bhmqk', q, k).astype(jnp.float32)
    p = jax.nn.softmax(s, axis=-1)
    a = p[:, :, 0] - lam * p[:, :, 1]
    return jnp.einsum('bhqk,bkhe->bqhe', a.astype(v.dtype), v)

def blocked_diff_attend(q, k, v, lam):
    b, n = q.shape[0], q.shape[1]
    qb = q.reshape(b, n // Q_BLOCK, Q_BLOCK, N_DIFF_HEADS, 2, DIFF_HEAD_DIM).swapaxes(0, 1)
    out = lax.map(lambda qq: diff_attend(qq, k, v, lam), qb)
    return out.swapaxes(0, 1).reshape(b, n, N_DIFF_HEADS, DIFF_V_DIM)

def fourier_mix(f):
    b, n = f.shape[0], f.shape[1]
    fg = f.reshape(b, n, N_FOURIER_GROUPS, FOURIER_GROUP_DIM).astype(jnp.float32)
    y = jnp.fft.fft2(fg, axes=(1, 3), norm='ortho').real
    return y.reshape(b, n, FOURIER_W).astype(f.dtype)

def merge_even(att, f, subln, lam_init, w_out):
    b, n = att.shape[0], att.shape[1]
    att = rmsnorm_2(att, subln) * (1.0 - lam_init)
    o = jnp.concatenate([att.reshape(b, n, ATTN_V_W), fourier_mix(f)], axis=-1)
    return o @ w_out

def even_mixer(h, hc, w_in, q_norm, k_norm, lam, subln, w_out, lam_init, cos, sin, ctx_out):
    scale = DIFF_HEAD_DIM ** -0.5
    cuts = [ATTN_QK_W, 2 * ATTN_QK_W, 2 * ATTN_QK_W + ATTN_V_W]
    q, k, v, f = jnp.split(h @ w_in, cuts, axis=-1)
    q = apply_rope(rmsnorm_2(qk_heads(q), q_norm), cos, sin) * scale
    k = apply_rope(rmsnorm_2(qk_heads(k), k_norm), cos, sin)
    qc = None
    fc = None
    if ctx_out:
        qc, kc, vc, fc = jnp.split(hc @ w_in, cuts, axis=-1)
    else:
        kc, vc = jnp.split(hc @ w_in[:, ATTN_QK_W:2 * ATTN_QK_W + ATTN_V_W], [ATTN_QK_W], axis=-1)
    kc = rmsnorm_2(qk_heads(kc), k_norm)
    vc = v_heads(vc)
    keys = jnp.concatenate([k, kc], axis=1)
    vals = jnp.concatenate([v_heads(v), vc], axis=1)
    y = merge_even(blocked_diff_attend(q, keys, vals, lam), f, subln, lam_init, w_out)
    yc = None
    if ctx_out:
        qc = rmsnorm_2(qk_heads(qc), q_norm) * scale
        yc = merge_even(diff_attend(qc, kc, vc, lam), fc, subln, lam_init, w_out)
    return y, yc

def shortconv(z, w):
    zp = jnp.pad(z, ((0, 0), (1, 1), (0, 0)))
    return w[0] * zp[:, :-2] + w[1] * zp[:, 1:-1] + w[2] * zp[:, 2:]

def odd_mixer(h, w_in, conv_w, w_out):
    bg, cg, u = jnp.split(h @ w_in, 3, axis=-1)
    return (bg * shortconv(cg * u, conv_w)) @ w_out

def ec_moe(h, w_router, w_gate, w_up, w_down):
    b, n, d = h.shape
    cap = EC_CAPACITY_FACTOR * n // N_EXPERTS_2
    aff = jax.nn.softmax(h.astype(jnp.float32) @ w_router.astype(jnp.float32), axis=-1)
    g, idx = lax.top_k(aff.swapaxes(1, 2), cap)
    xs = jax.vmap(lambda hb, ib: hb[ib])(h, idx)
    a = jax.nn.silu(jnp.einsum('becd,edf->becf', xs, w_gate)) * jnp.einsum('becd,edf->becf', xs, w_up)
    y = jnp.einsum('becf,efd->becd', a, w_down) * g[..., None].astype(h.dtype)
    return jax.vmap(lambda yb, ib: jnp.zeros((n, d), yb.dtype).at[ib.reshape(-1)].add(yb.reshape(-1, d)))(y, idx)

def second_inputs(seed: int = 0) -> dict:
    key = jax.random.key(seed)
    ks = jax.random.split(key, 24)

    def nrm(k, shape, s):
        return jax.random.normal(k, shape, jnp.float32) * s

    D = D_MODEL
    return {
        'x': nrm(ks[0], (BATCH, SEQ, D), 1.0),
        'c': nrm(ks[1], (BATCH, D), 1.0),
        'ctx': nrm(ks[2], (BATCH, CTX_LEN, D), 1.0),
        'c_ctx': nrm(ks[3], (D,), 1.0),
        'ada_w': nrm(ks[4], (DEPTH_2, D, 6 * D), 0.5 * D ** -0.5),
        'ada_b': nrm(ks[5], (DEPTH_2, 6 * D), 0.02),
        'norm_mix': 1.0 + nrm(ks[6], (DEPTH_2, D), 0.02),
        'norm_ffn': 1.0 + nrm(ks[7], (DEPTH_2, D), 0.02),
        'attn_w_in': nrm(ks[8], (N_EVEN, D, EVEN_IN_W), D ** -0.5),
        'attn_q_norm': 1.0 + nrm(ks[9], (N_EVEN, DIFF_HEAD_DIM), 0.02),
        'attn_k_norm': 1.0 + nrm(ks[10], (N_EVEN, DIFF_HEAD_DIM), 0.02),
        'lam_q1': nrm(ks[11], (N_EVEN, DIFF_HEAD_DIM), 0.1),
        'lam_k1': nrm(ks[12], (N_EVEN, DIFF_HEAD_DIM), 0.1),
        'lam_q2': nrm(ks[13], (N_EVEN, DIFF_HEAD_DIM), 0.1),
        'lam_k2': nrm(ks[14], (N_EVEN, DIFF_HEAD_DIM), 0.1),
        'attn_subln': 1.0 + nrm(ks[15], (N_EVEN, DIFF_V_DIM), 0.02),
        'attn_w_out': nrm(ks[16], (N_EVEN, EVEN_MIX_W, D), EVEN_MIX_W ** -0.5),
        'conv_w_in': nrm(ks[17], (N_ODD, D, 3 * D), D ** -0.5),
        'conv_w': nrm(ks[18], (N_ODD, CONV_K, D), CONV_K ** -0.5),
        'conv_w_out': nrm(ks[19], (N_ODD, D, D), D ** -0.5),
        'router_w': nrm(ks[20], (DEPTH_2, D, N_EXPERTS_2), D ** -0.5),
        'moe_w_gate': nrm(ks[21], (DEPTH_2, N_EXPERTS_2, D, D_EXPERT_2), D ** -0.5),
        'moe_w_up': nrm(ks[22], (DEPTH_2, N_EXPERTS_2, D, D_EXPERT_2), D ** -0.5),
        'moe_w_down': nrm(ks[23], (DEPTH_2, N_EXPERTS_2, D_EXPERT_2, D), D_EXPERT_2 ** -0.5),
    }

def second_block(x, c, ctx, c_ctx, ada_w, ada_b, norm_mix, norm_ffn,
              attn_w_in, attn_q_norm, attn_k_norm, lam_q1, lam_k1, lam_q2, lam_k2,
              attn_subln, attn_w_out, conv_w_in, conv_w, conv_w_out,
              router_w, moe_w_gate, moe_w_up, moe_w_down):
    cos, sin = axial_rope(x.shape[1], x.dtype)
    xc = ctx
    for l in range(DEPTH_2):
        ctx_out = any(j % 2 == 0 for j in range(l + 1, DEPTH_2))
        ctx_in = (l % 2 == 0) or ctx_out
        sh_m, sc_m, g_m, sh_f, sc_f, g_f = ada_params(c, ada_w[l], ada_b[l])
        h = modulate(x, norm_mix[l], sh_m, sc_m)
        hc = None
        cg_m = cg_f = csh_f = csc_f = None
        if ctx_in:
            csh_m, csc_m, cg_m, csh_f, csc_f, cg_f = ada_params(c_ctx, ada_w[l], ada_b[l])
            hc = modulate(xc, norm_mix[l], csh_m, csc_m)
        if l % 2 == 0:
            e = l // 2
            lam_init = 0.8 - 0.6 * math.exp(-0.3 * l)
            lam = (jnp.exp(jnp.sum(lam_q1[e].astype(jnp.float32) * lam_k1[e].astype(jnp.float32)))
                   - jnp.exp(jnp.sum(lam_q2[e].astype(jnp.float32) * lam_k2[e].astype(jnp.float32)))
                   + lam_init)
            y, yc = even_mixer(h, hc, attn_w_in[e], attn_q_norm[e], attn_k_norm[e], lam,
                               attn_subln[e], attn_w_out[e], lam_init, cos, sin, ctx_out)
        else:
            o = l // 2
            y = odd_mixer(h, conv_w_in[o], conv_w[o], conv_w_out[o])
            yc = odd_mixer(hc, conv_w_in[o], conv_w[o], conv_w_out[o]) if ctx_out else None
        x = x + g_m * y
        x = x + g_f * ec_moe(modulate(x, norm_ffn[l], sh_f, sc_f),
                             router_w[l], moe_w_gate[l], moe_w_up[l], moe_w_down[l])
        if ctx_out:
            xc = xc + cg_m * yc
            xc = xc + cg_f * ec_moe(modulate(xc, norm_ffn[l], csh_f, csc_f),
                                    router_w[l], moe_w_gate[l], moe_w_up[l], moe_w_down[l])
    return x


def setup_inputs(seed=0):
    out = dict(first_inputs(seed))
    for name, value in second_inputs(seed + 1).items():
        if name != "x":
            out[name + "_2"] = value
    return out


def reference(
    x, norm_mix, w_in, b_forget, q_norm_fox, k_norm_fox, q_norm_dil, k_norm_dil, out_norm_fox,
    out_norm_dil, w_out, norm_ffn, w_router_group, b_router_group, w_router_expert,
    b_router_expert, w_gate, w_up, w_down, c_2, ctx_2, c_ctx_2, ada_w_2, ada_b_2, norm_mix_2,
    norm_ffn_2, attn_w_in_2, attn_q_norm_2, attn_k_norm_2, lam_q1_2, lam_k1_2, lam_q2_2,
    lam_k2_2, attn_subln_2, attn_w_out_2, conv_w_in_2, conv_w_2, conv_w_out_2, router_w_2,
    moe_w_gate_2, moe_w_up_2, moe_w_down_2,
):
    x = first_block(
        x, norm_mix, w_in, b_forget, q_norm_fox, k_norm_fox, q_norm_dil, k_norm_dil,
        out_norm_fox, out_norm_dil, w_out, norm_ffn, w_router_group, b_router_group,
        w_router_expert, b_router_expert, w_gate, w_up, w_down,
    )
    return second_block(
        x, c_2, ctx_2, c_ctx_2, ada_w_2, ada_b_2, norm_mix_2, norm_ffn_2, attn_w_in_2,
        attn_q_norm_2, attn_k_norm_2, lam_q1_2, lam_k1_2, lam_q2_2, lam_k2_2, attn_subln_2,
        attn_w_out_2, conv_w_in_2, conv_w_2, conv_w_out_2, router_w_2, moe_w_gate_2, moe_w_up_2,
        moe_w_down_2,
    )


_drawn_inputs = setup_inputs


def setup_inputs(seed=0):
    import zlib

    import numpy as np

    out = dict(_drawn_inputs(seed))
    spreads = {}
    factors = {'q_norm_fox': 4.823,
     'k_norm_fox': 3.163,
     'q_norm_dil': 2.936,
     'k_norm_dil': 3.381,
     'out_norm_fox': 2.724,
     'out_norm_dil': 3.616,
     'b_router_group': 8.0,
     'b_router_expert': 4.656,
     'norm_mix_2': 5.848,
     'norm_ffn_2': 6.842,
     'attn_q_norm_2': 8.0,
     'attn_k_norm_2': 8.0,
     'lam_q1_2': 3.204,
     'lam_k1_2': 3.01,
     'lam_q2_2': 4.155,
     'lam_k2_2': 3.607,
     'attn_subln_2': 8.0}
    for name, (base, spread) in spreads.items():
        noise = np.random.default_rng([zlib.crc32(name.encode()), seed]).standard_normal(out[name].shape)
        drawn = base * np.exp(spread * noise) if base else spread * noise
        out[name] = __import__('jax').numpy.asarray(drawn.astype(out[name].dtype))
    for name, factor in factors.items():
        out[name] = (out[name] * factor).astype(out[name].dtype)
    return out
```

```python
from contextlib import ExitStack

import numpy as np

import concourse.bass as bass
from concourse import mybir

F32 = mybir.dt.float32
I32 = mybir.dt.int32
ALU = mybir.AluOpType
ACT = mybir.ActivationFunctionType
AX = mybir.AxisListType

P = 128
S = 256
T = S // P
D = 1024
KD = D // P
NC = 512
HD = 64
EPS = 1e-6
NEG = -1e30
SLOTS = 6
C = 32
E1, E2 = 32, 16
EP = 16
G1 = 4
PC = 7
ARENA = 12288
LAM_INIT = 0.8 - 0.6


class Mixture:

    def __init__(self, steps, nf, nd, arrived, done, first, done0, k0, scale, shift, gate):
        self.nf, self.nd, self.per = nf, nd, 2 * nf + nd
        self.arrived, self.done = arrived, done
        self.first, self.done0, self.k0 = first, done0, k0
        self.scale, self.shift, self.gate = scale, shift, gate
        (self.sel, self.wsel, self.gathered, self.xg_act, self.xg_dve, self.xs, self.ws, self.g_copied, self.u_copied,
         self.turned, self.silu, self.act, self.z0, self.z1, self.w_turned, self.wT, self.y, self.y_added) = steps


def rope_tables(ang, half):
    sign = np.where((np.arange(HD) // half) % 2 == 0, -1.0, 1.0)
    return np.cos(ang), np.sin(ang) * sign


def constants():
    p = np.arange(P)
    blocks = lambda a: a.reshape(T, P, -1).transpose(1, 0, 2).reshape(P, -1)
    q, k = np.arange(S)[:, None], np.arange(S)[None, :]
    d = q - k
    causal = np.where(d >= 0, 0.0, NEG)
    count = sum(((d >= 0) & (d % r == 0) & (d // r <= P)).astype(np.float64) for r in (1, 4, 16))
    dilated = np.where(count > 0, np.log(np.maximum(count, 1.0)), NEG)
    pos = np.arange(S, dtype=np.float32)
    inv = (1.0 / (np.float32(10000.0) ** (np.arange(0, HD, 2, dtype=np.float32) / np.float32(HD)))).astype(np.float32)
    a1 = pos[:, None] * inv[None, :]
    cos1, sin1 = rope_tables(np.concatenate([a1, a1], 1), HD // 2)
    nf = HD // 4
    inv2 = (np.float32(10000.0) ** (-np.arange(nf, dtype=np.float32) / np.float32(nf))).astype(np.float32)
    ar = np.floor(pos / HD).astype(np.float32)[:, None] * inv2
    ac = (pos % HD).astype(np.float32)[:, None] * inv2
    cos2, sin2 = rope_tables(np.concatenate([ar, ar, ac, ac], 1), nf)
    ws = 2 * np.pi * ((np.arange(S)[:, None] * np.arange(S)) % S) / S
    wd = 2 * np.pi * ((np.arange(HD)[:, None] * np.arange(HD)) % HD) / HD
    two = np.eye(2)
    parts = {
        "ident": np.eye(P), "before": p[:, None] < p[None, :], "ones": np.ones((P, P)),
        "row0": np.repeat((p % 32 == 0)[:, None], P, 1),
        "rows": np.stack([p % 32 == 0, p % 32 == 1], 1),
        "stack": p[:, None] % C == np.arange(C)[None, :],
        "iota": np.repeat(np.arange(C)[None, :], P, 0),
        "causal0": causal[:P, :P], "causal1": causal[P:, :],
        "dilated0": dilated[:P, :P], "dilated1": dilated[P:, :],
        "cos1": blocks(cos1), "sin1": blocks(sin1), "cos2": blocks(cos2), "sin2": blocks(sin2),
        "chan": np.concatenate([np.kron(two, np.cos(wd)), np.kron(two, np.sin(wd))], 1),
        "dftc": blocks(np.cos(ws) / np.sqrt(S * HD)), "dfts": blocks(-np.sin(ws) / np.sqrt(S * HD)),
    }
    at, cols = {}, 0
    for name, a in parts.items():
        at[name] = (cols, a.shape[1])
        cols += a.shape[1]
    return at, np.concatenate([a.astype(np.float32) for a in parts.values()], 1)


CONST_AT, CONST = constants()

COLS = ["norm_mix", "norm_ffn", "out_norm", "norm_mix0", "norm_mix1", "norm_ffn0", "norm_ffn1", "subln", "c", "c_ctx",
        "b00", "b01", "b03", "b04", "b10", "b11", "b13", "b14", "conv0", "conv1", "conv2", "b_forget"]
ROWS = ["q_fox", "k_fox", "q_dil", "k_dil", "q_att", "k_att", "lam_q1", "lam_k1", "lam_q2", "lam_k2", "b_router"]
ROW_W = [HD] * 10 + [G1 + E1]
ROW_AT = dict(zip(ROWS, np.cumsum([0] + ROW_W[:-1]).tolist()))

SH_M, SC_M, G_M, SH_F, SC_F, G_F = range(6)
W_IN_COLS = {"qa": 0, "ka": 512, "va": 1024, "qb": 1536, "kb": 2048, "vb": 2560}
CHUNKS1 = ["qa", "ka", "qb", "kb", "va", "vb"]


def plan_items():
    items, at = [], {}
    for c, name in enumerate(CHUNKS1):
        at["proj1", c] = len(items)
        items.append(("w_in", W_IN_COLS[name]))
    for c in range(6):
        at["ada", c] = len(items)
        items += [("ada", 0, c * D + n * NC) for n in range(2)]
    at["out", 0] = len(items)
    items += [("w_out", n * NC) for n in range(2)]
    at["moe", 0] = len(items)
    items += [("moe",)] * (3 * E1)
    at["proj2"] = len(items)
    items += [("attn_w_in", n * NC) for n in range(5)]
    for c in range(6):
        at["ada", 6 + c] = len(items)
        items += [("ada", 1, c * D + n * NC) for n in range(2)]
    at["out", 1] = len(items)
    items += [("attn_w_out", n * NC) for n in range(2)]
    at["moe", 1] = len(items)
    items += [("moe",)] * (6 * E2)
    at["proj3"] = len(items)
    items += [("conv_w_in", s * D + n * NC) for n in range(2) for s in (1, 2, 0)]
    at["out", 2] = len(items)
    items += [("conv_w_out", n * NC) for n in range(2)]
    at["moe", 2] = len(items)
    items += [("moe",)] * (6 * E2)
    return items, at


def transformer_blocks(nc, x, ctx_in, w_in, w_out, w_gate, w_up, w_down, ada_w, ada_b, attn_w_in, attn_w_out,
                       conv_w_in, conv_w_out, moe_w_gate, moe_w_up, moe_w_down, router, const_in, cols_in, rows_in, out,
                       stop=None):
    items, ITEM = plan_items()
    stack = ExitStack()
    with stack:
        def sb(name, shape, dt=F32):
            return stack.enter_context(nc.sbuf_tensor(name, shape, dt))

        def sem(name):
            return stack.enter_context(nc.semaphore(name))

        bank = [stack.enter_context(nc.psum_tensor(f"bank{i}", [P, NC], F32)) for i in range(8)]

        ring = [sb(f"ring{i}", [P, KD, NC]) for i in range(SLOTS)]
        cb = sb("cb", [P, CONST.shape[1]])
        cols = sb("cols", [P, len(COLS), KD])
        rows = sb("rows", [P, sum(ROW_W)])
        router_sb = sb("router_sb", [P, KD, G1 + E1 + 2 * E2 + 8])
        h = sb("h", [P, T, D])
        xn = sb("xn", [P, T, D])
        hT = sb("hT", [P, KD, S])
        gate_rows = sb("gate_rows", [P, 2, 2, D])
        mod = sb("mod", [P, 2, 4, KD])
        mod_ctx = sb("mod_ctx", [P, 2, KD])
        condT = sb("condT", [P, KD, 32])
        zero_col = sb("zero_col", [P, 1])
        minus_half = sb("minus_half", [P, 8])
        small = sb("small", [P, 256])
        flag = sb("flag", [P, 1], I32)
        arena = sb("arena", [P, ARENA])
        arena_at = [0]

        def carve(*shape, at=None):
            n = int(np.prod(shape))
            if at is not None:
                arena_at[0] = at
            a = arena[:, arena_at[0]:arena_at[0] + n]
            arena_at[0] += n
            assert arena_at[0] <= ARENA, arena_at[0]
            if len(shape) == 2:
                return a.rearrange("p (a b) -> p a b", b=shape[1])
            if len(shape) == 3:
                return a.rearrange("p (a b c) -> p a b c", b=shape[1], c=shape[2])
            return a

        def const(name):
            a, n = CONST_AT[name]
            return cb[:, a:a + n]

        def row(name, n=HD):
            return rows[:, ROW_AT[name]:ROW_AT[name] + n]

        def col(name):
            return cols[:, COLS.index(name), :]

        ident = const("ident")

        arrived = [sem(f"arrived{i}") for i in range(SLOTS)]
        item_done = sem("item_done")

        done_at, released, n_done = {}, {}, 0
        for i in range(len(items)):
            if not (items[i][0] in ("w_in", "attn_w_in") and i != ITEM["proj2"] + 4):
                n_done += 1
                done_at[i] = n_done
                released[i] = (item_done, n_done)

        def wait_item(pe, i):
            pe.wait_ge(arrived[i % SLOTS], 16 * (i // SLOTS + 1))

        x_loaded, const_loaded, ctx_loaded = sem("x_loaded"), sem("const_loaded"), sem("ctx_loaded")
        dve_chain, act_chain, pool_chain = sem("dve_chain"), sem("act_chain"), sem("pool_chain")
        chain_at = {"dve": 0, "act": 0, "pool": 0}

        def dve_step(ins):
            chain_at["dve"] += 1
            ins.then_inc(dve_chain, 1)
            nc.vector.wait_ge(dve_chain, chain_at["dve"])

        sums_ready, roots_done = sem("sums_ready"), sem("roots_done")
        chain_at["sums"] = chain_at["roots"] = 0

        def rooted(ins, sums, n):
            dve_step(ins)
            chain_at["sums"] += 1
            nc.vector.tensor_scalar(sums, sums, n * EPS, None, ALU.add).then_inc(sums_ready, 1)
            nc.vector.wait_ge(roots_done, chain_at["sums"])

        def root_pool(dst, src):
            chain_at["roots"] += 1
            nc.gpsimd.wait_ge(sums_ready, chain_at["roots"])
            nc.gpsimd.tensor_tensor(dst, src, minus_half[:, 0:src.shape[1]], ALU.pow).then_inc(roots_done, 1)

        def pool_step(ins):
            chain_at["pool"] += 1
            ins.then_inc(pool_chain, 1)
            nc.gpsimd.wait_ge(pool_chain, chain_at["pool"])

        sq_done, norm_sums, norm_roots = sem("sq_done"), sem("norm_sums"), sem("norm_roots")
        xn_done = sem("xn_done")
        tr_done, hT_act, hT_dve = sem("tr_done"), sem("hT_act"), sem("hT_dve")
        ss = small[:, 0:2]
        rs = small[:, 2:4]
        TR = [bank[6], bank[7]]

        def norm_act(j, src, i, ready):
            act = nc.scalar
            for s, v in ready:
                act.wait_ge(s, v)
            if i:
                act.wait_ge(tr_done, 4 * i)
            nc.scalar.activation(xn[:, 0, :], src[:, 0, :], ACT.Square, accum_out=ss[:, 0:1]).then_inc(sq_done, 1)
            act.wait_ge(norm_roots, j + 1)
            nc.scalar.activation(xn[:, 0, :], src[:, 0, :], ACT.Copy, scale=rs[:, 0:1]).then_inc(xn_done, 1)

        def norm_dve(j, src, i, ready):
            dve = nc.vector
            for s, v in ready:
                dve.wait_ge(s, v)
            if i:
                dve.wait_ge(tr_done, 4 * i)
            dve_step(nc.vector.tensor_tensor_reduce(out=xn[:, 1, :], in0=src[:, 1, :], in1=src[:, 1, :], scale=1.0, scalar=0.0,
                                                    op0=ALU.mult, op1=ALU.add, accum_out=ss[:, 1:2]))
            dve.wait_ge(sq_done, j + 1)
            nc.vector.tensor_scalar(ss, ss, 1.0 / D, EPS, ALU.mult, ALU.add).then_inc(norm_sums, 1)
            dve.wait_ge(norm_roots, j + 1)
            nc.vector.tensor_scalar(xn[:, 1, :], src[:, 1, :], rs[:, 1:2], None, ALU.mult).then_inc(xn_done, 1)

        def norm_pool(j):
            nc.gpsimd.wait_ge(norm_sums, j + 1)
            nc.gpsimd.tensor_tensor(rs, ss, minus_half[:, 0:T], ALU.pow).then_inc(norm_roots, 1)

        def tr_pe(i, ready):
            pe = nc.tensor
            for s, v in ready:
                pe.wait_ge(s, v)
            for kp in range(4):
                n = 2 * i + kp // 2
                if n:
                    pe.wait_ge(hT_dve if kp % 2 else hT_act, n)
                for kk in range(2):
                    for t in range(T):
                        last = nc.tensor.transpose(TR[kp % 2][:, kk * S + t * P:kk * S + (t + 1) * P],
                                                   xn[:, t, 2 * kp + kk::KD], ident)
                last.then_inc(tr_done, 1)

        def tr_act(i, dst, scale, shift):
            for kp in (0, 2):
                nc.scalar.wait_ge(tr_done, 4 * i + kp + 1)
                for kk in range(2):
                    k = 2 * kp + kk
                    bias = zero_col[:, 0:1] if shift is None else shift[:, k:k + 1]
                    last = nc.scalar.activation(dst[:, k, :], TR[0][:, kk * S:(kk + 1) * S], ACT.Identity, bias=bias,
                                                scale=scale[:, k:k + 1])
                last.then_inc(hT_act, 1)

        def tr_dve(i, dst, scale, shift):
            for kp in (1, 3):
                nc.vector.wait_ge(tr_done, 4 * i + kp + 1)
                for kk in range(2):
                    k = 2 * kp + kk
                    bias = zero_col[:, 0:1] if shift is None else shift[:, k:k + 1]
                    last = nc.vector.tensor_scalar(dst[:, k, :], TR[1][:, kk * S:(kk + 1) * S], scale[:, k:k + 1], bias,
                                                   ALU.mult, ALU.add)
                last.then_inc(hT_dve, 1)

        def hT_ready(i):
            return [(hT_act, 2 * (i + 1)), (hT_dve, 2 * (i + 1))]

        setup_done, cond_done, gate_loaded = sem("setup_done"), sem("cond_done"), sem("gate_loaded")
        ada_rows, ada_sums, ada_used = sem("ada_rows"), sem("ada_sums"), sem("ada_used")
        AB = [bank[4], bank[5]]
        ada_R = hT[:, 4:8, :].rearrange("p a b -> p (a b)")

        def ada_mm_pe(s):
            pe = nc.tensor
            if s == 0:
                pe.wait_ge(cond_done, 2)
                pe.wait_ge(fg_z, 1)
            elif s == 6:
                pe.wait_ge(fy_c, 1)
            else:
                pe.wait_ge(ada_used, s)
            for n in range(2):
                i = ITEM["ada", s] + n
                wait_item(pe, i)
                for kk in range(KD):
                    j = kk % 4
                    last = nc.tensor.matmul(AB[n][32 * j:32 * j + 32, :], condT[:, kk, :], ring[i % SLOTS][:, kk, :],
                                            start=(kk < 4), stop=(kk >= 4))
                last.then_inc(item_done, 1)

        def ada_rows_act(s):
            if s:
                nc.scalar.wait_ge(ada_sums, s)
            for n in range(2):
                nc.scalar.wait_ge(item_done, done_at[ITEM["ada", s] + n])
                nc.scalar.activation(ada_R[:, n * NC:(n + 1) * NC], AB[n][:, :], ACT.Copy).then_inc(ada_rows, 1)

        def ada_sum_pe(s):
            pe = nc.tensor
            pe.wait_ge(ada_rows, 2 * (s + 1))
            if s % 6 in (G_M, G_F):
                for n in range(2):
                    last = nc.tensor.matmul(AB[n][:, :], const("row0"), ada_R[:, n * NC:(n + 1) * NC], start=True, stop=True)
            else:
                for k in range(KD):
                    last = nc.tensor.matmul(AB[0][:, 2 * k:2 * k + 2], ada_R[:, k::KD], const("rows"), start=True, stop=True)
            last.then_inc(ada_sums, 1)

        def ada_use_dve(s):
            dve = nc.vector
            l, sec = divmod(s, 6)
            dve.wait_ge(ada_sums, s + 1)
            if sec in (G_M, G_F):
                g = gate_rows[:, l, sec // 3, :]
                if s == G_M:
                    dve.wait_ge(gate_loaded, 64)
                nc.vector.tensor_tensor(g[:, 0:NC], g[:, 0:NC], AB[0][:, :], ALU.add)
                nc.vector.tensor_tensor(g[:, NC:D], g[:, NC:D], AB[1][:, :], ALU.add).then_inc(ada_used, 1)
                return
            sums = AB[0][:, 0:2 * KD].rearrange("p (k c) -> p c k", c=2)
            m = (0 if sec < 3 else 2) + sec % 3
            both = [(mod[:, l, m, :], 0)] + ([(mod_ctx[:, m, :], 1)] if s < 2 else [])
            for n, (dst, c) in enumerate(both):
                ins = nc.vector.tensor_tensor(dst, sums[:, c, :], col(f"b{l}{sec}"), ALU.add)
                if sec % 3 == 1:
                    dve_step(ins)
                    gain = col(f"norm_mix{l}" if sec < 3 else f"norm_ffn{l}")
                    ins = nc.vector.scalar_tensor_tensor(dst, dst, 1.0, gain, ALU.add, ALU.mult)
            ins.then_inc(ada_used, 1)

        def heads(name, units, sq, qn, tmp, first_ready):
            pj, sqs, qns, qgs = sem(name + "_projected"), sem(name + "_squared"), sem(name + "_scaled"), sem(name + "_gained")
            rot, trs, put_, vput = sem(name + "_rotated"), sem(name + "_transposed"), sem(name + "_put"), sem(name + "_vput")
            qk = [u for u in range(len(units)) if units[u]["kind"] == "qk"]
            vs = [u for u in range(len(units)) if units[u]["kind"] == "v"]
            nq = {u: n for n, u in enumerate(qk)}
            nv = {u: n for n, u in enumerate(vs)}
            nrot = {u: sum(1 for w in qk[:nq[u] + 1] if units[w]["rope"]) for u in qk}
            NB = 4
            for u, un in enumerate(units):
                if un["item"] not in done_at:
                    released[un["item"]] = (pj, u + 1)

            def free(eng, u):
                w = u - NB
                if w >= 0:
                    if units[w]["kind"] == "qk":
                        eng.wait_ge(qns, nq[w] + 1)
                    else:
                        eng.wait_ge(vput, nv[w] + 1)

            def proj_pe(u):
                pe, un = nc.tensor, units[u]
                if u == 0:
                    for s, v in first_ready:
                        pe.wait_ge(s, v)
                for s, v in un.get("ready", []):
                    pe.wait_ge(s, v)
                wait_item(pe, un["item"])
                free(pe, u)
                a, n = un["cols"]
                for k in range(KD):
                    last = nc.tensor.matmul(bank[u % NB][:, 0:n], un["lhs"][:, k, :], ring[un["item"] % SLOTS][:, k, a:a + n],
                                            start=(k == 0), stop=(k == KD - 1))
                last.then_inc(pj, 1)

            def post_act(u):
                act, un = nc.scalar, units[u]
                act.wait_ge(pj, u + 1)
                if un["kind"] == "v":
                    for n, (c, dst) in enumerate(un["put"]):
                        ins = nc.scalar.activation(dst, bank[u % NB][:, c[0]:c[1]], ACT.Copy)
                    ins.then_inc(vput, 1)
                    return
                q = nq[u]
                if q >= 2:
                    act.wait_ge(qgs, q - 1)
                    if units[qk[q - 2]]["rope"]:
                        act.wait_ge(rot, nrot[qk[q - 2]])
                    else:
                        act.wait_ge(trs, q - 1)
                n = un["cols"][1]
                nc.scalar.activation(sq[:, q % 2, 0:n], bank[u % NB][:, 0:n], ACT.Square).then_inc(sqs, 1)

            def post_dve(u):
                dve, un = nc.vector, units[u]
                if un["kind"] == "v":
                    return
                q, n = nq[u], un["cols"][1]
                nh = n // HD
                s8, r8 = small[:, 16:16 + nh], small[:, 24:24 + nh]
                view = lambda a: a.rearrange("p (h d) -> p h d", d=HD)
                dve.wait_ge(sqs, q + 1)
                rooted(nc.vector.tensor_reduce(s8, view(sq[:, q % 2, 0:n]), AX.X, ALU.add), s8, HD)
                if q >= 2:
                    dve.wait_ge(trs, q - 1)
                ins = nc.vector.tensor_tensor(view(qn[:, q % 2, 0:n]), view(bank[u % NB][:, 0:n]),
                                              r8.unsqueeze(2).broadcast_to([P, nh, HD]), ALU.mult)
                ins.then_inc(qns, 1)
                dve.wait_ge(qns, q + 1)
                at = 0
                for m, gain in un["gains"]:
                    sl = slice(at * HD, (at + m) * HD)
                    ins = nc.vector.tensor_tensor(view(sq[:, q % 2, sl]), view(qn[:, q % 2, sl]),
                                                  gain.unsqueeze(1).broadcast_to([P, m, HD]), ALU.mult)
                    at += m
                ins.then_inc(qgs, 1)

            def rope_pool(u):
                un = units[u]
                if un["kind"] == "v":
                    return
                nh = un["cols"][1] // HD
                root_pool(small[:, 24:24 + nh], small[:, 16:16 + nh])
                if not un["rope"]:
                    return
                pool, q = nc.gpsimd, nq[u]
                cos, sin, half = un["rope"]
                n = un["cols"][1]
                nh, np_ = n // HD, HD // (2 * half)
                src, dst = sq[:, q % 2, 0:n], qn[:, q % 2, 0:n]
                pool.wait_ge(qgs, q + 1)
                view = lambda a: a.rearrange("p (h d) -> p h d", d=HD)
                pool_step(nc.gpsimd.tensor_tensor(view(dst), view(src), cos.unsqueeze(1).broadcast_to([P, nh, HD]), ALU.mult))
                for j in range(np_):
                    for a in range(2):
                        lo, so = (2 * j + a) * half, (2 * j + 1 - a) * half
                        ins = nc.gpsimd.tensor_tensor(view(tmp[:, 0:n])[:, :, lo:lo + half], view(src)[:, :, so:so + half],
                                                      sin[:, lo:lo + half].unsqueeze(1).broadcast_to([P, nh, half]), ALU.mult)
                pool_step(ins)
                nc.gpsimd.tensor_tensor(dst, dst, tmp[:, 0:n], ALU.add).then_inc(rot, 1)
                pool.wait_ge(rot, nrot[u])

            def tr_heads_pe(u):
                pe, un = nc.tensor, units[u]
                if un["kind"] == "v":
                    return
                q = nq[u]
                if un["rope"]:
                    pe.wait_ge(rot, nrot[u])
                    src = qn[:, q % 2, :]
                else:
                    pe.wait_ge(qgs, q + 1)
                    src = sq[:, q % 2, :]
                if q >= 2:
                    pe.wait_ge(put_, q - 1)
                for m in range(un["cols"][1] // P):
                    last = nc.tensor.transpose(TR[q % 2][:, m * P:(m + 1) * P], src[:, m * P:(m + 1) * P], ident)
                last.then_inc(trs, 1)

            def put_act(u):
                un = units[u]
                if un["kind"] == "v":
                    return
                q = nq[u]
                nc.scalar.wait_ge(trs, q + 1)
                for a, m, dst in un["put"]:
                    ins = nc.scalar.activation(dst, TR[q % 2][:, a * P:(a + m) * P].rearrange("p (m q) -> p m q", q=P), ACT.Copy)
                ins.then_inc(put_, 1)

            return dict(proj_pe=proj_pe, post_act=post_act, post_dve=post_dve, rope_pool=rope_pool, tr_pe=tr_heads_pe,
                        put_act=put_act, done=[(put_, len(qk)), (vput, len(vs))], put=put_)

        out_added = sem("out_added")
        out_scaled = arena[:, ARENA - NC:ARENA]

        def out_pe(o, lhs, ready):
            pe = nc.tensor
            for s, v in ready:
                pe.wait_ge(s, v)
            for n in range(2):
                i = ITEM["out", o] + n
                wait_item(pe, i)
                for t in range(T):
                    for k in range(KD):
                        last = nc.tensor.matmul(bank[2 * n + t][:, :], lhs[:, k, t * P:(t + 1) * P], ring[i % SLOTS][:, k, :],
                                                start=(k == 0), stop=(k == KD - 1))
                last.then_inc(item_done, 1)

        def out_dve(o, gate):
            dve = nc.vector
            for n in range(2):
                dve.wait_ge(item_done, done_at[ITEM["out", o] + n])
                sl = slice(n * NC, (n + 1) * NC)
                for t in range(T):
                    src = bank[2 * n + t][:, :]
                    if gate is not None:
                        dve_step(nc.vector.tensor_tensor(out_scaled[:, :], src, gate[:, sl], ALU.mult))
                        src = out_scaled[:, :]
                    ins = nc.vector.tensor_tensor(h[:, t, sl], h[:, t, sl], src, ALU.add)
                    ins.then_inc(out_added, 1)
                    dve.wait_ge(out_added, 4 * o + 2 * n + t + 1)

        arena_at[0] = 0
        sq_junk = carve(NC)
        qT = [carve(4, S) for _ in range(2)]
        kT = [carve(4, S) for _ in range(2)]
        vv = [carve(T, NC) for _ in range(2)]
        bias1 = carve(8, S)
        bias0 = hT[:, 0:4, :].rearrange("p a b -> p (a b)").rearrange("p (h k) -> p h k", k=P)
        temps_at = arena_at[0]
        sq1, qn1, tmp1 = carve(2, NC), carve(2, NC), carve(NC)
        fz, fa, fn = (xn[:, 0, n * S:(n + 1) * S] for n in range(3))
        sp, pr, pt = (a for a in (carve(2, S, at=temps_at), carve(2, S), carve(2, S)))

        rope1 = (const("cos1"), const("sin1"), HD // 2)
        rope2 = (const("cos2"), const("sin2"), HD // 4)

        def rope_of(rope, t):
            return (rope[0][:, t * HD:(t + 1) * HD], rope[1][:, t * HD:(t + 1) * HD], rope[2])

        units1 = []
        for c, name in enumerate(CHUNKS1):
            for t in range(T):
                un = dict(item=ITEM["proj1", c], lhs=hT[:, :, t * P:(t + 1) * P], cols=(0, NC))
                br = 0 if name[1] == "a" else 1
                if name[0] == "v":
                    un.update(kind="v", put=[((0, NC), vv[br][:, t, :])])
                else:
                    dst = (qT if name[0] == "q" else kT)[br]
                    un.update(kind="qk", gains=[(8, row(name[0] + ("_fox" if br == 0 else "_dil")))],
                              rope=rope_of(rope1, t) if br else None, put=[(0, 4, dst[:, :, t * P:(t + 1) * P])])
                units1.append(un)
        h1 = heads("h1", units1, sq1, qn1, tmp1, hT_ready(0))

        fg_mm, fg_z, fg_ln, fg_c = sem("fg_mm"), sem("fg_z"), sem("fg_ln"), sem("fg_c")
        FG = bank[5][0:8, 0:S]

        def forget_pe():
            for s_, v in hT_ready(0):
                nc.tensor.wait_ge(s_, v)
            for k in range(KD):
                last = nc.tensor.matmul(FG, router_sb[:, k, 68:76], hT[:, k, :], start=(k == 0), stop=(k == KD - 1))
            last.then_inc(fg_mm, 1)

        def forget_dve():
            nc.vector.wait_ge(fg_mm, 1)
            dve_step(nc.vector.tensor_scalar(fz[0:8, :], FG, cols[0:8, COLS.index("b_forget"), 0:1], None, ALU.add))
            nc.vector.scalar_tensor_tensor(fa[0:8, :], fz[0:8, :], -1.0, fz[0:8, :], ALU.mult, ALU.max).then_inc(fg_z, 1)

        def forget_act():
            nc.scalar.wait_ge(fg_z, 1)
            nc.scalar.activation(fa[0:8, :], fa[0:8, :], ACT.Exp, scale=-1.0).then_inc(act_chain, 1)
            nc.scalar.wait_ge(act_chain, 1)
            nc.scalar.activation(fa[0:8, :], fa[0:8, :], ACT.Ln, bias=const("ones")[0:8, 0:1]).then_inc(fg_ln, 1)

        def forget_sum_dve():
            nc.vector.wait_ge(fg_ln, 1)
            dve_step(nc.vector.scalar_tensor_tensor(fz[0:8, :], fz[0:8, :], 0.0, fa[0:8, :], ALU.min, ALU.subtract))
            dve_step(nc.vector.tensor_scalar(fz[0:8, :], fz[0:8, :], -1.0, None, ALU.mult))
            nc.vector.memset(fa[0:8, :], 1.0).then_inc(dve_chain, 1)
            chain_at["dve"] += 1
            nc.vector.wait_ge(dve_chain, chain_at["dve"])
            nc.vector.tensor_tensor_scan(fn[0:8, :], fa[0:8, :], fz[0:8, :], 0.0, ALU.mult, ALU.add).then_inc(fg_c, 1)

        cb_mm, cb_done = sem("cb_mm"), sem("cb_done")
        BIAS = [(0, 0, 0, 4), (1, 0, 4, 4), (2, 1, 0, 2), (3, 1, 2, 2), (0, 1, 4, 2), (1, 1, 6, 2)]

        def bias_pe():
            pe = nc.tensor
            pe.wait_ge(fg_c, 1)
            for s_, v in h1["done"]:
                pe.wait_ge(s_, v)
            for n, (b, t, h0, nh) in enumerate(BIAS):
                if n >= 4:
                    pe.wait_ge(cb_done, n - 3)
                w = P * (t + 1)
                for j in range(nh):
                    last = nc.tensor.matmul(bank[b][:, j * w:(j + 1) * w], ident[0:8, h0 + j:h0 + j + 1].broadcast_to([8, P]),
                                            fn[0:8, 0:w], start=True, stop=True)
                last.then_inc(cb_mm, 1)

        def bias_dve():
            for n, (b, t, h0, nh) in enumerate(BIAS):
                nc.vector.wait_ge(cb_mm, n + 1)
                w = P * (t + 1)
                dst = (bias1 if t else bias0)[:, h0:h0 + nh, :]
                nc.vector.tensor_tensor(dst, bank[b][:, 0:nh * w].rearrange("p (h k) -> p h k", k=w),
                                        const(f"causal{t}").unsqueeze(1).broadcast_to([P, nh, w]), ALU.add).then_inc(cb_done, 1)

        at_s, at_m, at_e, at_t, at_c, at_v = (sem("at_" + n) for n in ("scores", "max", "exp", "turned", "copied", "values"))
        at_o, at_q, at_n = sem("at_out"), sem("at_outsq"), sem("at_normed")
        att1 = [(t, br, hd) for t in range(T) for br in (1, 0) for hd in range(8)]
        negm, lsum = small[:, 32:64], small[:, 64:96]

        def scores_pe(u):
            pe = nc.tensor
            t, br, hd = att1[u]
            if u >= 2:
                pe.wait_ge(at_m, u - 1)
            if u == 0:
                pe.wait_ge(cb_done, len(BIAS))
            a = HD * (hd % 2)
            w = P * (t + 1)
            nc.tensor.matmul(bank[u % 2][:, 0:w], qT[br][a:a + HD, hd // 2, t * P:(t + 1) * P],
                             kT[br][a:a + HD, hd // 2, 0:w], start=True, stop=True).then_inc(at_s, 1)

        def max_dve(u):
            dve = nc.vector
            t, br, hd = att1[u]
            w = P * (t + 1)
            dve.wait_ge(at_s, u + 1)
            if u >= 2:
                dve.wait_ge(at_e, u - 1)
            bias = const(f"dilated{t}") if br else (bias1 if t else bias0)[:, hd, :]
            nc.vector.tensor_tensor_reduce(out=sp[:, u % 2, 0:w], in0=bank[u % 2][:, 0:w], in1=bias, scale=-1.0, scalar=3e38,
                                           op0=ALU.add, op1=ALU.min, accum_out=negm[:, u:u + 1]).then_inc(at_m, 1)

        def exp_act(u):
            act = nc.scalar
            w = P * (att1[u][0] + 1)
            act.wait_ge(at_m, u + 1)
            if u >= 2:
                act.wait_ge(at_t, u - 1)
            nc.scalar.activation(pr[:, u % 2, 0:w], sp[:, u % 2, 0:w], ACT.Exp, bias=negm[:, u:u + 1], scale=-1.0,
                                 accum_out=lsum[:, u:u + 1]).then_inc(at_e, 1)

        def turn_pe(u):
            pe = nc.tensor
            pe.wait_ge(at_e, u + 1)
            if u >= 2:
                pe.wait_ge(at_c, u - 1)
            for b in range(att1[u][0] + 1):
                last = nc.tensor.transpose(bank[2 + u % 2][:, b * P:(b + 1) * P], pr[:, u % 2, b * P:(b + 1) * P], ident)
            last.then_inc(at_t, 1)

        def copy_dve(u):
            dve = nc.vector
            w = P * (att1[u][0] + 1)
            dve.wait_ge(at_t, u + 1)
            if u >= 2:
                dve.wait_ge(at_v, u - 1)
            nc.vector.tensor_copy(pt[:, u % 2, 0:w], bank[2 + u % 2][:, 0:w]).then_inc(at_c, 1)

        def values_pe(u):
            pe = nc.tensor
            t, br, hd = att1[u]
            pe.wait_ge(at_c, u + 1)
            if t and hd == 0:
                pe.wait_ge(at_o, u // 8 - 1)
            for b in range(t + 1):
                last = nc.tensor.matmul(bank[6 + br][:, hd * HD:(hd + 1) * HD], pt[:, u % 2, b * P:(b + 1) * P],
                                        vv[br][:, b, hd * HD:(hd + 1) * HD], start=(b == 0), stop=(b == t))
            last.then_inc(at_v, 1)

        def out1_dve(g):
            dve = nc.vector
            t, br, _ = att1[8 * g]
            rl = small[:, 96:104]
            dve.wait_ge(at_v, 8 * (g + 1))
            dve.wait_ge(at_e, 8 * (g + 1))
            dve_step(nc.vector.reciprocal(rl, lsum[:, 8 * g:8 * g + 8]))
            nc.vector.tensor_tensor(xn[:, t, br * NC:(br + 1) * NC].rearrange("p (h d) -> p h d", d=HD),
                                    bank[6 + br][:, :].rearrange("p (h d) -> p h d", d=HD),
                                    rl.unsqueeze(2).broadcast_to([P, 8, HD]), ALU.mult).then_inc(at_o, 1)

        def out1_act(g):
            t, br, _ = att1[8 * g]
            nc.scalar.wait_ge(at_o, g + 1)
            if g:
                nc.scalar.wait_ge(at_q, g)
            nc.scalar.activation(sq_junk[:, :], xn[:, t, br * NC:(br + 1) * NC], ACT.Square,
                                 accum_out=small[:, 104 + g:105 + g]).then_inc(at_q, 1)

        def out1_norm_dve(g):
            dve = nc.vector
            t, br, _ = att1[8 * g]
            sl = xn[:, t, br * NC:(br + 1) * NC]
            sums, r = small[:, 104 + g:105 + g], small[:, 108 + g:109 + g]
            dve.wait_ge(at_q, g + 1)
            rooted(nc.vector.tensor_scalar(sums, sums, 0.0, None, ALU.add), sums, NC)
            nc.vector.tensor_scalar(sl, sl, r, float(NC) ** 0.5, ALU.mult, ALU.mult).then_inc(at_n, 1)

        def out1_pool(g):
            root_pool(small[:, 108 + g:109 + g], small[:, 104 + g:105 + g])

        LAST1 = len(att1) - 1

        def steps1():
            for u in range(len(units1)):
                yield "proj", u
                if u >= 2:
                    yield "tr", u - 2
            for u in (len(units1) - 2, len(units1) - 1):
                yield "tr", u
            yield "bias", 0
            s = 0
            for u in range(LAST1 + 4):
                if u <= LAST1:
                    yield "scores", u
                if 2 <= u <= LAST1 + 2:
                    yield "turn", u - 2
                if u >= 3:
                    yield "values", u - 3
                    if (u - 3) % 8 == 7:
                        yield "out", (u - 3) // 8
                if u % 5 == 2 and s < 6:
                    yield "ada_mm", s
                if u % 5 == 4 and s < 6:
                    yield "ada_sum", s
                    s += 1

        def block1_pe():
            pe = nc.tensor
            pe.wait_ge(const_loaded, 16 * 4)
            tr_pe(0, [(xn_done, 2)])
            forget_pe()
            for what, i in steps1():
                if what == "proj":
                    h1["proj_pe"](i)
                elif what == "ada_mm":
                    ada_mm_pe(i)
                elif what == "ada_sum":
                    ada_sum_pe(i)
                elif what == "tr":
                    h1["tr_pe"](i)
                elif what == "bias":
                    bias_pe()
                elif what == "scores":
                    scores_pe(i)
                elif what == "turn":
                    turn_pe(i)
                elif what == "values":
                    values_pe(i)
            tr_pe(1, [(at_n, 4)])
            out_pe(0, hT, hT_ready(1))

        def block1_act():
            act = nc.scalar
            norm_act(0, h, 0, [(x_loaded, 16)])
            tr_act(0, hT, col("norm_mix"), None)
            forget_act()
            for what, i in steps1():
                if what == "proj":
                    h1["post_act"](i)
                elif what == "ada_mm":
                    ada_rows_act(i)
                elif what == "tr":
                    h1["put_act"](i)
                elif what == "scores":
                    exp_act(i)
                elif what == "out":
                    out1_act(i)
            tr_act(1, hT, col("out_norm"), None)

        def block1_dve():
            norm_dve(0, h, 0, [(x_loaded, 16)])
            tr_dve(0, hT, col("norm_mix"), None)
            forget_dve()
            for what, i in steps1():
                if what == "proj":
                    h1["post_dve"](i)
                    if i == 1:
                        forget_sum_dve()
                elif what == "ada_sum":
                    ada_use_dve(i)
                elif what == "bias":
                    bias_dve()
                elif what == "scores":
                    max_dve(i)
                elif what == "turn":
                    copy_dve(i)
                elif what == "out":
                    out1_dve(i)
                    out1_norm_dve(i)
            tr_dve(1, hT, col("out_norm"), None)
            out_dve(0, None)

        def block1_pool():
            norm_pool(0)
            for u in range(len(units1)):
                h1["rope_pool"](u)
            for g in range(4):
                out1_pool(g)

        arena_at[0] = 0
        xgT = carve(KD, EP * C)
        sel = carve(T, EP * C)
        wsel = carve(T, EP * C)
        xs, ws = carve(2 * KD, C), carve(2 * T, 4 * C)
        gate_s, up_s = carve(2, NC), carve(2, NC)
        silu_s = carve(2, 4 * C)
        act_s = carve(2 * KD, C)
        z_s = carve(D)
        wselT = carve(2, S)
        rankm, comb = carve(T, E1), carve(T, E1)
        r_temps = [carve(T, E1) for _ in range(6)]
        logits = carve(T, G1 + E1)

        lg_mm, rt_act, rt_dve, rk_mm = sem("logits_mm"), sem("route_act"), sem("route_dve"), sem("rank_mm")
        rk_done, flag_done = sem("rank_done"), sem("flag_done")
        route_n = {"act": 0, "dve": 0, "pe": 0}

        def logits_pe(m, i, c0, n):
            pe = nc.tensor
            for s_, v in hT_ready(i):
                pe.wait_ge(s_, v)
            for t in range(T):
                for k in range(KD):
                    last = nc.tensor.matmul(bank[0][:, t * n:(t + 1) * n], hT[:, k, t * P:(t + 1) * P], router_sb[:, k, c0:c0 + n],
                                            start=(k == 0), stop=(k == KD - 1))
            last.then_inc(lg_mm, 1)

        def bc(a, *shape):
            return a.broadcast_to([P, *shape])

        def first_max_dve(z, iota, n, best, eq, idx):
            v = nc.vector
            dve_step(v.tensor_reduce(best, z, AX.X, ALU.max))
            dve_step(v.tensor_tensor(eq, z, bc(best.unsqueeze(2), T, n), ALU.is_equal))
            dve_step(v.scalar_tensor_tensor(eq, eq, -64.0, bc(iota.unsqueeze(1), T, n), ALU.mult, ALU.add))
            dve_step(v.tensor_reduce(idx, eq, AX.X, ALU.min))
            dve_step(v.tensor_tensor(eq, eq, bc(idx.unsqueeze(2), T, n), ALU.is_equal))

        one_g, one_a, one_b = r_temps[0][:, :, 0:G1], r_temps[1], r_temps[2]
        zsel, zg = r_temps[3], r_temps[4][:, :, 0:G1]
        gmax, gidx, gsum, best1, best2, eidx, ediff, gtop = (small[:, 120 + 2 * n:122 + 2 * n] for n in range(8))
        gpen = r_temps[4][:, :, 8:8 + G1]

        def route1_dve():
            v = nc.vector
            v.wait_ge(lg_mm, 1)
            dve_step(v.tensor_tensor(logits[:, :, :], bank[0][:, 0:T * (G1 + E1)].rearrange("p (t e) -> p t e", t=T),
                                     bc(row("b_router", G1 + E1).unsqueeze(1), T, G1 + E1), ALU.add))
            iota = const("iota")
            first_max_dve(logits[:, :, 0:G1], iota[:, 0:G1], G1, gmax, one_g, gidx)
            v.tensor_tensor(zg, logits[:, :, 0:G1], bc(gmax.unsqueeze(2), T, G1), ALU.subtract).then_inc(rt_dve, 1)
            dve_step(v.tensor_scalar(gpen, one_g, -NEG, NEG, ALU.mult, ALU.add))
            dve_step(v.tensor_tensor(zsel[:, :, :].rearrange("p t (g e) -> p t g e", g=G1),
                                     logits[:, :, G1:].rearrange("p t (g e) -> p t g e", g=G1),
                                     gpen.unsqueeze(3).broadcast_to([P, T, G1, E1 // G1]), ALU.add))
            first_max_dve(zsel[:, :, :], iota, E1, best1, one_a[:, :, :], eidx)
            dve_step(v.scalar_tensor_tensor(zsel[:, :, :], one_a[:, :, :], 2 * NEG, zsel[:, :, :], ALU.mult, ALU.add))
            first_max_dve(zsel[:, :, :], iota, E1, best2, one_b[:, :, :], eidx)
            v.tensor_tensor(ediff, best2, best1, ALU.subtract).then_inc(rt_dve, 1)
            v.wait_ge(rt_act, 2)
            dve_step(v.tensor_reduce(gsum, zg, AX.X, ALU.add))
            dve_step(v.scalar_tensor_tensor(gsum, ediff, 1.0, gsum, ALU.add, ALU.mult))
            dve_step(v.reciprocal(gtop, gsum))
            dve_step(v.tensor_tensor(ediff, ediff, gtop, ALU.mult))
            dve_step(v.tensor_tensor(comb[:, :, :], one_a[:, :, :], bc(gtop.unsqueeze(2), T, E1), ALU.mult))
            dve_step(v.tensor_tensor(zsel[:, :, :], one_b[:, :, :], bc(ediff.unsqueeze(2), T, E1), ALU.mult))
            dve_step(v.tensor_tensor(comb[:, :, :], comb[:, :, :], zsel[:, :, :], ALU.add))
            v.tensor_tensor(one_a[:, :, :], one_a[:, :, :], one_b[:, :, :], ALU.add).then_inc(rt_dve, 1)
            v.wait_ge(rt_dve, 3)
            v.wait_ge(rk_mm, 1)
            dve_step(v.tensor_tensor(zsel[:, :, :], bank[1][:, 0:T * E1].rearrange("p (t e) -> p t e", t=T), one_a[:, :, :], ALU.mult))
            dve_step(v.scalar_tensor_tensor(rankm[:, :, :], zsel[:, :, :], -1.0, one_a[:, :, :], ALU.add, ALU.add))
            dve_step(v.tensor_reduce(small[:, 140:141], bank[1][:, T * E1:(T + 1) * E1], AX.X, ALU.max))
            dve_step(v.tensor_scalar(small[:, 144:144 + PC], iota[:, 1:1 + PC], float(C), small[:, 140:141], ALU.mult, ALU.is_lt))
            dve_step(v.tensor_reduce(small[:, 141:142], small[:, 144:144 + PC], AX.X, ALU.add))
            v.tensor_copy(flag[:, :], small[:, 141:142]).then_inc(flag_done, 1)

        def route1_act():
            nc.scalar.wait_ge(rt_dve, 1)
            nc.scalar.activation(zg, zg, ACT.Exp).then_inc(rt_act, 1)
            nc.scalar.wait_ge(rt_dve, 2)
            nc.scalar.activation(ediff, ediff, ACT.Exp).then_inc(rt_act, 1)

        def rank_pe():
            nc.tensor.wait_ge(rt_dve, 3)
            R = bank[1]
            nc.tensor.matmul(R[:, 0:E1], const("before"), one_a[:, 0, :], start=True, stop=True)
            nc.tensor.matmul(R[:, E1:2 * E1], const("ones"), one_a[:, 0, :], start=True, stop=False)
            nc.tensor.matmul(R[:, E1:2 * E1], const("before"), one_a[:, 1, :], start=False, stop=True)
            nc.tensor.matmul(R[:, 2 * E1:3 * E1], const("ones"), one_a[:, 0, :], start=True, stop=False)
            nc.tensor.matmul(R[:, 2 * E1:3 * E1], const("ones"), one_a[:, 1, :], start=False, stop=True).then_inc(rk_mm, 1)

        CAP = 2 * S // E2
        aff = r_temps[0][:, :, 0:E2]
        affT, workT, maskT, slotT = (sel[0:E2, t, n * S:(n + 1) * S] for t in range(2) for n in range(2))
        best8 = wsel[0:E2, 0, 0:8]
        onesT = wsel[0:E2, 1, 0:S]
        af_dve, af_act, af_tr, af_slot, af_back = sem("aff_dve"), sem("aff_act"), sem("aff_tr"), sem("aff_slot"), sem("aff_back")

        def route2_dve(l):
            v = nc.vector
            v.wait_ge(lg_mm, 2 + l)
            z = bank[0][:, 0:T * E2].rearrange("p (t e) -> p t e", t=T)
            dve_step(v.tensor_reduce(gmax, z, AX.X, ALU.max))
            v.tensor_tensor(aff, z, bc(gmax.unsqueeze(2), T, E2), ALU.subtract).then_inc(af_dve, 1)
            v.wait_ge(af_act, l + 1)
            dve_step(v.tensor_reduce(gsum, aff, AX.X, ALU.add))
            dve_step(v.reciprocal(gtop, gsum))
            v.tensor_tensor(comb[:, :, 0:E2], aff, bc(gtop.unsqueeze(2), T, E2), ALU.mult).then_inc(af_dve, 1)
            v.wait_ge(af_tr, l + 1)
            dve_step(v.tensor_copy(workT, bank[1][0:E2, 0:S]))
            for n in range(CAP // 8):
                dve_step(v.max(best8, workT))
                dve_step(v.match_replace(workT, best8, workT, -1.0))
            dve_step(v.memset(onesT, 1.0))
            dve_step(v.tensor_scalar(maskT, workT, 0.0, None, ALU.is_lt))
            dve_step(v.tensor_tensor_scan(slotT, onesT, maskT, 0.0, ALU.mult, ALU.add))
            dve_step(v.tensor_tensor(slotT, slotT, maskT, ALU.mult))
            v.tensor_scalar(slotT, slotT, -1.0, None, ALU.add).then_inc(af_slot, 1)
            v.wait_ge(af_back, l + 1)
            dve_step(v.tensor_copy(rankm[:, :, 0:E2], bank[2][:, 0:T * E2].rearrange("p (t e) -> p t e", t=T)))

        def route2_act(l):
            nc.scalar.wait_ge(af_dve, 2 * l + 1)
            nc.scalar.activation(aff, aff, ACT.Exp).then_inc(af_act, 1)

        def route2_pe(l):
            pe = nc.tensor
            pe.wait_ge(af_dve, 2 * l + 2)
            for t in range(T):
                last = nc.tensor.transpose(bank[1][0:E2, t * P:(t + 1) * P], comb[:, t, 0:E2], ident)
            last.then_inc(af_tr, 1)
            pe.wait_ge(af_slot, l + 1)
            for t in range(T):
                last = nc.tensor.transpose(bank[2][:, t * E2:(t + 1) * E2], slotT[:, t * P:(t + 1) * P], ident[0:E2, 0:E2])
            last.then_inc(af_back, 1)

        STEPS = ("sel", "wsel", "gathered", "xg_act", "xg_dve", "xs", "ws", "g_copied", "u_copied", "turned", "silu",
                 "act", "z0", "z1", "w_turned", "wT", "y", "y_added")
        kind1, kind2 = ([sem(f"{kind}_{n}") for n in STEPS] for kind in ("m1", "m2"))

        def place_up(M, e, hf, up):
            return (2 * M.nf + (e - 1) * M.per if e else 0) + 2 * hf + up

        def place_down(M, e, n):
            return 2 * M.nf + e * M.per + (2 * M.nf if e < EP - 1 else 0) + n

        def nth(value, per_expert, r, k):
            return (r * (2 * per_expert)) + ((k * (EP * per_expert)) + value)

        def wait_moe_item(pe, M, i, r, k):
            pe.wait_ge(M.arrived[(M.first + i) % SLOTS],
                       (r * (2 * M.per // SLOTS * 16)) + (((k - M.k0) * (EP * M.per // SLOTS * 16)) + 16 * ((M.first + i) // SLOTS + 1)))
            return ring[(M.first + i) % SLOTS]

        def wait_moe_done(eng, M, i, r, k):
            eng.wait_ge(M.done, nth(M.done0 + i + 1, M.per, r, k - M.k0))

        GATHER = [bank[1], bank[2]]
        YB = [bank[5], bank[6]]

        PARTS = [(0, 2 * C), (2 * C, EP * C)]

        def gather_pe(M, k, part):
            pe = nc.tensor
            a, b = PARTS[part]
            if part == 0:
                pe.wait_ge(M.sel, k + 1)
            else:
                pe.wait_ge(M.u_copied, (k * (EP * M.nf)) + 2 * M.nf)
                pe.wait_ge(M.act, (k * (EP * M.nf)) + 2 * M.nf)
            for kk in range(KD):
                if kk >= 2:
                    pe.wait_ge(M.xg_dve if kk % 2 else M.xg_act, (k * KD) + (4 * part + kk // 2))
                for t in range(T):
                    last = nc.tensor.matmul(GATHER[kk % 2][:, 0:b - a], xn[:, t, kk::KD], sel[:, t, a:b], start=(t == 0), stop=(t == T - 1))
                last.then_inc(M.gathered, 1)
            pe.wait_ge(M.xg_act, (k * KD) + 4 * (part + 1))
            pe.wait_ge(M.xg_dve, (k * KD) + 4 * (part + 1))
            pe.nop(nofuse=True)

        def gather_act(M, k, part):
            a, b = PARTS[part]
            for kk in range(0, KD, 2):
                nc.scalar.wait_ge(M.gathered, (k * 2 * KD) + (KD * part + kk + 1))
                bias = zero_col[:, 0:1] if M.shift is None else M.shift[:, kk:kk + 1]
                nc.scalar.activation(xgT[:, kk, a:b], GATHER[0][:, 0:b - a], ACT.Identity, bias=bias,
                                     scale=M.scale[:, kk:kk + 1]).then_inc(M.xg_act, 1)

        def gather_dve(M, k, part):
            v = nc.vector
            a, b = PARTS[part]
            for kk in range(1, KD, 2):
                v.wait_ge(M.gathered, (k * 2 * KD) + (KD * part + kk + 1))
                bias = zero_col[:, 0:1] if M.shift is None else M.shift[:, kk:kk + 1]
                v.tensor_scalar(xgT[:, kk, a:b], GATHER[1][:, 0:b - a], M.scale[:, kk:kk + 1], bias, ALU.mult, ALU.add).then_inc(M.xg_dve, 1)

        def select_dve(M, k, half):
            v = nc.vector
            iota = const("iota").unsqueeze(1).broadcast_to([P, EP, C])
            four = lambda a: a.rearrange("p (e c) -> p e c", c=C)
            e0 = EP * half
            for t in range(T):
                last = v.tensor_tensor(four(sel[:, t, :]), iota, rankm[:, t, e0:e0 + EP].unsqueeze(2).broadcast_to([P, EP, C]),
                                       ALU.is_equal)
            last.then_inc(M.sel, 1)
            v.wait_ge(M.sel, k + 1)
            for t in range(T):
                last = v.tensor_tensor(four(wsel[:, t, :]), four(sel[:, t, :]),
                                       comb[:, t, e0:e0 + EP].unsqueeze(2).broadcast_to([P, EP, C]), ALU.mult)
            last.then_inc(M.wsel, 1)

        def expert_up_pe(M, k, e, r):
            pe = nc.tensor
            b = e % 2
            pe.wait_ge(M.xs, nth(e + 1, 1, r, k))
            for hf in range(M.nf):
                q = e * M.nf + hf
                for up in range(2):
                    i = place_up(M, e, hf, up)
                    w = wait_moe_item(pe, M, i, r, k)
                    if q:
                        pe.wait_ge(M.u_copied if up else M.g_copied, nth(q, M.nf, r, k))
                    for kk in range(KD):
                        j = kk % 4
                        last = nc.tensor.matmul(bank[up][32 * j:32 * j + 32, :], xs[:, b * KD + kk, :], w[:, kk, :],
                                                start=(kk < 4), stop=(kk >= 4))
                    last.then_inc(M.done, 1)

        def expert_wT_pe(M, k, e, r):
            pe = nc.tensor
            pe.wait_ge(M.ws, nth(e + 1, 1, r, k))
            if e:
                pe.wait_ge(M.wT, nth(e, 1, r, k))
            for t in range(T):
                last = nc.tensor.transpose(bank[7][:, t * P:(t + 1) * P], ws[:, (e % 2) * T + t, :], ident)
            last.then_inc(M.w_turned, 1)

        def expert_turn_pe(M, k, e, hf, r):
            pe = nc.tensor
            q = e * M.nf + hf
            pe.wait_ge(M.g_copied, nth(q + 1, M.nf, r, k))
            pe.wait_ge(M.u_copied, nth(q + 1, M.nf, r, k))
            if q:
                pe.wait_ge(M.act, nth(q, M.nf, r, k))
            for up, src in enumerate((gate_s, up_s)):
                for f in range(4):
                    c = (2 * hf + up) * 4 * C + f * C
                    last = nc.tensor.matmul(bank[2][:, c:c + C], src[:, q % 2, f * P:(f + 1) * P], const("stack"), start=True, stop=True)
            last.then_inc(M.turned, 1)

        def expert_down_pe(M, k, e, r):
            pe = nc.tensor
            b = e % 2
            pe.wait_ge(M.act, nth((e + 1) * M.nf, M.nf, r, k))
            if e:
                pe.wait_ge(M.z0, nth(e, 1, r, k))
                pe.wait_ge(M.z1, nth(e, 1, r, k))
            if M.nd == 1:
                w = wait_moe_item(pe, M, place_down(M, e, 0), r, k)[:, :, :].rearrange("p a b -> p (a b)").rearrange("p (k n) -> p k n", n=D)
                for n in range(2):
                    for j in range(4):
                        last = nc.tensor.matmul(bank[3 + n][32 * j:32 * j + 32, :], act_s[:, b * KD + j, :],
                                                w[:, j, n * NC:(n + 1) * NC], start=True, stop=True)
                last.then_inc(M.done, 1)
                return
            for n in range(2):
                w = wait_moe_item(pe, M, place_down(M, e, n), r, k)
                for kk in range(KD):
                    j = kk % 4
                    last = nc.tensor.matmul(bank[3 + n][32 * j:32 * j + 32, :], act_s[:, b * KD + kk, :], w[:, kk, :],
                                            start=(kk < 4), stop=(kk >= 4))
                last.then_inc(M.done, 1)

        def expert_back_pe(M, k, e, r):
            pe = nc.tensor
            pe.wait_ge(M.z0, nth(e + 1, 1, r, k))
            pe.wait_ge(M.z1, nth(e + 1, 1, r, k))
            pe.wait_ge(M.wT, nth(e + 1, 1, r, k))
            for n in range(2):
                for t in range(T):
                    i = 4 * e + 2 * n + t
                    if i >= 2:
                        pe.wait_ge(M.y_added, nth(i - 1, 4, r, k))
                    nc.tensor.matmul(YB[i % 2][:, :], wselT[:, e % 2, t * P:(t + 1) * P], z_s[:, n * NC:(n + 1) * NC],
                                     start=True, stop=True).then_inc(M.y, 1)

        def copy_up(M, k, e, hf, r, up):
            eng = nc.scalar if up == 0 or M.gate is not None else nc.vector
            q = e * M.nf + hf
            wait_moe_done(eng, M, place_up(M, e, hf, up), r, k)
            if q >= 2:
                eng.wait_ge(M.turned, nth(q - 1, M.nf, r, k))
            dst = (up_s if up else gate_s)[:, q % 2, :]
            if up == 0 or M.gate is not None:
                nc.scalar.activation(dst, bank[up][:, :], ACT.Copy).then_inc(M.u_copied if up else M.g_copied, 1)
            else:
                nc.vector.tensor_copy(dst, bank[up][:, :]).then_inc(M.u_copied, 1)

        def copy_wT_act(M, k, e, r):
            nc.scalar.wait_ge(M.w_turned, nth(e + 1, 1, r, k))
            if e >= 2:
                nc.scalar.wait_ge(M.y, nth(4 * (e - 1), 4, r, k))
            nc.scalar.activation(wselT[:, e % 2, :], bank[7][:, 0:S], ACT.Copy).then_inc(M.wT, 1)

        def silu_act(M, k, e, hf, r):
            q = e * M.nf + hf
            nc.scalar.wait_ge(M.turned, nth(q + 1, M.nf, r, k))
            if q >= 2:
                nc.scalar.wait_ge(M.act, nth(q - 1, M.nf, r, k))
            c = 2 * hf * 4 * C
            nc.scalar.activation(silu_s[:, q % 2, :], bank[2][:, c:c + 4 * C], ACT.Silu).then_inc(M.silu, 1)

        def act_dve(M, k, e, hf, r):
            q = e * M.nf + hf
            nc.vector.wait_ge(M.silu, nth(q + 1, M.nf, r, k))
            c = (2 * hf + 1) * 4 * C
            at = (e % 2) * KD + 4 * hf
            nc.vector.tensor_tensor(act_s[:, at:at + 4, :], silu_s[:, q % 2, :].rearrange("p (f c) -> p f c", c=C),
                                    bank[2][:, c:c + 4 * C].rearrange("p (f c) -> p f c", c=C), ALU.mult).then_inc(M.act, 1)

        def copy_z(M, k, e, n, r):
            eng = nc.scalar if n == 0 and M.gate is None else nc.vector
            wait_moe_done(eng, M, place_down(M, e, n if M.nd == 2 else 0), r, k)
            if e:
                eng.wait_ge(M.y, nth(4 * e, 4, r, k))
            dst, src = z_s[:, n * NC:(n + 1) * NC], bank[3 + n][:, :]
            if M.gate is not None:
                nc.vector.tensor_tensor(dst, src, M.gate[:, n * NC:(n + 1) * NC], ALU.mult).then_inc(M.z1 if n else M.z0, 1)
            elif n == 0:
                nc.scalar.activation(dst, src, ACT.Copy).then_inc(M.z0, 1)
            else:
                nc.vector.tensor_copy(dst, src).then_inc(M.z1, 1)

        def add_y_dve(M, k, e, r):
            for n in range(2):
                for t in range(T):
                    i = 4 * e + 2 * n + t
                    nc.vector.wait_ge(M.y, nth(i + 1, 4, r, k))
                    dst = h[:, t, n * NC:(n + 1) * NC]
                    nc.vector.tensor_tensor(dst, dst, YB[i % 2][:, :], ALU.add).then_inc(M.y_added, 1)

        def expert_pe(M, k, e, r):
            expert_up_pe(M, k, e, r)
            expert_wT_pe(M, k, e, r)
            for hf in range(M.nf - 1):
                expert_turn_pe(M, k, e, hf, r)
            if e:
                expert_down_pe(M, k, e - 1, r)
            expert_turn_pe(M, k, e, M.nf - 1, r)
            if e:
                expert_back_pe(M, k, e - 1, r)

        def expert_act(M, k, e, r):
            for hf in range(M.nf):
                copy_up(M, k, e, hf, r, 0)
                if M.gate is not None:
                    copy_up(M, k, e, hf, r, 1)
            copy_wT_act(M, k, e, r)
            for hf in range(M.nf - 1):
                silu_act(M, k, e, hf, r)
            if e and M.gate is None:
                copy_z(M, k, e - 1, 0, r)
            silu_act(M, k, e, M.nf - 1, r)

        def expert_dve(M, k, e, r):
            if M.gate is None:
                for hf in range(M.nf):
                    copy_up(M, k, e, hf, r, 1)
            for hf in range(M.nf - 1):
                act_dve(M, k, e, hf, r)
            if e:
                if M.gate is not None:
                    copy_z(M, k, e - 1, 0, r)
                copy_z(M, k, e - 1, 1, r)
            act_dve(M, k, e, M.nf - 1, r)
            if e:
                add_y_dve(M, k, e - 1, r)

        def expert_pool(M, k, e, r):
            pool = nc.gpsimd
            b = e % 2
            at = (r * (2 * C)) + e * C
            if e >= 2:
                wait_moe_done(pool, M, place_up(M, e - 2, M.nf - 1, 1), r, k)
            nc.gpsimd.nop(nofuse=True)
            nc.gpsimd.tensor_copy(xs[:, b * KD:(b + 1) * KD, :], xgT[:, :, bass.ds(at, C)]).then_inc(M.xs, 1)
            if e >= 2:
                pool.wait_ge(M.w_turned, nth(e - 1, 1, r, k))
            nc.gpsimd.nop(nofuse=True)
            for t in range(T):
                last = nc.gpsimd.tensor_copy(ws[:, b * T + t, :].rearrange("p (j c) -> p j c", c=C),
                                             wsel[:, t, bass.ds(at, C)].unsqueeze(1).broadcast_to([P, 4, C]))
            last.then_inc(M.ws, 1)

        def all_experts(eng, step, M, k, between=None):
            step(M, k, 0, 0)
            step(M, k, 1, 0)
            if between:
                between()
            with eng.Fori(0, EP // 2 - 1) as r:
                step(M, k, 2, r)
                step(M, k, 3, r)

        def pass_pe(M, k):
            gather_pe(M, k, 0)
            all_experts(nc.tensor, expert_pe, M, k, lambda: gather_pe(M, k, 1))
            expert_down_pe(M, k, EP - 1, 0)
            expert_back_pe(M, k, EP - 1, 0)

        def pass_act(M, k):
            gather_act(M, k, 0)
            all_experts(nc.scalar, expert_act, M, k, lambda: gather_act(M, k, 1))
            if M.gate is None:
                copy_z(M, k, EP - 1, 0, 0)

        def pass_dve(M, k, half):
            select_dve(M, k, half)
            gather_dve(M, k, 0)
            all_experts(nc.vector, expert_dve, M, k, lambda: gather_dve(M, k, 1))
            if M.gate is not None:
                copy_z(M, k, EP - 1, 0, 0)
            copy_z(M, k, EP - 1, 1, 0)
            add_y_dve(M, k, EP - 1, 0)

        def pass_pool(M, k):
            def gathered(part):
                nc.gpsimd.wait_ge(M.xg_act, (k * KD) + 4 * (part + 1))
                nc.gpsimd.wait_ge(M.xg_dve, (k * KD) + 4 * (part + 1))

            nc.gpsimd.wait_ge(M.wsel, k + 1)
            gathered(0)
            nc.gpsimd.nop(nofuse=True)
            all_experts(nc.gpsimd, expert_pool, M, k, lambda: (gathered(1), nc.gpsimd.nop(nofuse=True)))

        def load_expert(M, k, e, r, src, free):
            def put(i, rows_):
                free(M, k, i, r)
                slot = (M.first + i) % SLOTS
                nc.sync.dma_start(ring[slot][:, :, :].rearrange("p a b -> p (a b)").rearrange("p (k n) -> p k n", n=rows_.shape[2]),
                                  rows_).then_inc(M.arrived[slot], 16)

            if e < EP:
                x = (r * 2) + e
                for hf in range(M.nf):
                    for up in range(2):
                        put(place_up(M, e, hf, up), src(up, x, hf))
            if e:
                x = (r * 2) + (e - 1)
                for n in range(M.nd):
                    put(place_down(M, e - 1, n), src(2, x, n))

        def pass_sp(M, k, src, free):
            all_experts(nc.sync, lambda M, k, e, r: load_expert(M, k, e, r, src, free), M, k)
            load_expert(M, k, EP, 0, src, free)

        def free_in_pass(M, k, i, r):
            nc.sync.wait_ge(M.done, nth(M.done0 + i + 1 - SLOTS, M.per, r, k - M.k0))

        def src1(half):
            def src(what, x, n):
                if what == 2:
                    return w_down[0, x + EP * half].rearrange("(k p) n -> p k n", p=P)
                return (w_up if what else w_gate)[0, x + EP * half].rearrange("(p k) n -> p k n", p=P)
            return src

        def src2(l):
            def src(what, x, n):
                w = (moe_w_gate, moe_w_up, moe_w_down)[what][l, x][:, n * NC:(n + 1) * NC]
                return w.rearrange("(k p) n -> p k n" if what == 2 else "(p k) n -> p k n", p=P)
            return src

        main = (arrived, item_done)
        M1 = Mixture(kind1, 1, 1, *main, ITEM["moe", 0], done_at[ITEM["moe", 0]] - 1, 0, col("norm_ffn"), None, None)
        MX = Mixture(kind1, 1, 1, [sem(f"more_arrived{i}") for i in range(SLOTS)], sem("more_item_done"), 0, 0, 2, col("norm_ffn"), None, None)
        shifted = sem("slots_shifted")

        def more_passes(eng, one_pass, at_end=None):
            eng.wait_ge(flag_done, 1)
            passes = eng.value_load(flag[0:1, 0:1], min_val=0, max_val=PC)
            with eng.If(passes > 0):
                with eng.Fori(0, passes) as p:
                    for half in range(2):
                        one_pass(p, (p * 2) + (2 + half), half)
                if at_end:
                    eng.wait_ge(MX.y_added, (passes * (2 * 4 * EP)) + 2 * 4 * EP)
                    eng.nop(nofuse=True)

        def more_dve(p, k, half):
            if half == 0:
                nc.vector.tensor_scalar(rankm[:, :, :], rankm[:, :, :], -float(C), None, ALU.add).then_inc(shifted, 1)
                nc.vector.wait_ge(shifted, p + 1)
            pass_dve(MX, k, half)

        def free_more(M, k, i, r):
            if i < SLOTS and isinstance(r, int):
                nc.sync.wait_ge(MX.sel, k + 1)
            else:
                free_in_pass(M, k, i, r)

        M2 = [Mixture(kind2, 2, 2, *main, ITEM["moe", 1 + l], done_at[ITEM["moe", 1 + l]] - 1, l, mod[:, l, 3, :], mod[:, l, 2, :],
                      gate_rows[:, l, 1, :]) for l in range(2)]

        NH2 = 6
        KB = 2 * T
        DV = 2 * HD
        AW = NH2 * DV
        arena_at[0] = 0
        qT2, kT2 = carve(NH2, S), carve(NH2, 2 * S)
        v_at = arena_at[0]
        v2 = carve(KB, AW)
        ctx_at = arena_at[0]
        ctxT = carve(KD, S)
        temps2_at = arena_at[0]
        sq2, qn2, tmp2 = carve(2, NC), carve(2, NC), carve(NC)
        ctx_rows = carve(T, D, at=v_at)
        fT = carve(2, S, at=ctx_at)
        fCS = carve(T, NC, at=temps2_at)
        pr2 = carve(4, NC, at=ctx_at)
        mixw, mixT = carve(2, NC), carve(2, NC)
        V0 = 2 * AW

        def block(a, t):
            return a[:, :, t * P:(t + 1) * P]

        q_row, k_row = row("q_att"), row("k_att")
        units2 = []
        for n in range(5):
            for t in range(T):
                un = dict(item=ITEM["proj2"] + n, lhs=block(hT, t), cols=(0, NC), kind="qk", rope=rope_of(rope2, t))
                if n == 0:
                    un.update(gains=[(8, q_row)], put=[(0, 4, block(qT2[:, 0:4, :], t))])
                elif n == 1:
                    un.update(gains=[(4, q_row), (4, k_row)],
                              put=[(0, 2, block(qT2[:, 4:6, :], t)), (2, 2, block(kT2[:, 0:2, :], t))])
                elif n == 2:
                    un.update(gains=[(8, k_row)], put=[(0, 4, block(kT2[:, 2:6, :], t))])
                else:
                    w = (NC, AW - NC)[n - 3]
                    un.update(kind="v", cols=(0, w), put=[((0, w), v2[:, t, (n - 3) * NC:(n - 3) * NC + w])])
                units2.append(un)
            for t in range(T):
                un = dict(item=ITEM["proj2"] + n, lhs=block(ctxT, t), cols=(0, NC), kind="qk", rope=None)
                if n == 0:
                    continue
                if n == 1:
                    un.update(cols=(NC // 2, NC // 2), gains=[(4, k_row)], put=[(0, 2, block(kT2[:, 0:2, :], T + t))])
                elif n == 2:
                    un.update(gains=[(8, k_row)], put=[(0, 4, block(kT2[:, 2:6, :], T + t))])
                else:
                    w = (NC, AW - NC)[n - 3]
                    un.update(kind="v", cols=(0, w), put=[((0, w), v2[:, T + t, (n - 3) * NC:(n - 3) * NC + w])])
                units2.append(un)
        FIRST_CTX = next(u for u, un in enumerate(units2) if un["rope"] is None and un["kind"] == "qk")
        units2[FIRST_CTX]["ready"] = hT_ready(4)
        h2 = heads("h2", units2, sq2, qn2, tmp2, hT_ready(3))
        NU2 = len(units2)

        ft_c, fa_mm, fa_c, fy_mm, fy_c = sem("ft_c"), sem("fa_mm"), sem("fa_c"), sem("fy_mm"), sem("fy_c")

        def fourier_pe():
            pe = nc.tensor
            i = ITEM["proj2"] + 4
            for b in range(2):
                for k in range(KD):
                    last = nc.tensor.matmul(bank[4][:, b * S:(b + 1) * S], ring[i % SLOTS][:, k, S + b * P:S + (b + 1) * P],
                                            hT[:, k, :], start=(k == 0), stop=(k == KD - 1))
            last.then_inc(item_done, 1)
            pe.wait_ge(ft_c, 1)
            for t in range(T):
                for b in range(2):
                    last = nc.tensor.matmul(bank[4 + t][:, b * S:(b + 1) * S], fT[:, b, t * P:(t + 1) * P], const("chan"),
                                            start=True, stop=True)
            last.then_inc(fa_mm, 1)
            pe.wait_ge(fa_c, 1)
            for t2 in range(T):
                n = 0
                for t in range(T):
                    for c, name in enumerate(("dftc", "dfts")):
                        rhs = fCS[:, t, :].rearrange("p (b c d) -> p c b d", b=2, c=2)[:, c, :, :]
                        last = nc.tensor.matmul(bank[4 + t2][:, 0:S], const(name)[:, t * S + t2 * P:t * S + (t2 + 1) * P], rhs,
                                                start=(n == 0), stop=(n == 3))
                        n += 1
            last.then_inc(fy_mm, 1)

        def fourier_act():
            act = nc.scalar
            act.wait_ge(item_done, done_at[ITEM["proj2"] + 4])
            act.activation(fT[:, :, :], bank[4][:, :].rearrange("p (b s) -> p b s", b=2), ACT.Copy).then_inc(ft_c, 1)
            act.wait_ge(fa_mm, 1)
            for s_, v in h2["done"]:
                act.wait_ge(s_, v)
            for t in range(T):
                last = nc.scalar.activation(fCS[:, t, :], bank[4 + t][:, :], ACT.Copy)
            last.then_inc(fa_c, 1)
            act.wait_ge(fy_mm, 1)
            for t in range(T):
                last = nc.scalar.activation(xn[:, t, AW:D], bank[4 + t][:, 0:S], ACT.Copy)
            last.then_inc(fy_c, 1)

        a2_s, a2_m, a2_e, a2_r, a2_p, a2_w = (sem("a2_" + n) for n in ("scores", "max", "exp", "recip", "first", "mixed"))
        a2_t, a2_c, a2_v, a2_o, a2_q, a2_n = (sem("a2_" + n) for n in ("turned", "copied", "values", "out", "outsq", "normed"))
        att2 = [(t, hd) for t in range(T) for hd in range(NH2)]
        negm2, lsum2, neglam = small[:, 160:184], small[:, 184:208], small[:, 208:209]
        r2 = small[:, 212:216]

        def lambda_dve():
            v = nc.vector
            lp = small[:, 216:218]
            for n in range(2):
                dve_step(v.tensor_tensor(tmp2[:, 0:HD], row(f"lam_q{n + 1}"), row(f"lam_k{n + 1}"), ALU.mult))
                ins = v.tensor_reduce(lp[:, n:n + 1], tmp2[:, 0:HD], AX.X, ALU.add)
                dve_step(ins) if n == 0 else ins.then_inc(lam_dot, 1)
            v.wait_ge(lam_exp, 1)
            dve_step(v.tensor_tensor(neglam, lp[:, 1:2], lp[:, 0:1], ALU.subtract))
            dve_step(v.tensor_scalar(neglam, neglam, -LAM_INIT, None, ALU.add))
            dve_step(v.tensor_scalar(cols[0:AW // KD, COLS.index("subln"), :], cols[0:AW // KD, COLS.index("subln"), :],
                                     (1.0 - LAM_INIT) * float(DV) ** 0.5, None, ALU.mult))

        lam_dot, lam_exp = sem("lam_dot"), sem("lam_exp")

        def lambda_act():
            nc.scalar.wait_ge(lam_dot, 1)
            nc.scalar.activation(small[:, 216:218], small[:, 216:218], ACT.Exp).then_inc(lam_exp, 1)

        def scores2_pe(u):
            pe = nc.tensor
            t, hd = att2[u]
            if u == 0:
                pe.wait_ge(fy_c, 1)
                for s_, v in h2["done"]:
                    pe.wait_ge(s_, v)
            for m in range(2):
                w = 2 * u + m
                if w >= 3:
                    pe.wait_ge(a2_e, w - 2)
                nc.tensor.matmul(bank[w % 3][:, :], qT2[m * HD:(m + 1) * HD, hd, t * P:(t + 1) * P],
                                 kT2[m * HD:(m + 1) * HD, hd, :], start=True, stop=True).then_inc(a2_s, 1)

        def max2_dve(u):
            for m in range(2):
                w = 2 * u + m
                nc.vector.wait_ge(a2_s, w + 1)
                nc.vector.tensor_reduce(negm2[:, w:w + 1], bank[w % 3][:, :], AX.X, ALU.max, negate=True).then_inc(a2_m, 1)

        def exp2_act(u):
            for m in range(2):
                w = 2 * u + m
                nc.scalar.wait_ge(a2_m, w + 1)
                if u >= 2:
                    nc.scalar.wait_ge(a2_w, u - 1)
                nc.scalar.activation(pr2[:, w % 4, :], bank[w % 3][:, :], ACT.Exp, bias=negm2[:, w:w + 1],
                                     accum_out=lsum2[:, w:w + 1]).then_inc(a2_e, 1)

        def recip2_dve(u):
            v = nc.vector
            r = r2[:, 2 * (u % 2):2 * (u % 2) + 2]
            v.wait_ge(a2_e, 2 * u + 2)
            dve_step(v.reciprocal(r, lsum2[:, 2 * u:2 * u + 2]))
            v.tensor_tensor(r[:, 1:2], r[:, 1:2], neglam, ALU.mult).then_inc(a2_r, 1)

        def first2_act(u):
            act = nc.scalar
            act.wait_ge(a2_r, u + 1)
            if u >= 2:
                act.wait_ge(a2_t, u - 1)
            nc.scalar.activation(mixw[:, u % 2, :], pr2[:, 2 * (u % 2), :], ACT.Copy,
                                 scale=r2[:, 2 * (u % 2):2 * (u % 2) + 1]).then_inc(a2_p, 1)

        def mix2_dve(u):
            v = nc.vector
            v.wait_ge(a2_p, u + 1)
            v.wait_ge(a2_r, u + 1)
            v.scalar_tensor_tensor(mixw[:, u % 2, :], pr2[:, 2 * (u % 2) + 1, :], r2[:, 2 * (u % 2) + 1:2 * (u % 2) + 2],
                                   mixw[:, u % 2, :], ALU.mult, ALU.add).then_inc(a2_w, 1)

        def turn2_pe(u):
            pe = nc.tensor
            pe.wait_ge(a2_w, u + 1)
            if u:
                pe.wait_ge(a2_c, u)
            for b in range(KB):
                last = nc.tensor.transpose(bank[3][:, b * P:(b + 1) * P], mixw[:, u % 2, b * P:(b + 1) * P], ident)
            last.then_inc(a2_t, 1)

        def copy2_act(u):
            nc.scalar.wait_ge(a2_t, u + 1)
            if u >= 2:
                nc.scalar.wait_ge(a2_v, u - 1)
            nc.scalar.activation(mixT[:, u % 2, :], bank[3][:, :], ACT.Copy).then_inc(a2_c, 1)

        def values2_pe(u):
            pe = nc.tensor
            t, hd = att2[u]
            pe.wait_ge(a2_c, u + 1)
            if t and hd == 0:
                pe.wait_ge(a2_o, 1)
            for b in range(KB):
                last = nc.tensor.matmul(bank[6 + hd // 4][:, (hd % 4) * DV:(hd % 4 + 1) * DV], mixT[:, u % 2, b * P:(b + 1) * P],
                                        v2[:, b, hd * DV:(hd + 1) * DV], start=(b == 0), stop=(b == KB - 1))
            last.then_inc(a2_v, 1)

        sq_out = tmp2

        def out2_dve(t):
            v = nc.vector
            s6, r6 = small[:, 218:224], small[:, 224:230]
            v.wait_ge(a2_v, NH2 * (t + 1))
            for n, (h0, nh) in enumerate(((0, 4), (4, 2))):
                dst = xn[:, t, h0 * DV:(h0 + nh) * DV]
                dve_step(v.tensor_copy(dst, bank[6 + n][:, 0:nh * DV]))
                dve_step(v.tensor_tensor(out_scaled[:, 0:nh * DV], dst, dst, ALU.mult))
                ins = v.tensor_reduce(s6[:, h0:h0 + nh], out_scaled[:, 0:nh * DV].rearrange("p (h d) -> p h d", d=DV), AX.X, ALU.add)
                rooted(ins, s6, DV) if n else dve_step(ins)
            o = xn[:, t, 0:AW].rearrange("p (h d) -> p h d", d=DV)
            v.tensor_tensor(o, o, r6.unsqueeze(2).broadcast_to([P, NH2, DV]), ALU.mult).then_inc(a2_o, 1)

        L2 = len(att2) - 1

        def steps2():
            for u in range(NU2):
                yield "proj", u
                if u >= 2:
                    yield "tr", u - 2
            yield "tr", NU2 - 2
            yield "tr", NU2 - 1
            yield "fourier", 0
            s = 6
            for u in range(L2 + 4):
                if u <= L2:
                    yield "scores", u
                if 1 <= u <= L2 + 1:
                    yield "mix", u - 1
                if 2 <= u <= L2 + 2:
                    yield "turn", u - 2
                if u >= 3:
                    yield "values", u - 3
                    if (u - 3) % NH2 == NH2 - 1:
                        yield "out", (u - 3) // NH2
                if u % 2 == 0 and s < 12:
                    yield "ada_mm", s
                if u % 2 == 1 and s < 12:
                    yield "ada_sum", s
                    s += 1

        def block2_pe():
            tr_pe(3, [(xn_done, 6)])
            for what, i in steps2():
                if what == "proj":
                    if i == FIRST_CTX:
                        tr_pe(4, [(xn_done, 8), (h2["put"], FIRST_CTX - 2)])
                    h2["proj_pe"](i)
                elif what == "tr":
                    h2["tr_pe"](i)
                elif what == "fourier":
                    fourier_pe()
                elif what == "scores":
                    scores2_pe(i)
                elif what == "turn":
                    turn2_pe(i)
                elif what == "values":
                    values2_pe(i)
                elif what == "ada_mm":
                    ada_mm_pe(i)
                elif what == "ada_sum":
                    ada_sum_pe(i)
            tr_pe(5, [(a2_o, 2)])
            out_pe(1, hT, hT_ready(5))

        def block2_act(ready):
            norm_act(2, h, 3, ready)
            tr_act(3, hT, mod[:, 0, 1, :], mod[:, 0, 0, :])
            norm_act(3, ctx_rows, 4, [(ctx_loaded, 16)])
            lambda_act()
            for what, i in steps2():
                if what == "proj":
                    if i == FIRST_CTX:
                        tr_act(4, ctxT, mod_ctx[:, 1, :], mod_ctx[:, 0, :])
                    h2["post_act"](i)
                elif what == "tr":
                    h2["put_act"](i)
                elif what == "fourier":
                    fourier_act()
                elif what == "scores":
                    exp2_act(i)
                elif what == "mix":
                    first2_act(i)
                elif what == "turn":
                    copy2_act(i)
                elif what == "ada_mm":
                    ada_rows_act(i)
            tr_act(5, hT, col("subln"), None)

        def block2_dve(ready):
            norm_dve(2, h, 3, ready)
            tr_dve(3, hT, mod[:, 0, 1, :], mod[:, 0, 0, :])
            norm_dve(3, ctx_rows, 4, [(ctx_loaded, 16)])
            lambda_dve()
            for what, i in steps2():
                if what == "proj":
                    if i == FIRST_CTX:
                        tr_dve(4, ctxT, mod_ctx[:, 1, :], mod_ctx[:, 0, :])
                    h2["post_dve"](i)
                elif what == "scores":
                    max2_dve(i)
                    recip2_dve(i)
                elif what == "mix":
                    mix2_dve(i)
                elif what == "out":
                    out2_dve(i)
                elif what == "ada_sum":
                    ada_use_dve(i)
            tr_dve(5, hT, col("subln"), None)
            out_dve(1, gate_rows[:, 0, 0, :])

        def block2_pool():
            norm_pool(2)
            norm_pool(3)
            for what, i in steps2():
                if what == "proj":
                    h2["rope_pool"](i)
                elif what == "out":
                    root_pool(small[:, 224:230], small[:, 218:224])

        arena_at[0] = 0
        cg = carve(4, S)
        zp = carve(KD, S + 2)
        conv = carve(KD, S)
        mix3 = carve(KD, S)
        c_copied, z_done, cv_done, mix_done = sem("c_copied"), sem("z_done"), sem("conv_done"), sem("mix_done")

        def odd_banks(i):
            return [bank[2 * (i % 3)], bank[2 * (i % 3) + 1]]

        def odd_pe():
            pe = nc.tensor
            tr_pe(7, [(xn_done, 12)])
            for s_, v in hT_ready(7):
                pe.wait_ge(s_, v)
            for i in range(6):
                it = ITEM["proj3"] + i
                wait_item(pe, it)
                if i >= 3:
                    if i == 3:
                        pe.wait_ge(c_copied, 1)
                    elif i == 4:
                        pe.wait_ge(z_done, 4)
                    else:
                        pe.wait_ge(mix_done, 4)
                for b in range(4):
                    for k in range(KD):
                        last = nc.tensor.matmul(odd_banks(i)[b // 2][:, (b % 2) * S:(b % 2 + 1) * S],
                                                ring[it % SLOTS][:, k, b * P:(b + 1) * P], hT[:, k, :],
                                                start=(k == 0), stop=(k == KD - 1))
                last.then_inc(item_done, 1)
            out_pe(2, mix3, [(mix_done, 8)])

        def odd_act(ready):
            norm_act(5, h, 7, ready)
            tr_act(7, hT, mod[:, 1, 1, :], mod[:, 1, 0, :])
            for n in range(2):
                i = 3 * n
                nc.scalar.wait_ge(item_done, done_at[ITEM["proj3"] + i])
                if n:
                    nc.scalar.wait_ge(z_done, 4)
                for b in range(2):
                    last = nc.scalar.activation(cg[:, 2 * b:2 * b + 2, :], odd_banks(i)[b][:, :].rearrange("p (a s) -> p a s", a=2), ACT.Copy)
                last.then_inc(c_copied, 1)

        def odd_dve(ready):
            v = nc.vector
            norm_dve(5, h, 7, ready)
            tr_dve(7, hT, mod[:, 1, 1, :], mod[:, 1, 0, :])
            dve_step(v.memset(zp[:, :, 0:1], 0.0))
            dve_step(v.memset(zp[:, :, S + 1:S + 2], 0.0))
            for n in range(2):
                i = 3 * n
                v.wait_ge(item_done, done_at[ITEM["proj3"] + i + 1])
                v.wait_ge(c_copied, n + 1)
                for b in range(4):
                    v.tensor_tensor(zp[:, 4 * n + b, 1:S + 1], odd_banks(i + 1)[b // 2][:, (b % 2) * S:(b % 2 + 1) * S],
                                    cg[:, b, :], ALU.mult).then_inc(z_done, 1)
                v.wait_ge(z_done, 4 * (n + 1))
                for j in range(3):
                    for b in range(4):
                        c = 4 * n + b
                        w = col(f"conv{j}")[:, c:c + 1]
                        if j == 0:
                            ins = v.tensor_scalar(conv[:, c, :], zp[:, c, 0:S], w, None, ALU.mult)
                        else:
                            ins = v.scalar_tensor_tensor(conv[:, c, :], zp[:, c, j:j + S], w, conv[:, c, :], ALU.mult, ALU.add)
                        ins.then_inc(cv_done, 1)
                    v.wait_ge(cv_done, 12 * n + 4 * (j + 1))
                v.wait_ge(item_done, done_at[ITEM["proj3"] + i + 2])
                for b in range(4):
                    c = 4 * n + b
                    v.tensor_tensor(mix3[:, c, :], conv[:, c, :], odd_banks(i + 2)[b // 2][:, (b % 2) * S:(b % 2 + 1) * S],
                                    ALU.mult).then_inc(mix_done, 1)
            out_dve(2, gate_rows[:, 1, 0, :])

        stored = sem("stored")
        block = stack.enter_context(nc.Block())

        @block.sync
        def _(sp):
            sp.dma_start(h[:, :, :], x[0].rearrange("(t p) d -> p t d", p=P)).then_inc(x_loaded, 16)
            sp.dma_start(cols[:, :, :], cols_in.rearrange("p (n k) -> p n k", k=KD)).then_inc(const_loaded, 16)
            sp.dma_start(cb[:, :], const_in).then_inc(const_loaded, 16)
            sp.dma_start(router_sb[:, :, :], router.rearrange("(p k) n -> p k n", k=KD)).then_inc(const_loaded, 16)
            sp.dma_start(rows[:, :], rows_in.broadcast_to([P, sum(ROW_W)])).then_inc(const_loaded, 16)
            big = {"w_in": w_in[0], "w_out": w_out[0], "attn_w_in": attn_w_in[0], "attn_w_out": attn_w_out[0],
                   "conv_w_in": conv_w_in[0], "conv_w_out": conv_w_out[0]}

            def load(a, b):
                for i in range(a, b):
                    what = items[i]
                    if i >= SLOTS:
                        sp.wait_ge(*released[i - SLOTS])
                    src, c = (ada_w[what[1]], what[2]) if what[0] == "ada" else (big[what[0]], what[1])
                    order = "(k p) n -> p k n" if what[0] == "conv_w_out" else "(p k) n -> p k n"
                    sp.dma_start(ring[i % SLOTS][:, :, :], src[:, c:c + NC].rearrange(order, p=P)).then_inc(arrived[i % SLOTS], 16)

            def free_main(M, k, i, r):
                j = M.first + i - SLOTS
                if i < SLOTS and isinstance(r, int) and k == M.k0:
                    sp.wait_ge(*released[j])
                else:
                    free_in_pass(M, k, i, r)

            load(0, ITEM["moe", 0])
            for half in range(2):
                pass_sp(M1, half, src1(half), free_main)
            more_passes(sp, lambda p, k, half: pass_sp(MX, k, src1(half), free_more), at_end=True)
            sp.wait_ge(M1.y_added, 8 * EP)
            sp.dma_start(ctx_rows[:, :, :], ctx_in[0].rearrange("(t p) d -> p t d", p=P)).then_inc(ctx_loaded, 16)
            load(ITEM["proj2"], ITEM["moe", 1])
            pass_sp(M2[0], 0, src2(0), free_main)
            load(ITEM["proj3"], ITEM["moe", 2])
            pass_sp(M2[1], 1, src2(1), free_main)
            sp.wait_ge(M2[1].y_added, 8 * EP)
            sp.dma_start(out[0].rearrange("(t p) d -> p t d", p=P), h[:, :, :]).then_inc(stored, 16)
            sp.wait_ge(stored, 16)

        @block.gpsimd
        def _(pool):
            nc.gpsimd.memset(zero_col[:, :], 0.0)
            nc.gpsimd.memset(minus_half[:, :], -0.5)
            nc.gpsimd.memset(condT[:, :, :], 0.0).then_inc(setup_done, 1)
            block1_pool()
            norm_pool(1)
            for k in range(2):
                pass_pool(M1, k)
            more_passes(pool, lambda p, k, half: pass_pool(MX, k))
            block2_pool()
            norm_pool(4)
            pass_pool(M2[0], 0)
            norm_pool(5)
            norm_pool(6)
            pass_pool(M2[1], 1)

        @block.scalar
        def _(act):
            act.wait_ge(setup_done, 1)
            act.wait_ge(const_loaded, 16 * 4)
            for c, name in enumerate(("c", "c_ctx")):
                nc.scalar.activation(condT[:, :, c], col(name), ACT.Silu).then_inc(cond_done, 1)
            for l in range(2):
                for n, sec in enumerate((G_M, G_F)):
                    act.dma_start(gate_rows[:, l, n, :], ada_b[l:l + 1, sec * D:(sec + 1) * D].broadcast_to([P, D])).then_inc(gate_loaded, 16)
            block1_act()
            norm_act(1, h, 2, [(out_added, 4)])
            tr_act(2, hT, col("norm_ffn"), None)
            route1_act()
            for k in range(2):
                pass_act(M1, k)
            more_passes(act, lambda p, k, half: pass_act(MX, k), at_end=True)
            block2_act([(M1.y_added, 8 * EP)])
            norm_act(4, h, 6, [(out_added, 8)])
            tr_act(6, hT, mod[:, 0, 3, :], mod[:, 0, 2, :])
            route2_act(0)
            pass_act(M2[0], 0)
            odd_act([(M2[0].y_added, 4 * EP)])
            norm_act(6, h, 8, [(out_added, 12)])
            tr_act(8, hT, mod[:, 1, 3, :], mod[:, 1, 2, :])
            route2_act(1)
            pass_act(M2[1], 1)

        @block.vector
        def _(dve):
            dve.wait_ge(setup_done, 1)
            dve.wait_ge(const_loaded, 16 * 4)
            for name in ("k_fox", "k_dil", "k_att"):
                dve_step(nc.vector.tensor_scalar(row(name), row(name), float(HD) ** 0.5, None, ALU.mult))
            block1_dve()
            norm_dve(1, h, 2, [(out_added, 4)])
            tr_dve(2, hT, col("norm_ffn"), None)
            route1_dve()
            for k in range(2):
                pass_dve(M1, k, k)
            more_passes(dve, more_dve, at_end=True)
            block2_dve([(M1.y_added, 8 * EP)])
            norm_dve(4, h, 6, [(out_added, 8)])
            tr_dve(6, hT, mod[:, 0, 3, :], mod[:, 0, 2, :])
            route2_dve(0)
            pass_dve(M2[0], 0, 0)
            odd_dve([(M2[0].y_added, 4 * EP)])
            norm_dve(6, h, 8, [(out_added, 12)])
            tr_dve(8, hT, mod[:, 1, 3, :], mod[:, 1, 2, :])
            route2_dve(1)
            pass_dve(M2[1], 1, 0)

        @block.tensor
        def _(pe):
            block1_pe()
            tr_pe(2, [(xn_done, 4)])
            logits_pe(0, 2, 0, G1 + E1)
            rank_pe()
            for k in range(2):
                pass_pe(M1, k)
            more_passes(pe, lambda p, k, half: pass_pe(MX, k))
            block2_pe()
            tr_pe(6, [(xn_done, 10)])
            logits_pe(1, 6, G1 + E1, E2)
            route2_pe(0)
            pass_pe(M2[0], 0)
            odd_pe()
            tr_pe(8, [(xn_done, 14)])
            logits_pe(2, 8, G1 + E1 + E2, E2)
            route2_pe(1)
            pass_pe(M2[1], 1)


_BIG = ["x", "ctx_2", "w_in", "w_out", "w_gate", "w_up", "w_down", "ada_w_2", "ada_b_2", "attn_w_in_2", "attn_w_out_2",
        "conv_w_in_2", "conv_w_out_2", "moe_w_gate_2", "moe_w_up_2", "moe_w_down_2"]


def layout(inputs):
    a = {n: np.asarray(v) for n, v in inputs.items()}
    f = np.float32
    pk = lambda v: v.reshape(P, KD)
    bf = np.zeros((P, KD), f)
    bf[:N_HEADS, 0] = a["b_forget"][0]
    b = a["ada_b_2"].reshape(2, 6, D)
    per = {"norm_mix": pk(a["norm_mix"][0]), "norm_ffn": pk(a["norm_ffn"][0]),
           "out_norm": pk(np.concatenate([a["out_norm_fox"][0], a["out_norm_dil"][0]])),
           "norm_mix0": pk(a["norm_mix_2"][0]), "norm_mix1": pk(a["norm_mix_2"][1]),
           "norm_ffn0": pk(a["norm_ffn_2"][0]), "norm_ffn1": pk(a["norm_ffn_2"][1]),
           "subln": pk(np.concatenate([a["attn_subln_2"][0]] * 6 + [np.ones(D - 6 * 2 * HD, f)])),
           "c": pk(a["c_2"][0]), "c_ctx": pk(a["c_ctx_2"]), "b_forget": bf}
    for l in range(2):
        for s in (SH_M, SC_M, SH_F, SC_F):
            per[f"b{l}{s}"] = pk(b[l, s])
    for j in range(3):
        per[f"conv{j}"] = a["conv_w_2"][0, j].reshape(KD, P).T
    every = [a[n][0] for n in ("q_norm_fox", "k_norm_fox", "q_norm_dil", "k_norm_dil", "attn_q_norm_2", "attn_k_norm_2",
                               "lam_q1_2", "lam_k1_2", "lam_q2_2", "lam_k2_2")]
    every += [a["b_router_group"][0], a["b_router_expert"][0].reshape(-1)]
    router = [a["w_router_group"][0], a["w_router_expert"][0].transpose(1, 0, 2).reshape(D, E1),
              a["router_w_2"][0], a["router_w_2"][1], a["w_in"][0][:, 6 * NC:]]
    return {"router": np.concatenate(router, 1), "const": CONST, "cols": np.concatenate([per[n] for n in COLS], 1),
            "rows": np.concatenate(every)[None, :]}


N_HEADS = 8


def kernel(**inputs):
    import concourse.bacc as _bacc
    from concourse.bass_utils import run_bass_kernel_spmd as _run

    nc = _bacc.Bacc("TRN2", target_bir_lowering=False, num_devices=1)
    arrays = {n: np.ascontiguousarray(inputs[n]) for n in _BIG}
    arrays.update({n: np.ascontiguousarray(v) for n, v in layout(inputs).items()})
    args = [nc.dram_tensor(f"in_{n}", a.shape, mybir.dt.from_np(a.dtype), kind="ExternalInput").ap() for n, a in arrays.items()]
    out = nc.dram_tensor("out", (1, S, D), F32, kind="ExternalOutput").ap()
    transformer_blocks(nc, *args, out)
    r = _run(nc, [{f"in_{n}": a for n, a in arrays.items()}], core_ids=[0])
    return r.results[0]["out"]
```

```python
from contextlib import ExitStack

import numpy as np

import concourse.bass as bass
from concourse import mybir

F32 = mybir.dt.float32
I32 = mybir.dt.int32
ALU = mybir.AluOpType
ACT = mybir.ActivationFunctionType
AX = mybir.AxisListType

P = 128
S = 256
T = S // P
D = 1024
KD = D // P
NC = 512
HD = 64
EPS = 1e-6
NEG = -1e30
SLOTS = 6
C = 32
E1, E2 = 32, 16
EP = 16
G1 = 4
PC = 7
ARENA = 12288
LAM_INIT = 0.8 - 0.6


class Mixture:

    def __init__(self, steps, nf, nd, arrived, done, first, done0, k0, scale, shift, gate):
        self.nf, self.nd, self.per = nf, nd, 2 * nf + nd
        self.arrived, self.done = arrived, done
        self.first, self.done0, self.k0 = first, done0, k0
        self.scale, self.shift, self.gate = scale, shift, gate
        (self.sel, self.wsel, self.gathered, self.xg_act, self.xg_dve, self.xs, self.ws, self.g_copied, self.u_copied,
         self.turned, self.silu, self.act, self.z0, self.z1, self.w_turned, self.wT, self.y, self.y_added) = steps


def rope_tables(ang, half):
    sign = np.where((np.arange(HD) // half) % 2 == 0, -1.0, 1.0)
    return np.cos(ang), np.sin(ang) * sign


def constants():
    p = np.arange(P)
    blocks = lambda a: a.reshape(T, P, -1).transpose(1, 0, 2).reshape(P, -1)
    q, k = np.arange(S)[:, None], np.arange(S)[None, :]
    d = q - k
    causal = np.where(d >= 0, 0.0, NEG)
    count = sum(((d >= 0) & (d % r == 0) & (d // r <= P)).astype(np.float64) for r in (1, 4, 16))
    dilated = np.where(count > 0, np.log(np.maximum(count, 1.0)), NEG)
    pos = np.arange(S, dtype=np.float32)
    inv = (1.0 / (np.float32(10000.0) ** (np.arange(0, HD, 2, dtype=np.float32) / np.float32(HD)))).astype(np.float32)
    a1 = pos[:, None] * inv[None, :]
    cos1, sin1 = rope_tables(np.concatenate([a1, a1], 1), HD // 2)
    nf = HD // 4
    inv2 = (np.float32(10000.0) ** (-np.arange(nf, dtype=np.float32) / np.float32(nf))).astype(np.float32)
    ar = np.floor(pos / HD).astype(np.float32)[:, None] * inv2
    ac = (pos % HD).astype(np.float32)[:, None] * inv2
    cos2, sin2 = rope_tables(np.concatenate([ar, ar, ac, ac], 1), nf)
    ws = 2 * np.pi * ((np.arange(S)[:, None] * np.arange(S)) % S) / S
    wd = 2 * np.pi * ((np.arange(HD)[:, None] * np.arange(HD)) % HD) / HD
    two = np.eye(2)
    parts = {
        "ident": np.eye(P), "before": p[:, None] < p[None, :], "ones": np.ones((P, P)),
        "row0": np.repeat((p % 32 == 0)[:, None], P, 1),
        "rows": np.stack([p % 32 == 0, p % 32 == 1], 1),
        "stack": p[:, None] % C == np.arange(C)[None, :],
        "iota": np.repeat(np.arange(C)[None, :], P, 0),
        "causal0": causal[:P, :P], "causal1": causal[P:, :],
        "dilated0": dilated[:P, :P], "dilated1": dilated[P:, :],
        "cos1": blocks(cos1), "sin1": blocks(sin1), "cos2": blocks(cos2), "sin2": blocks(sin2),
        "chan": np.concatenate([np.kron(two, np.cos(wd)), np.kron(two, np.sin(wd))], 1),
        "dftc": blocks(np.cos(ws) / np.sqrt(S * HD)), "dfts": blocks(-np.sin(ws) / np.sqrt(S * HD)),
    }
    at, cols = {}, 0
    for name, a in parts.items():
        at[name] = (cols, a.shape[1])
        cols += a.shape[1]
    return at, np.concatenate([a.astype(np.float32) for a in parts.values()], 1)


CONST_AT, CONST = constants()

COLS = ["norm_mix", "norm_ffn", "out_norm", "norm_mix0", "norm_mix1", "norm_ffn0", "norm_ffn1", "subln", "c", "c_ctx",
        "b00", "b01", "b03", "b04", "b10", "b11", "b13", "b14", "conv0", "conv1", "conv2", "b_forget"]
ROWS = ["q_fox", "k_fox", "q_dil", "k_dil", "q_att", "k_att", "lam_q1", "lam_k1", "lam_q2", "lam_k2", "b_router"]
ROW_W = [HD] * 10 + [G1 + E1]
ROW_AT = dict(zip(ROWS, np.cumsum([0] + ROW_W[:-1]).tolist()))

SH_M, SC_M, G_M, SH_F, SC_F, G_F = range(6)
EARLY = 4
W_IN_COLS = {"qa": 0, "ka": 512, "va": 1024, "qb": 1536, "kb": 2048, "vb": 2560}
CHUNKS1 = ["qa", "ka", "qb", "kb", "va", "vb"]


def plan_items():
    items, at = [], {}
    for c, name in enumerate(CHUNKS1):
        at["proj1", c] = len(items)
        items.append(("w_in", W_IN_COLS[name]))

    def conditioning(layer, sections):
        for c in sections:
            at["ada", 6 * layer + c] = len(items)
            items.extend(("ada", layer, c * D + n * NC) for n in range(2))

    conditioning(0, range(EARLY))
    at["out", 0] = len(items)
    items += [("w_out", n * NC) for n in range(2)]
    conditioning(0, range(EARLY, 6))
    at["moe", 0] = len(items)
    items += [("moe",)] * (3 * E1)
    at["proj2"] = len(items)
    items += [("attn_w_in", n * NC) for n in range(5)]
    conditioning(1, range(EARLY))
    at["out", 1] = len(items)
    items += [("attn_w_out", n * NC) for n in range(2)]
    conditioning(1, range(EARLY, 6))
    at["moe", 1] = len(items)
    items += [("moe",)] * (6 * E2)
    at["proj3"] = len(items)
    items += [("conv_w_in", s * D + n * NC) for n in range(2) for s in (1, 2, 0)]
    at["out", 2] = len(items)
    items += [("conv_w_out", n * NC) for n in range(2)]
    at["moe", 2] = len(items)
    items += [("moe",)] * (6 * E2)
    return items, at


def transformer_blocks(nc, x, ctx_in, w_in, w_out, w_gate, w_up, w_down, ada_w, ada_b, attn_w_in, attn_w_out,
                       conv_w_in, conv_w_out, moe_w_gate, moe_w_up, moe_w_down, router, const_in, cols_in, rows_in, out):
    items, ITEM = plan_items()
    stack = ExitStack()
    with stack:
        def sb(name, shape, dt=F32):
            return stack.enter_context(nc.sbuf_tensor(name, shape, dt))

        def sem(name):
            return stack.enter_context(nc.semaphore(name))

        bank = [stack.enter_context(nc.psum_tensor(f"bank{i}", [P, NC], F32)) for i in range(8)]

        ring = [sb(f"ring{i}", [P, KD, NC]) for i in range(SLOTS)]
        cb = sb("cb", [P, CONST.shape[1]])
        cols = sb("cols", [P, len(COLS), KD])
        rows = sb("rows", [P, sum(ROW_W)])
        router_sb = sb("router_sb", [P, KD, G1 + E1 + 2 * E2 + 8])
        h = sb("h", [P, T, D])
        xn = sb("xn", [P, T, D])
        hT = sb("hT", [P, KD, S])
        gate_rows = sb("gate_rows", [P, 2, 2, D])
        mod = sb("mod", [P, 2, 4, KD])
        mod_ctx = sb("mod_ctx", [P, 2, KD])
        condT = sb("condT", [P, KD, 32])
        zero_col = sb("zero_col", [P, 1])
        minus_half = sb("minus_half", [P, 8])
        small = sb("small", [P, 256])
        flag = sb("flag", [P, 1], I32)
        arena = sb("arena", [P, ARENA])
        arena_at = [0]

        def carve(*shape, at=None):
            n = int(np.prod(shape))
            if at is not None:
                arena_at[0] = at
            a = arena[:, arena_at[0]:arena_at[0] + n]
            arena_at[0] += n
            assert arena_at[0] <= ARENA, arena_at[0]
            if len(shape) == 2:
                return a.rearrange("p (a b) -> p a b", b=shape[1])
            if len(shape) == 3:
                return a.rearrange("p (a b c) -> p a b c", b=shape[1], c=shape[2])
            return a

        def const(name):
            a, n = CONST_AT[name]
            return cb[:, a:a + n]

        def row(name, n=HD):
            return rows[:, ROW_AT[name]:ROW_AT[name] + n]

        def col(name):
            return cols[:, COLS.index(name), :]

        ident = const("ident")

        arrived = [sem(f"arrived{i}") for i in range(SLOTS)]
        item_done = sem("item_done")

        done_at, released, n_done = {}, {}, 0
        for i in range(len(items)):
            if items[i][0] not in ("w_in", "attn_w_in", "w_out", "attn_w_out", "conv_w_out") or i == ITEM["proj2"] + 4:
                n_done += 1
                done_at[i] = n_done
                released[i] = (item_done, n_done)

        def wait_item(pe, i):
            pe.wait_ge(arrived[i % SLOTS], 16 * (i // SLOTS + 1))

        x_loaded, first_loaded, const_loaded, ctx_loaded = (sem(n + "_loaded") for n in ("x", "first", "const", "ctx"))
        dve_chain, act_chain, pool_chain = sem("dve_chain"), sem("act_chain"), sem("pool_chain")
        chain_at = {"dve": 0, "act": 0, "pool": 0}

        def dve_step(ins):
            chain_at["dve"] += 1
            ins.then_inc(dve_chain, 1)
            nc.vector.wait_ge(dve_chain, chain_at["dve"])

        sums_ready, roots_done = sem("sums_ready"), sem("roots_done")
        chain_at["sums"] = chain_at["roots"] = 0

        def sums_added(sums, n):
            chain_at["sums"] += 1
            nc.vector.tensor_scalar(sums, sums, n * EPS, None, ALU.add).then_inc(sums_ready, 1)

        def rooted(ins, sums, n):
            dve_step(ins)
            sums_added(sums, n)
            nc.vector.wait_ge(roots_done, chain_at["sums"])

        def root_pool(dst, src):
            chain_at["roots"] += 1
            nc.gpsimd.wait_ge(sums_ready, chain_at["roots"])
            nc.gpsimd.tensor_tensor(dst, src, minus_half[:, 0:src.shape[1]], ALU.pow).then_inc(roots_done, 1)

        def pool_step(ins):
            chain_at["pool"] += 1
            ins.then_inc(pool_chain, 1)
            nc.gpsimd.wait_ge(pool_chain, chain_at["pool"])

        sq_done, norm_roots, xn_done = ([sem(f"{n}{t}") for t in range(T)] for n in ("sq_done", "norm_roots", "xn_done"))
        tr_done, hT_act, hT_dve = sem("tr_done"), sem("hT_act"), sem("hT_dve")
        ss = small[:, 0:2]
        rs = small[:, 2:4]
        TR = [bank[6], bank[7]]
        AB = [bank[4], bank[5]]
        ZB = [bank[3], bank[4]]

        def norm_act(j, src, i, ready):
            act = nc.scalar
            for s, v in ready:
                act.wait_ge(s, v)
            if i:
                act.wait_ge(tr_done, 4 * i - 2)
            nc.scalar.activation(xn[:, 0, :], src[:, 0, :], ACT.Square, accum_out=ss[:, 0:1]).then_inc(sq_done[0], 1)
            act.wait_ge(norm_roots[0], j + 1)
            nc.scalar.activation(xn[:, 0, :], src[:, 0, :], ACT.Copy, scale=rs[:, 0:1]).then_inc(xn_done[0], 1)

        def norm_dve(j, src, i, ready):
            dve = nc.vector
            for s, v in ready:
                dve.wait_ge(s, v)
            if i:
                dve.wait_ge(tr_done, 4 * i)
            nc.vector.tensor_tensor_reduce(out=xn[:, 1, :], in0=src[:, 1, :], in1=src[:, 1, :], scale=1.0, scalar=0.0,
                                           op0=ALU.mult, op1=ALU.add, accum_out=ss[:, 1:2]).then_inc(sq_done[1], 1)
            dve.wait_ge(norm_roots[1], j + 1)
            nc.vector.tensor_scalar(xn[:, 1, :], src[:, 1, :], rs[:, 1:2], None, ALU.mult).then_inc(xn_done[1], 1)

        def norm_pool(j):
            for t in range(T):
                nc.gpsimd.wait_ge(sq_done[t], j + 1)
                pool_step(nc.gpsimd.tensor_scalar(ss[:, t:t + 1], ss[:, t:t + 1], 1.0 / D, EPS, ALU.mult, ALU.add))
                nc.gpsimd.tensor_tensor(rs[:, t:t + 1], ss[:, t:t + 1], minus_half[:, 0:1], ALU.pow).then_inc(norm_roots[t], 1)

        def xn_ready(j, t):
            return [(xn_done[t], j + 1)]

        def tr_pe(i, t, ready, banks=TR):
            pe = nc.tensor
            for s, v in ready:
                pe.wait_ge(s, v)
            for b in range(2):
                if 2 * i + t:
                    pe.wait_ge((hT_act, hT_dve)[b], 2 * i + t)
                for kk in range(4):
                    last = nc.tensor.transpose(banks[b][:, kk * P:(kk + 1) * P], xn[:, t, 4 * b + kk::KD], ident)
                last.then_inc(tr_done, 1)

        def tr_act(i, t, dst, scale, shift, banks=TR):
            nc.scalar.wait_ge(tr_done, 4 * i + 2 * t + 1)
            for k in range(4):
                bias = zero_col[:, 0:1] if shift is None else shift[:, k:k + 1]
                last = nc.scalar.activation(dst[:, k, t * P:(t + 1) * P], banks[0][:, k * P:(k + 1) * P], ACT.Identity, bias=bias,
                                            scale=scale[:, k:k + 1])
            last.then_inc(hT_act, 1)

        def tr_dve(i, t, dst, scale, shift, banks=TR):
            nc.vector.wait_ge(tr_done, 4 * i + 2 * t + 2)
            for k in range(4, KD):
                bias = zero_col[:, 0:1] if shift is None else shift[:, k:k + 1]
                last = nc.vector.tensor_scalar(dst[:, k, t * P:(t + 1) * P], banks[1][:, (k - 4) * P:(k - 3) * P], scale[:, k:k + 1], bias,
                                               ALU.mult, ALU.add)
            last.then_inc(hT_dve, 1)

        def both_act(i, *args):
            for t in range(T):
                tr_act(i, t, *args)

        def both_dve(i, *args):
            for t in range(T):
                tr_dve(i, t, *args)

        def hT_ready(i, t=T - 1):
            return [(hT_act, 2 * i + t + 1), (hT_dve, 2 * i + t + 1)]

        setup_done, cond_done, gate_loaded = sem("setup_done"), sem("cond_done"), sem("gate_loaded")
        ada_rows, ada_sums, ada_used = sem("ada_rows"), sem("ada_sums"), sem("ada_used")
        def ada_R(s):
            return (hT[:, 4:8, :] if s % 6 < EARLY else gate_s).rearrange("p a b -> p (a b)")


        def ada_mm_pe(s, halves=(0, 1)):
            pe = nc.tensor
            if s == 0:
                pe.wait_ge(cond_done, 2)
                pe.wait_ge(fg_z, 1)
            elif s == 6:
                pe.wait_ge(fy_c, 1)
            else:
                pe.wait_ge(ada_used, s)
            for n in halves:
                i = ITEM["ada", s] + n
                wait_item(pe, i)
                for kk in range(KD):
                    j = kk % 4
                    last = nc.tensor.matmul(AB[n][32 * j:32 * j + 32, :], condT[:, kk, :], ring[i % SLOTS][:, kk, :],
                                            start=(kk < 4), stop=(kk >= 4))
                last.then_inc(item_done, 1)

        def ada_rows_act(s):
            if s:
                nc.scalar.wait_ge(ada_sums, s)
            for n in range(2):
                nc.scalar.wait_ge(item_done, done_at[ITEM["ada", s] + n])
                nc.scalar.activation(ada_R(s)[:, n * NC:(n + 1) * NC], AB[n][:, :], ACT.Copy).then_inc(ada_rows, 1)

        def ada_sum_pe(s):
            pe = nc.tensor
            pe.wait_ge(ada_rows, 2 * (s + 1))
            if s % 6 in (G_M, G_F):
                for n in range(2):
                    last = nc.tensor.matmul(AB[n][:, :], const("row0"), ada_R(s)[:, n * NC:(n + 1) * NC], start=True, stop=True)
            else:
                for k in range(KD):
                    last = nc.tensor.matmul(AB[0][:, 2 * k:2 * k + 2], ada_R(s)[:, k::KD], const("rows"), start=True, stop=True)
            last.then_inc(ada_sums, 1)

        def ada_use_dve(s):
            dve = nc.vector
            l, sec = divmod(s, 6)
            dve.wait_ge(ada_sums, s + 1)
            if sec in (G_M, G_F):
                g = gate_rows[:, l, sec // 3, :]
                if sec == G_M:
                    dve.wait_ge(gate_loaded, 32 * (l + 1))
                nc.vector.tensor_tensor(g[:, 0:NC], g[:, 0:NC], AB[0][:, :], ALU.add)
                nc.vector.tensor_tensor(g[:, NC:D], g[:, NC:D], AB[1][:, :], ALU.add).then_inc(ada_used, 1)
                return
            sums = AB[0][:, 0:2 * KD].rearrange("p (k c) -> p c k", c=2)
            m = (0 if sec < 3 else 2) + sec % 3
            both = [(mod[:, l, m, :], 0)] + ([(mod_ctx[:, m, :], 1)] if s < 2 else [])
            for n, (dst, c) in enumerate(both):
                ins = nc.vector.tensor_tensor(dst, sums[:, c, :], col(f"b{l}{sec}"), ALU.add)
                if sec % 3 == 1:
                    dve_step(ins)
                    gain = col(f"norm_mix{l}" if sec < 3 else f"norm_ffn{l}")
                    ins = nc.vector.scalar_tensor_tensor(dst, dst, 1.0, gain, ALU.add, ALU.mult)
            ins.then_inc(ada_used, 1)

        def heads(name, units, sq, qn, tmp, first_ready):
            pj, sqs, qns, qgs = sem(name + "_projected"), sem(name + "_squared"), sem(name + "_scaled"), sem(name + "_gained")
            rot, trs, put_, vput = sem(name + "_rotated"), sem(name + "_transposed"), sem(name + "_put"), sem(name + "_vput")
            qk = [u for u in range(len(units)) if units[u]["kind"] == "qk"]
            vs = [u for u in range(len(units)) if units[u]["kind"] == "v"]
            nq = {u: n for n, u in enumerate(qk)}
            nv = {u: n for n, u in enumerate(vs)}
            nrot = {u: sum(1 for w in qk[:nq[u] + 1] if units[w]["rope"]) for u in qk}
            NB = 4
            for u, un in enumerate(units):
                if un["item"] not in done_at:
                    released[un["item"]] = (pj, u + 1)

            def free(eng, u):
                w = u - NB
                if w >= 0:
                    if units[w]["kind"] == "qk":
                        eng.wait_ge(qns, nq[w] + 1)
                    else:
                        eng.wait_ge(vput, nv[w] + 1)

            def proj_pe(u):
                pe, un = nc.tensor, units[u]
                if u == 0:
                    for s, v in first_ready:
                        pe.wait_ge(s, v)
                for s, v in un.get("ready", []):
                    pe.wait_ge(s, v)
                wait_item(pe, un["item"])
                free(pe, u)
                a, n = un["cols"]
                for k in range(KD):
                    last = nc.tensor.matmul(bank[u % NB][:, 0:n], un["lhs"][:, k, :], ring[un["item"] % SLOTS][:, k, a:a + n],
                                            start=(k == 0), stop=(k == KD - 1))
                last.then_inc(pj, 1)

            def post_act(u):
                act, un = nc.scalar, units[u]
                act.wait_ge(pj, u + 1)
                if un["kind"] == "v":
                    for n, (c, dst) in enumerate(un["put"]):
                        ins = nc.scalar.activation(dst, bank[u % NB][:, c[0]:c[1]], ACT.Copy)
                    ins.then_inc(vput, 1)
                    return
                q = nq[u]
                if q >= 2:
                    act.wait_ge(qgs, q - 1)
                    if units[qk[q - 2]]["rope"]:
                        act.wait_ge(rot, nrot[qk[q - 2]])
                    else:
                        act.wait_ge(trs, q - 1)
                n = un["cols"][1]
                nc.scalar.activation(sq[:, q % 2, 0:n], bank[u % NB][:, 0:n], ACT.Square).then_inc(sqs, 1)

            def post_dve(u):
                dve, un = nc.vector, units[u]
                if un["kind"] == "v":
                    return
                q, n = nq[u], un["cols"][1]
                nh = n // HD
                s8, r8 = small[:, 16:16 + nh], small[:, 24:24 + nh]
                view = lambda a: a.rearrange("p (h d) -> p h d", d=HD)
                dve.wait_ge(sqs, q + 1)
                rooted(nc.vector.tensor_reduce(s8, view(sq[:, q % 2, 0:n]), AX.X, ALU.add), s8, HD)
                if q >= 2:
                    dve.wait_ge(trs, q - 1)
                ins = nc.vector.tensor_tensor(view(qn[:, q % 2, 0:n]), view(bank[u % NB][:, 0:n]),
                                              r8.unsqueeze(2).broadcast_to([P, nh, HD]), ALU.mult)
                ins.then_inc(qns, 1)
                dve.wait_ge(qns, q + 1)
                at = 0
                for m, gain in un["gains"]:
                    sl = slice(at * HD, (at + m) * HD)
                    ins = nc.vector.tensor_tensor(view(sq[:, q % 2, sl]), view(qn[:, q % 2, sl]),
                                                  gain.unsqueeze(1).broadcast_to([P, m, HD]), ALU.mult)
                    at += m
                if not un["rope"]:
                    ins.then_inc(qgs, 1)
                    return
                dve_step(ins)
                nc.vector.tensor_tensor(view(qn[:, q % 2, 0:n]), view(sq[:, q % 2, 0:n]),
                                        un["rope"][0].unsqueeze(1).broadcast_to([P, nh, HD]), ALU.mult).then_inc(qgs, 1)

            def rope_pool(u):
                un = units[u]
                if un["kind"] == "v":
                    return
                nh = un["cols"][1] // HD
                root_pool(small[:, 24:24 + nh], small[:, 16:16 + nh])
                if not un["rope"]:
                    return
                pool, q = nc.gpsimd, nq[u]
                _, sin, half = un["rope"]
                n = un["cols"][1]
                nh, np_ = n // HD, HD // (2 * half)
                src, dst = sq[:, q % 2, 0:n], qn[:, q % 2, 0:n]
                pool.wait_ge(qgs, q + 1)
                view = lambda a: a.rearrange("p (h d) -> p h d", d=HD)
                for j in range(np_):
                    for a in range(2):
                        lo, so = (2 * j + a) * half, (2 * j + 1 - a) * half
                        ins = nc.gpsimd.tensor_tensor(view(tmp[:, 0:n])[:, :, lo:lo + half], view(src)[:, :, so:so + half],
                                                      sin[:, lo:lo + half].unsqueeze(1).broadcast_to([P, nh, half]), ALU.mult)
                pool_step(ins)
                nc.gpsimd.tensor_tensor(dst, dst, tmp[:, 0:n], ALU.add).then_inc(rot, 1)
                pool.wait_ge(rot, nrot[u])

            def tr_heads_pe(u):
                pe, un = nc.tensor, units[u]
                if un["kind"] == "v":
                    return
                q = nq[u]
                if un["rope"]:
                    pe.wait_ge(rot, nrot[u])
                    src = qn[:, q % 2, :]
                else:
                    pe.wait_ge(qgs, q + 1)
                    src = sq[:, q % 2, :]
                if q >= 2:
                    pe.wait_ge(put_, q - 1)
                for m in range(un["cols"][1] // P):
                    last = nc.tensor.transpose(TR[q % 2][:, m * P:(m + 1) * P], src[:, m * P:(m + 1) * P], ident)
                last.then_inc(trs, 1)

            def put_act(u):
                un = units[u]
                if un["kind"] == "v":
                    return
                q = nq[u]
                nc.scalar.wait_ge(trs, q + 1)
                for a, m, dst in un["put"]:
                    ins = nc.scalar.activation(dst, TR[q % 2][:, a * P:(a + m) * P].rearrange("p (m q) -> p m q", q=P), ACT.Copy)
                ins.then_inc(put_, 1)

            return dict(proj_pe=proj_pe, post_act=post_act, post_dve=post_dve, rope_pool=rope_pool, tr_pe=tr_heads_pe,
                        put_act=put_act, done=[(put_, len(qk)), (vput, len(vs))])

        out_mm, out_added = sem("out_mm"), sem("out_added")
        out_scaled = arena[:, ARENA - NC:ARENA]
        for o in range(3):
            for n in range(2):
                released[ITEM["out", o] + n] = (out_mm, 4 * o + 2 + n + 1)

        def out_pe(o, t, lhs, ready, halves=(0, 1)):
            pe = nc.tensor
            for s, v in ready:
                pe.wait_ge(s, v)
            for n in halves:
                i = ITEM["out", o] + n
                wait_item(pe, i)
                for k in range(KD):
                    last = nc.tensor.matmul(bank[2 * t + n][:, :], lhs[:, k, t * P:(t + 1) * P], ring[i % SLOTS][:, k, :],
                                            start=(k == 0), stop=(k == KD - 1))
                last.then_inc(out_mm, 1)

        def out_dve(o, gate, before_last):
            dve = nc.vector
            for t in range(T):
                for n in range(2):
                    if t and n:
                        before_last()
                    dve.wait_ge(out_mm, 4 * o + 2 * t + n + 1)
                    sl = slice(n * NC, (n + 1) * NC)
                    src = bank[2 * t + n][:, :]
                    if gate is not None:
                        dve_step(nc.vector.tensor_tensor(out_scaled[:, :], src, gate[:, sl], ALU.mult))
                        src = out_scaled[:, :]
                    ins = nc.vector.tensor_tensor(h[:, t, sl], h[:, t, sl], src, ALU.add)
                    ins.then_inc(out_added, 1)
                    dve.wait_ge(out_added, 4 * o + 2 * t + n + 1)

        def out_ready(o, t):
            return [(out_added, 4 * o + 2 * t + 2)]

        arena_at[0] = 0
        sq_junk = carve(NC)
        qT = [carve(4, S) for _ in range(2)]
        kT = [carve(4, S) for _ in range(2)]
        vv = [carve(T, NC) for _ in range(2)]
        bias1 = carve(8, S)
        bias0 = hT[:, 0:4, :].rearrange("p a b -> p (a b)").rearrange("p (h k) -> p h k", k=P)
        temps_at = arena_at[0]
        sq1, qn1, tmp1 = carve(2, NC), carve(2, NC), carve(NC)
        fz, fa, fn = (xn[:, 0, n * S:(n + 1) * S] for n in range(3))
        sp, pr, pt = (a for a in (carve(2, S, at=temps_at), carve(2, S), carve(2, S)))

        rope1 = (const("cos1"), const("sin1"), HD // 2)
        rope2 = (const("cos2"), const("sin2"), HD // 4)

        def rope_of(rope, t):
            return (rope[0][:, t * HD:(t + 1) * HD], rope[1][:, t * HD:(t + 1) * HD], rope[2])

        units1 = []
        for c, name in enumerate(CHUNKS1):
            for t in range(T):
                un = dict(item=ITEM["proj1", c], lhs=hT[:, :, t * P:(t + 1) * P], cols=(0, NC))
                br = 0 if name[1] == "a" else 1
                if name[0] == "v":
                    un.update(kind="v", put=[((0, NC), vv[br][:, t, :])])
                else:
                    dst = (qT if name[0] == "q" else kT)[br]
                    un.update(kind="qk", gains=[(8, row(name[0] + ("_fox" if br == 0 else "_dil")))],
                              rope=rope_of(rope1, t) if br else None, put=[(0, 4, dst[:, :, t * P:(t + 1) * P])])
                units1.append(un)
        units1[1]["ready"] = hT_ready(0)
        h1 = heads("h1", units1, sq1, qn1, tmp1, hT_ready(0, 0))

        fg_mm, fg_z, fg_ln, fg_c = sem("fg_mm"), sem("fg_z"), sem("fg_ln"), sem("fg_c")
        FG = bank[5][0:8, 0:S]

        def forget_pe():
            nc.tensor.wait_ge(const_loaded, 48)
            for s_, v in hT_ready(0):
                nc.tensor.wait_ge(s_, v)
            for k in range(KD):
                last = nc.tensor.matmul(FG, router_sb[:, k, 68:76], hT[:, k, :], start=(k == 0), stop=(k == KD - 1))
            last.then_inc(fg_mm, 1)

        def forget_dve():
            nc.vector.wait_ge(fg_mm, 1)
            dve_step(nc.vector.tensor_scalar(fz[0:8, :], FG, cols[0:8, COLS.index("b_forget"), 0:1], None, ALU.add))
            nc.vector.scalar_tensor_tensor(fa[0:8, :], fz[0:8, :], -1.0, fz[0:8, :], ALU.mult, ALU.max).then_inc(fg_z, 1)

        def forget_act():
            nc.scalar.wait_ge(fg_z, 1)
            nc.scalar.activation(fa[0:8, :], fa[0:8, :], ACT.Exp, scale=-1.0).then_inc(act_chain, 1)
            nc.scalar.wait_ge(act_chain, 1)
            nc.scalar.activation(fa[0:8, :], fa[0:8, :], ACT.Ln, bias=const("ones")[0:8, 0:1]).then_inc(fg_ln, 1)

        def forget_sum_dve():
            nc.vector.wait_ge(fg_ln, 1)
            dve_step(nc.vector.scalar_tensor_tensor(fz[0:8, :], fz[0:8, :], 0.0, fa[0:8, :], ALU.min, ALU.subtract))
            dve_step(nc.vector.tensor_scalar(fz[0:8, :], fz[0:8, :], -1.0, None, ALU.mult))
            nc.vector.memset(fa[0:8, :], 1.0).then_inc(dve_chain, 1)
            chain_at["dve"] += 1
            nc.vector.wait_ge(dve_chain, chain_at["dve"])
            nc.vector.tensor_tensor_scan(fn[0:8, :], fa[0:8, :], fz[0:8, :], 0.0, ALU.mult, ALU.add).then_inc(fg_c, 1)

        cb_mm, cb_done = sem("cb_mm"), sem("cb_done")

        def bias_pe():
            pe = nc.tensor
            pe.wait_ge(fg_c, 1)
            for s_, v in h1["done"]:
                pe.wait_ge(s_, v)
            for n in range(4):
                for j in range(2):
                    last = nc.tensor.matmul(bank[n][:, j * S:(j + 1) * S], ident[0:8, 2 * n + j:2 * n + j + 1].broadcast_to([8, P]),
                                            fn[0:8, 0:S], start=True, stop=True)
                last.then_inc(cb_mm, 1)

        def bias_dve():
            for n in range(4):
                nc.vector.wait_ge(cb_mm, n + 1)
                for t in range(T):
                    w = P * (t + 1)
                    nc.vector.tensor_tensor((bias1 if t else bias0)[:, 2 * n:2 * n + 2, :],
                                            bank[n][:, :].rearrange("p (h k) -> p h k", k=S)[:, :, 0:w],
                                            const(f"causal{t}").unsqueeze(1).broadcast_to([P, 2, w]), ALU.add).then_inc(cb_done, 1)

        at_s, at_m, at_e, at_t, at_c, at_v = (sem("at_" + n) for n in ("scores", "max", "exp", "turned", "copied", "values"))
        at_o, at_q, at_n = sem("at_out"), sem("at_outsq"), sem("at_normed")
        att1 = [(t, br, hd) for t in range(T) for br in (1, 0) for hd in range(8)]
        negm, lsum = small[:, 32:64], small[:, 64:96]

        def scores_pe(u):
            pe = nc.tensor
            t, br, hd = att1[u]
            if u >= 2:
                pe.wait_ge(at_m, u - 1)
            if u == 0:
                pe.wait_ge(cb_done, 4 * T)
            a = HD * (hd % 2)
            w = P * (t + 1)
            nc.tensor.matmul(bank[u % 2][:, 0:w], qT[br][a:a + HD, hd // 2, t * P:(t + 1) * P],
                             kT[br][a:a + HD, hd // 2, 0:w], start=True, stop=True).then_inc(at_s, 1)

        def max_dve(u):
            dve = nc.vector
            t, br, hd = att1[u]
            w = P * (t + 1)
            dve.wait_ge(at_s, u + 1)
            if u >= 2:
                dve.wait_ge(at_e, u - 1)
            bias = const(f"dilated{t}") if br else (bias1 if t else bias0)[:, hd, :]
            nc.vector.tensor_tensor_reduce(out=sp[:, u % 2, 0:w], in0=bank[u % 2][:, 0:w], in1=bias, scale=-1.0, scalar=3e38,
                                           op0=ALU.add, op1=ALU.min, accum_out=negm[:, u:u + 1]).then_inc(at_m, 1)

        def exp_act(u):
            act = nc.scalar
            w = P * (att1[u][0] + 1)
            act.wait_ge(at_m, u + 1)
            if u >= 2:
                act.wait_ge(at_t, u - 1)
            nc.scalar.activation(pr[:, u % 2, 0:w], sp[:, u % 2, 0:w], ACT.Exp, bias=negm[:, u:u + 1], scale=-1.0,
                                 accum_out=lsum[:, u:u + 1]).then_inc(at_e, 1)

        def turn_pe(u):
            pe = nc.tensor
            pe.wait_ge(at_e, u + 1)
            if u >= 2:
                pe.wait_ge(at_c, u - 1)
            for b in range(att1[u][0] + 1):
                last = nc.tensor.transpose(bank[2 + u % 2][:, b * P:(b + 1) * P], pr[:, u % 2, b * P:(b + 1) * P], ident)
            last.then_inc(at_t, 1)

        def copy_dve(u):
            dve = nc.vector
            w = P * (att1[u][0] + 1)
            dve.wait_ge(at_t, u + 1)
            if u >= 2:
                dve.wait_ge(at_v, u - 1)
            nc.vector.tensor_copy(pt[:, u % 2, 0:w], bank[2 + u % 2][:, 0:w]).then_inc(at_c, 1)

        def values_pe(u):
            pe = nc.tensor
            t, br, hd = att1[u]
            pe.wait_ge(at_c, u + 1)
            if t and hd == 0:
                pe.wait_ge(at_o, u // 8 - 1)
            for b in range(t + 1):
                last = nc.tensor.matmul(bank[6 + br][:, hd * HD:(hd + 1) * HD], pt[:, u % 2, b * P:(b + 1) * P],
                                        vv[br][:, b, hd * HD:(hd + 1) * HD], start=(b == 0), stop=(b == t))
            last.then_inc(at_v, 1)

        def out1_dve(g):
            dve = nc.vector
            t, br, _ = att1[8 * g]
            rl = small[:, 96:104]
            dve.wait_ge(at_v, 8 * (g + 1))
            dve.wait_ge(at_e, 8 * (g + 1))
            dve_step(nc.vector.reciprocal(rl, lsum[:, 8 * g:8 * g + 8]))
            nc.vector.tensor_tensor(xn[:, t, br * NC:(br + 1) * NC].rearrange("p (h d) -> p h d", d=HD),
                                    bank[6 + br][:, :].rearrange("p (h d) -> p h d", d=HD),
                                    rl.unsqueeze(2).broadcast_to([P, 8, HD]), ALU.mult).then_inc(at_o, 1)

        def out1_act(g):
            t, br, _ = att1[8 * g]
            nc.scalar.wait_ge(at_o, g + 1)
            if g:
                nc.scalar.wait_ge(at_q, g)
            nc.scalar.activation(sq_junk[:, :], xn[:, t, br * NC:(br + 1) * NC], ACT.Square,
                                 accum_out=small[:, 104 + g:105 + g]).then_inc(at_q, 1)

        def out1_norm_dve(g):
            dve = nc.vector
            t, br, _ = att1[8 * g]
            sl = xn[:, t, br * NC:(br + 1) * NC]
            sums, r = small[:, 104 + g:105 + g], small[:, 108 + g:109 + g]
            dve.wait_ge(at_q, g + 1)
            rooted(nc.vector.tensor_scalar(sums, sums, 0.0, None, ALU.add), sums, NC)
            nc.vector.tensor_scalar(sl, sl, r, float(NC) ** 0.5, ALU.mult, ALU.mult).then_inc(at_n, 1)

        def out1_pool(g):
            root_pool(small[:, 108 + g:109 + g], small[:, 104 + g:105 + g])

        LAST1 = len(att1) - 1

        def steps1():
            for u in range(len(units1)):
                yield "proj", u
                if u >= 2:
                    yield "tr", u - 2
            for u in (len(units1) - 2, len(units1) - 1):
                yield "tr", u
            yield "bias", 0
            s = 0
            for u in range(LAST1 + 4):
                if u <= LAST1:
                    yield "scores", u
                if 2 <= u <= LAST1 + 2:
                    yield "turn", u - 2
                if u == LAST1 + 1:
                    yield "first", 0
                if u >= 3:
                    yield "values", u - 3
                    if (u - 3) % 8 == 7:
                        yield "out", (u - 3) // 8
                if u % 8 == 2 and s < EARLY:
                    yield "ada_mm", s
                if u % 8 == 5 and s < EARLY:
                    yield "ada_sum", s
                    s += 1

        def block1_pe():
            pe = nc.tensor
            pe.wait_ge(first_loaded, 32)
            tr_pe(0, 0, xn_ready(0, 0))
            for what, i in steps1():
                if what == "proj":
                    if i == 1:
                        tr_pe(0, 1, xn_ready(0, 1))
                        forget_pe()
                    h1["proj_pe"](i)
                elif what == "first":
                    tr_pe(1, 0, [(at_n, 2), (ada_used, EARLY)], AB)
                elif what == "ada_mm":
                    ada_mm_pe(i)
                elif what == "ada_sum":
                    ada_sum_pe(i)
                elif what == "tr":
                    h1["tr_pe"](i)
                elif what == "bias":
                    bias_pe()
                elif what == "scores":
                    scores_pe(i)
                elif what == "turn":
                    turn_pe(i)
                elif what == "values":
                    values_pe(i)
            out_pe(0, 0, hT, hT_ready(1, 0), (0,))
            tr_pe(1, 1, [(at_n, 4)], AB)
            out_pe(0, 0, hT, [], (1,))
            last_out_pe(0, hT, hT_ready(1), 1, 2)

        def load_gates_act(l):
            for n, sec in enumerate((G_M, G_F)):
                nc.scalar.dma_start(gate_rows[:, l, n, :], ada_b[l:l + 1, sec * D:(sec + 1) * D].broadcast_to([P, D])).then_inc(gate_loaded, 16)

        def block1_act():
            act = nc.scalar
            norm_act(0, h, 0, [(x_loaded, 16)])
            act.wait_ge(first_loaded, 32)
            both_act(0, hT, col("norm_mix"), None)
            for c, name in enumerate(("c", "c_ctx")):
                nc.scalar.activation(condT[:, :, c], col(name), ACT.Silu).then_inc(cond_done, 1)
            act.wait_ge(const_loaded, 48)
            forget_act()
            for what, i in steps1():
                if what == "proj":
                    h1["post_act"](i)
                elif what == "ada_mm":
                    ada_rows_act(i)
                elif what == "tr":
                    h1["put_act"](i)
                elif what == "bias":
                    load_gates_act(0)
                    act.dma_start(ctx_rows, ctx_in[0].rearrange("(t p) d -> p t d", p=P)).then_inc(ctx_loaded, 16)
                elif what == "scores":
                    exp_act(i)
                elif what == "out":
                    out1_act(i)
                elif what == "first":
                    tr_act(1, 0, hT, col("out_norm"), None, AB)
            tr_act(1, 1, hT, col("out_norm"), None, AB)

        def block1_dve():
            norm_dve(0, h, 0, [(x_loaded, 16)])
            nc.vector.wait_ge(first_loaded, 32)
            both_dve(0, hT, col("norm_mix"), None)
            nc.vector.wait_ge(const_loaded, 48)
            for name in ("k_fox", "k_dil", "k_att"):
                dve_step(nc.vector.tensor_scalar(row(name), row(name), float(HD) ** 0.5, None, ALU.mult))
            forget_dve()
            for what, i in steps1():
                if what == "proj":
                    h1["post_dve"](i)
                    if i == 1:
                        forget_sum_dve()
                elif what == "ada_sum":
                    ada_use_dve(i)
                elif what == "bias":
                    bias_dve()
                elif what == "scores":
                    max_dve(i)
                elif what == "turn":
                    copy_dve(i)
                elif what == "out":
                    out1_dve(i)
                    out1_norm_dve(i)
                elif what == "first":
                    tr_dve(1, 0, hT, col("out_norm"), None, AB)
            tr_dve(1, 1, hT, col("out_norm"), None, AB)
            out_dve(0, None, lambda: tr_dve(2, 0, hT, col("norm_ffn"), None))

        def block1_pool():
            norm_pool(0)
            for u in range(len(units1)):
                h1["rope_pool"](u)
            for g in range(4):
                out1_pool(g)

        arena_at[0] = 0
        xgT = carve(KD, EP * C)
        sel = carve(T, EP * C)
        wsel = carve(T, EP * C)
        xs, ws = carve(2 * KD, C), carve(2 * T, 4 * C)
        gate_s, up_s = carve(2, NC), carve(2, NC)
        silu_s = carve(2, 4 * C)
        act_s = carve(2 * KD, C)
        z_s = carve(D)
        wselT = carve(2, S)
        rankm, comb = carve(T, E1), carve(T, E1)
        r_temps = [carve(T, E1) for _ in range(6)]
        logits = carve(T, G1 + E1)

        lg_mm, rt_act, rt_dve, rk_mm = sem("logits_mm"), sem("route_act"), sem("route_dve"), sem("rank_mm")
        flag_done = sem("flag_done")
        route_n = {"act": 0, "dve": 0, "pe": 0}

        def last_out_pe(o, lhs, ready, j, i):
            out_pe(o, 1, lhs, ready, (0,))
            tr_pe(i, 0, xn_ready(j, 0))
            out_pe(o, 1, lhs, [], (1,))

        def logits_pe(j, i, c0, n, section=None):
            pe = nc.tensor
            for t in range(T):
                if t:
                    if section is not None:
                        ada_mm_pe(section, (0,))
                    tr_pe(i, t, xn_ready(j, t))
                    if section is not None:
                        ada_mm_pe(section, (1,))
                for s_, v in hT_ready(i, t):
                    pe.wait_ge(s_, v)
                for k in range(KD):
                    last = nc.tensor.matmul(bank[0][:, t * n:(t + 1) * n], hT[:, k, t * P:(t + 1) * P], router_sb[:, k, c0:c0 + n],
                                            start=(k == 0), stop=(k == KD - 1))
            last.then_inc(lg_mm, 1)

        def bc(a, *shape):
            return a.broadcast_to([P, *shape])

        def first_max_dve(z, iota, n, best, eq, idx):
            v = nc.vector
            dve_step(v.tensor_reduce(best, z, AX.X, ALU.max))
            dve_step(v.tensor_tensor(eq, z, bc(best.unsqueeze(2), T, n), ALU.is_equal))
            dve_step(v.scalar_tensor_tensor(eq, eq, -64.0, bc(iota.unsqueeze(1), T, n), ALU.mult, ALU.add))
            dve_step(v.tensor_reduce(idx, eq, AX.X, ALU.min))
            dve_step(v.tensor_tensor(eq, eq, bc(idx.unsqueeze(2), T, n), ALU.is_equal))

        one_g, one_a, one_b = r_temps[0][:, :, 0:G1], r_temps[1], r_temps[2]
        zsel, zg = r_temps[3], r_temps[4][:, :, 0:G1]
        gmax, gidx, gsum, best1, best2, eidx, ediff, gtop = (small[:, 120 + 2 * n:122 + 2 * n] for n in range(8))
        gpen = r_temps[4][:, :, 8:8 + G1]

        def route1_dve(section):
            v = nc.vector
            v.wait_ge(lg_mm, 1)
            dve_step(v.tensor_tensor(logits[:, :, :], bank[0][:, 0:T * (G1 + E1)].rearrange("p (t e) -> p t e", t=T),
                                     bc(row("b_router", G1 + E1).unsqueeze(1), T, G1 + E1), ALU.add))
            iota = const("iota")
            first_max_dve(logits[:, :, 0:G1], iota[:, 0:G1], G1, gmax, one_g, gidx)
            v.tensor_tensor(zg, logits[:, :, 0:G1], bc(gmax.unsqueeze(2), T, G1), ALU.subtract).then_inc(rt_dve, 1)
            dve_step(v.tensor_scalar(gpen, one_g, -NEG, NEG, ALU.mult, ALU.add))
            dve_step(v.tensor_tensor(zsel[:, :, :].rearrange("p t (g e) -> p t g e", g=G1),
                                     logits[:, :, G1:].rearrange("p t (g e) -> p t g e", g=G1),
                                     gpen.unsqueeze(3).broadcast_to([P, T, G1, E1 // G1]), ALU.add))
            first_max_dve(zsel[:, :, :], iota, E1, best1, one_a[:, :, :], eidx)
            ada_use_dve(section)
            dve_step(v.scalar_tensor_tensor(zsel[:, :, :], one_a[:, :, :], 2 * NEG, zsel[:, :, :], ALU.mult, ALU.add))
            first_max_dve(zsel[:, :, :], iota, E1, best2, one_b[:, :, :], eidx)
            v.tensor_tensor(ediff, best2, best1, ALU.subtract).then_inc(rt_dve, 1)
            v.wait_ge(rt_act, 2)
            dve_step(v.tensor_reduce(gsum, zg, AX.X, ALU.add))
            dve_step(v.scalar_tensor_tensor(gsum, ediff, 1.0, gsum, ALU.add, ALU.mult))
            dve_step(v.reciprocal(gtop, gsum))
            dve_step(v.tensor_tensor(ediff, ediff, gtop, ALU.mult))
            dve_step(v.tensor_tensor(comb[:, :, :], one_a[:, :, :], bc(gtop.unsqueeze(2), T, E1), ALU.mult))
            dve_step(v.tensor_tensor(zsel[:, :, :], one_b[:, :, :], bc(ediff.unsqueeze(2), T, E1), ALU.mult))
            dve_step(v.tensor_tensor(comb[:, :, :], comb[:, :, :], zsel[:, :, :], ALU.add))
            v.tensor_tensor(one_a[:, :, :], one_a[:, :, :], one_b[:, :, :], ALU.add).then_inc(rt_dve, 1)
            v.wait_ge(rt_dve, 3)
            v.wait_ge(rk_mm, 1)
            dve_step(v.tensor_tensor(zsel[:, :, :], bank[1][:, 0:T * E1].rearrange("p (t e) -> p t e", t=T), one_a[:, :, :], ALU.mult))
            dve_step(v.scalar_tensor_tensor(rankm[:, :, :], zsel[:, :, :], -1.0, one_a[:, :, :], ALU.add, ALU.add))
            dve_step(v.tensor_reduce(small[:, 140:141], bank[1][:, T * E1:(T + 1) * E1], AX.X, ALU.max))
            dve_step(v.tensor_scalar(small[:, 144:144 + PC], iota[:, 1:1 + PC], float(C), small[:, 140:141], ALU.mult, ALU.is_lt))
            dve_step(v.tensor_reduce(small[:, 141:142], small[:, 144:144 + PC], AX.X, ALU.add))
            v.tensor_copy(flag[:, :], small[:, 141:142]).then_inc(flag_done, 1)

        def route1_act(section):
            nc.scalar.wait_ge(rt_dve, 1)
            nc.scalar.activation(zg, zg, ACT.Exp).then_inc(rt_act, 1)
            nc.scalar.wait_ge(rt_dve, 2)
            nc.scalar.activation(ediff, ediff, ACT.Exp).then_inc(rt_act, 1)
            ada_rows_act(section + 1)

        def rank_pe(section):
            ada_sum_pe(section)
            ada_mm_pe(section + 1)
            nc.tensor.wait_ge(rt_dve, 3)
            R = bank[1]
            nc.tensor.matmul(R[:, 0:E1], const("before"), one_a[:, 0, :], start=True, stop=True)
            nc.tensor.matmul(R[:, E1:2 * E1], const("ones"), one_a[:, 0, :], start=True, stop=False)
            nc.tensor.matmul(R[:, E1:2 * E1], const("before"), one_a[:, 1, :], start=False, stop=True)
            nc.tensor.matmul(R[:, 2 * E1:3 * E1], const("ones"), one_a[:, 0, :], start=True, stop=False)
            nc.tensor.matmul(R[:, 2 * E1:3 * E1], const("ones"), one_a[:, 1, :], start=False, stop=True).then_inc(rk_mm, 1)
            ada_sum_pe(section + 1)

        CAP = 2 * S // E2
        aff = r_temps[0][:, :, 0:E2]
        affT, workT, maskT, slotT = (sel[0:E2, t, n * S:(n + 1) * S] for t in range(2) for n in range(2))
        best8 = wsel[0:E2, 0, 0:8]
        onesT = wsel[0:E2, 1, 0:S]
        af_dve, af_act, af_tr, af_slot, af_back = sem("aff_dve"), sem("aff_act"), sem("aff_tr"), sem("aff_slot"), sem("aff_back")

        def route2_dve(l, section=None):
            v = nc.vector
            v.wait_ge(lg_mm, 2 + l)
            z = bank[0][:, 0:T * E2].rearrange("p (t e) -> p t e", t=T)
            dve_step(v.tensor_reduce(gmax, z, AX.X, ALU.max))
            v.tensor_tensor(aff, z, bc(gmax.unsqueeze(2), T, E2), ALU.subtract).then_inc(af_dve, 1)
            v.wait_ge(af_act, l + 1)
            dve_step(v.tensor_reduce(gsum, aff, AX.X, ALU.add))
            dve_step(v.reciprocal(gtop, gsum))
            v.tensor_tensor(comb[:, :, 0:E2], aff, bc(gtop.unsqueeze(2), T, E2), ALU.mult).then_inc(af_dve, 1)
            v.wait_ge(af_tr, l + 1)
            dve_step(v.tensor_copy(workT, bank[1][0:E2, 0:S]))
            for n in range(CAP // 8):
                dve_step(v.max(best8, workT))
                dve_step(v.match_replace(workT, best8, workT, -1.0))
                if n == 1 and section is not None:
                    ada_use_dve(section)
            dve_step(v.memset(onesT, 1.0))
            dve_step(v.tensor_scalar(maskT, workT, 0.0, None, ALU.is_lt))
            dve_step(v.tensor_tensor_scan(slotT, onesT, maskT, 0.0, ALU.mult, ALU.add))
            dve_step(v.tensor_tensor(slotT, slotT, maskT, ALU.mult))
            v.tensor_scalar(slotT, slotT, -1.0, None, ALU.add).then_inc(af_slot, 1)
            v.wait_ge(af_back, l + 1)
            dve_step(v.tensor_copy(rankm[:, :, 0:E2], bank[2][:, 0:T * E2].rearrange("p (t e) -> p t e", t=T)))

        def route2_act(l, section=None):
            nc.scalar.wait_ge(af_dve, 2 * l + 1)
            nc.scalar.activation(aff, aff, ACT.Exp).then_inc(af_act, 1)
            if section is not None:
                ada_rows_act(section + 1)

        def route2_pe(l, section=None):
            pe = nc.tensor
            pe.wait_ge(af_dve, 2 * l + 2)
            for t in range(T):
                last = nc.tensor.transpose(bank[1][0:E2, t * P:(t + 1) * P], comb[:, t, 0:E2], ident)
            last.then_inc(af_tr, 1)
            if section is not None:
                ada_sum_pe(section)
                ada_mm_pe(section + 1)
            pe.wait_ge(af_slot, l + 1)
            for t in range(T):
                last = nc.tensor.transpose(bank[2][:, t * E2:(t + 1) * E2], slotT[:, t * P:(t + 1) * P], ident[0:E2, 0:E2])
            last.then_inc(af_back, 1)
            if section is not None:
                ada_sum_pe(section + 1)

        STEPS = ("sel", "wsel", "gathered", "xg_act", "xg_dve", "xs", "ws", "g_copied", "u_copied", "turned", "silu",
                 "act", "z0", "z1", "w_turned", "wT", "y", "y_added")
        kind1, kind2 = ([sem(f"{kind}_{n}") for n in STEPS] for kind in ("m1", "m2"))

        def place_up(M, e, hf, up):
            return (2 * M.nf + (e - 1) * M.per if e else 0) + 2 * hf + up

        def place_down(M, e, n):
            return 2 * M.nf + e * M.per + (2 * M.nf if e < EP - 1 else 0) + n

        def nth(value, per_expert, r, k):
            return (r * (2 * per_expert)) + ((k * (EP * per_expert)) + value)

        def wait_moe_item(pe, M, i, r, k):
            pe.wait_ge(M.arrived[(M.first + i) % SLOTS],
                       (r * (2 * M.per // SLOTS * 16)) + (((k - M.k0) * (EP * M.per // SLOTS * 16)) + 16 * ((M.first + i) // SLOTS + 1)))
            return ring[(M.first + i) % SLOTS]

        def wait_moe_done(eng, M, i, r, k):
            eng.wait_ge(M.done, nth(M.done0 + i + 1, M.per, r, k - M.k0))

        GATHER = [bank[1], bank[2]]
        YB = [bank[5], bank[6]]

        PARTS = [(0, 2 * C), (2 * C, EP * C)]

        def gather_pe(M, k, part):
            pe = nc.tensor
            a, b = PARTS[part]
            if part == 0:
                pe.wait_ge(M.sel, k + 1)
            else:
                pe.wait_ge(M.u_copied, (k * (EP * M.nf)) + 2 * M.nf)
                pe.wait_ge(M.act, (k * (EP * M.nf)) + 2 * M.nf)
            for kk in range(KD):
                if kk >= 2:
                    pe.wait_ge(M.xg_dve if kk % 2 else M.xg_act, (k * KD) + (4 * part + kk // 2))
                for t in range(T):
                    last = nc.tensor.matmul(GATHER[kk % 2][:, 0:b - a], xn[:, t, kk::KD], sel[:, t, a:b], start=(t == 0), stop=(t == T - 1))
                last.then_inc(M.gathered, 1)
            pe.wait_ge(M.xg_act, (k * KD) + 4 * (part + 1))
            pe.wait_ge(M.xg_dve, (k * KD) + 4 * (part + 1))
            pe.nop(nofuse=True)

        def gather_act(M, k, part):
            a, b = PARTS[part]
            for kk in range(0, KD, 2):
                nc.scalar.wait_ge(M.gathered, (k * 2 * KD) + (KD * part + kk + 1))
                bias = zero_col[:, 0:1] if M.shift is None else M.shift[:, kk:kk + 1]
                nc.scalar.activation(xgT[:, kk, a:b], GATHER[0][:, 0:b - a], ACT.Identity, bias=bias,
                                     scale=M.scale[:, kk:kk + 1]).then_inc(M.xg_act, 1)

        def gather_dve(M, k, part):
            v = nc.vector
            a, b = PARTS[part]
            for kk in range(1, KD, 2):
                v.wait_ge(M.gathered, (k * 2 * KD) + (KD * part + kk + 1))
                bias = zero_col[:, 0:1] if M.shift is None else M.shift[:, kk:kk + 1]
                v.tensor_scalar(xgT[:, kk, a:b], GATHER[1][:, 0:b - a], M.scale[:, kk:kk + 1], bias, ALU.mult, ALU.add).then_inc(M.xg_dve, 1)

        def select_dve(M, k, half, section=None):
            v = nc.vector
            iota = const("iota").unsqueeze(1).broadcast_to([P, EP, C])
            four = lambda a: a.rearrange("p (e c) -> p e c", c=C)
            e0 = EP * half
            for t in range(T):
                last = v.tensor_tensor(four(sel[:, t, :]), iota, rankm[:, t, e0:e0 + EP].unsqueeze(2).broadcast_to([P, EP, C]),
                                       ALU.is_equal)
            last.then_inc(M.sel, 1)
            if section is not None:
                ada_use_dve(section)
            v.wait_ge(M.sel, k + 1)
            for t in range(T):
                last = v.tensor_tensor(four(wsel[:, t, :]), four(sel[:, t, :]),
                                       comb[:, t, e0:e0 + EP].unsqueeze(2).broadcast_to([P, EP, C]), ALU.mult)
            last.then_inc(M.wsel, 1)

        def expert_up_pe(M, k, e, r):
            pe = nc.tensor
            b = e % 2
            pe.wait_ge(M.xs, nth(e + 1, 1, r, k))
            for hf in range(M.nf):
                q = e * M.nf + hf
                for up in range(2):
                    i = place_up(M, e, hf, up)
                    w = wait_moe_item(pe, M, i, r, k)
                    if q:
                        pe.wait_ge(M.u_copied if up else M.g_copied, nth(q, M.nf, r, k))
                    for kk in range(KD):
                        j = kk % 4
                        last = nc.tensor.matmul(bank[up][32 * j:32 * j + 32, :], xs[:, b * KD + kk, :], w[:, kk, :],
                                                start=(kk < 4), stop=(kk >= 4))
                    last.then_inc(M.done, 1)

        def expert_wT_pe(M, k, e, r):
            pe = nc.tensor
            pe.wait_ge(M.ws, nth(e + 1, 1, r, k))
            if e:
                pe.wait_ge(M.wT, nth(e, 1, r, k))
            for t in range(T):
                last = nc.tensor.transpose(bank[7][:, t * P:(t + 1) * P], ws[:, (e % 2) * T + t, :], ident)
            last.then_inc(M.w_turned, 1)

        def expert_turn_pe(M, k, e, hf, r):
            pe = nc.tensor
            q = e * M.nf + hf
            pe.wait_ge(M.g_copied, nth(q + 1, M.nf, r, k))
            pe.wait_ge(M.u_copied, nth(q + 1, M.nf, r, k))
            if q:
                pe.wait_ge(M.act, nth(q, M.nf, r, k))
            for up, src in enumerate((gate_s, up_s)):
                for f in range(4):
                    c = (2 * hf + up) * 4 * C + f * C
                    last = nc.tensor.matmul(bank[2][:, c:c + C], src[:, q % 2, f * P:(f + 1) * P], const("stack"), start=True, stop=True)
            last.then_inc(M.turned, 1)

        def expert_down_pe(M, k, e, r):
            pe = nc.tensor
            b = e % 2
            pe.wait_ge(M.act, nth((e + 1) * M.nf, M.nf, r, k))
            if e:
                pe.wait_ge(M.z0, nth(e, 1, r, k))
                pe.wait_ge(M.z1, nth(e, 1, r, k))
            if M.nd == 1:
                w = wait_moe_item(pe, M, place_down(M, e, 0), r, k)[:, :, :].rearrange("p a b -> p (a b)").rearrange("p (k n) -> p k n", n=D)
                for n in range(2):
                    for j in range(4):
                        last = nc.tensor.matmul(bank[3 + n][32 * j:32 * j + 32, :], act_s[:, b * KD + j, :],
                                                w[:, j, n * NC:(n + 1) * NC], start=True, stop=True)
                last.then_inc(M.done, 1)
                return
            for n in range(2):
                w = wait_moe_item(pe, M, place_down(M, e, n), r, k)
                for kk in range(KD):
                    j = kk % 4
                    last = nc.tensor.matmul(bank[3 + n][32 * j:32 * j + 32, :], act_s[:, b * KD + kk, :], w[:, kk, :],
                                            start=(kk < 4), stop=(kk >= 4))
                last.then_inc(M.done, 1)

        def expert_back_pe(M, k, e, r):
            pe = nc.tensor
            pe.wait_ge(M.z0, nth(e + 1, 1, r, k))
            pe.wait_ge(M.z1, nth(e + 1, 1, r, k))
            pe.wait_ge(M.wT, nth(e + 1, 1, r, k))
            for t in range(T):
                for n in range(2):
                    i = 4 * e + 2 * t + n
                    if i >= 2:
                        pe.wait_ge(M.y_added, nth(i - 1, 4, r, k))
                    nc.tensor.matmul(YB[i % 2][:, :], wselT[:, e % 2, t * P:(t + 1) * P], z_s[:, n * NC:(n + 1) * NC],
                                     start=True, stop=True).then_inc(M.y, 1)

        def copy_up(M, k, e, hf, r, up):
            eng = nc.scalar if up == 0 or M.gate is not None else nc.vector
            q = e * M.nf + hf
            wait_moe_done(eng, M, place_up(M, e, hf, up), r, k)
            if q >= 2:
                eng.wait_ge(M.turned, nth(q - 1, M.nf, r, k))
            dst = (up_s if up else gate_s)[:, q % 2, :]
            if up == 0 or M.gate is not None:
                nc.scalar.activation(dst, bank[up][:, :], ACT.Copy).then_inc(M.u_copied if up else M.g_copied, 1)
            else:
                nc.vector.tensor_copy(dst, bank[up][:, :]).then_inc(M.u_copied, 1)

        def copy_wT_act(M, k, e, r):
            nc.scalar.wait_ge(M.w_turned, nth(e + 1, 1, r, k))
            if e >= 2:
                nc.scalar.wait_ge(M.y, nth(4 * (e - 1), 4, r, k))
            nc.scalar.activation(wselT[:, e % 2, :], bank[7][:, 0:S], ACT.Copy).then_inc(M.wT, 1)

        def silu_act(M, k, e, hf, r):
            q = e * M.nf + hf
            nc.scalar.wait_ge(M.turned, nth(q + 1, M.nf, r, k))
            if q >= 2:
                nc.scalar.wait_ge(M.act, nth(q - 1, M.nf, r, k))
            c = 2 * hf * 4 * C
            nc.scalar.activation(silu_s[:, q % 2, :], bank[2][:, c:c + 4 * C], ACT.Silu).then_inc(M.silu, 1)

        def act_dve(M, k, e, hf, r):
            q = e * M.nf + hf
            nc.vector.wait_ge(M.silu, nth(q + 1, M.nf, r, k))
            c = (2 * hf + 1) * 4 * C
            at = (e % 2) * KD + 4 * hf
            nc.vector.tensor_tensor(act_s[:, at:at + 4, :], silu_s[:, q % 2, :].rearrange("p (f c) -> p f c", c=C),
                                    bank[2][:, c:c + 4 * C].rearrange("p (f c) -> p f c", c=C), ALU.mult).then_inc(M.act, 1)

        def copy_z(M, k, e, n, r):
            eng = nc.scalar if n == 0 and M.gate is None else nc.vector
            wait_moe_done(eng, M, place_down(M, e, n if M.nd == 2 else 0), r, k)
            if e:
                eng.wait_ge(M.y, nth(4 * e, 4, r, k))
            dst, src = z_s[:, n * NC:(n + 1) * NC], bank[3 + n][:, :]
            if M.gate is not None:
                nc.vector.tensor_tensor(dst, src, M.gate[:, n * NC:(n + 1) * NC], ALU.mult).then_inc(M.z1 if n else M.z0, 1)
            elif n == 0:
                nc.scalar.activation(dst, src, ACT.Copy).then_inc(M.z0, 1)
            else:
                nc.vector.tensor_copy(dst, src).then_inc(M.z1, 1)

        def add_y_dve(M, k, e, r):
            for t in range(T):
                for n in range(2):
                    i = 4 * e + 2 * t + n
                    nc.vector.wait_ge(M.y, nth(i + 1, 4, r, k))
                    dst = h[:, t, n * NC:(n + 1) * NC]
                    nc.vector.tensor_tensor(dst, dst, YB[i % 2][:, :], ALU.add).then_inc(M.y_added, 1)

        def expert_pe(M, k, e, r):
            expert_up_pe(M, k, e, r)
            expert_wT_pe(M, k, e, r)
            for hf in range(M.nf - 1):
                expert_turn_pe(M, k, e, hf, r)
            if e:
                expert_down_pe(M, k, e - 1, r)
            expert_turn_pe(M, k, e, M.nf - 1, r)
            if e:
                expert_back_pe(M, k, e - 1, r)

        def expert_act(M, k, e, r):
            for hf in range(M.nf):
                copy_up(M, k, e, hf, r, 0)
                if M.gate is not None:
                    copy_up(M, k, e, hf, r, 1)
            copy_wT_act(M, k, e, r)
            for hf in range(M.nf - 1):
                silu_act(M, k, e, hf, r)
            if e and M.gate is None:
                copy_z(M, k, e - 1, 0, r)
            silu_act(M, k, e, M.nf - 1, r)

        def expert_dve(M, k, e, r):
            if M.gate is None:
                for hf in range(M.nf):
                    copy_up(M, k, e, hf, r, 1)
            for hf in range(M.nf - 1):
                act_dve(M, k, e, hf, r)
            if e:
                if M.gate is not None:
                    copy_z(M, k, e - 1, 0, r)
                copy_z(M, k, e - 1, 1, r)
            act_dve(M, k, e, M.nf - 1, r)
            if e:
                add_y_dve(M, k, e - 1, r)

        def expert_pool(M, k, e, r):
            pool = nc.gpsimd
            b = e % 2
            at = (r * (2 * C)) + e * C
            if e >= 2:
                wait_moe_done(pool, M, place_up(M, e - 2, M.nf - 1, 1), r, k)
            nc.gpsimd.nop(nofuse=True)
            nc.gpsimd.tensor_copy(xs[:, b * KD:(b + 1) * KD, :], xgT[:, :, bass.ds(at, C)]).then_inc(M.xs, 1)
            if e >= 2:
                pool.wait_ge(M.w_turned, nth(e - 1, 1, r, k))
            nc.gpsimd.nop(nofuse=True)
            for t in range(T):
                last = nc.gpsimd.tensor_copy(ws[:, b * T + t, :].rearrange("p (j c) -> p j c", c=C),
                                             wsel[:, t, bass.ds(at, C)].unsqueeze(1).broadcast_to([P, 4, C]))
            last.then_inc(M.ws, 1)

        def all_experts(eng, step, M, k, between=None):
            step(M, k, 0, 0)
            step(M, k, 1, 0)
            if between:
                between()
            with eng.Fori(0, EP // 2 - 1) as r:
                step(M, k, 2, r)
                step(M, k, 3, r)

        def pass_pe(M, k):
            gather_pe(M, k, 0)
            all_experts(nc.tensor, expert_pe, M, k, lambda: gather_pe(M, k, 1))
            expert_down_pe(M, k, EP - 1, 0)
            expert_back_pe(M, k, EP - 1, 0)

        def pass_act(M, k):
            gather_act(M, k, 0)
            all_experts(nc.scalar, expert_act, M, k, lambda: gather_act(M, k, 1))
            if M.gate is None:
                copy_z(M, k, EP - 1, 0, 0)

        def pass_dve(M, k, half, section=None):
            select_dve(M, k, half, section)
            gather_dve(M, k, 0)
            all_experts(nc.vector, expert_dve, M, k, lambda: gather_dve(M, k, 1))
            if M.gate is not None:
                copy_z(M, k, EP - 1, 0, 0)
            copy_z(M, k, EP - 1, 1, 0)
            add_y_dve(M, k, EP - 1, 0)

        def pass_pool(M, k):
            def gathered(part):
                nc.gpsimd.wait_ge(M.xg_act, (k * KD) + 4 * (part + 1))
                nc.gpsimd.wait_ge(M.xg_dve, (k * KD) + 4 * (part + 1))

            nc.gpsimd.wait_ge(M.wsel, k + 1)
            gathered(0)
            nc.gpsimd.nop(nofuse=True)
            all_experts(nc.gpsimd, expert_pool, M, k, lambda: (gathered(1), nc.gpsimd.nop(nofuse=True)))

        def load_expert(M, k, e, r, src, free):
            def put(i, rows_):
                free(M, k, i, r)
                slot = (M.first + i) % SLOTS
                nc.sync.dma_start(ring[slot][:, :, :].rearrange("p a b -> p (a b)").rearrange("p (k n) -> p k n", n=rows_.shape[2]),
                                  rows_).then_inc(M.arrived[slot], 16)

            if e < EP:
                x = (r * 2) + e
                for hf in range(M.nf):
                    for up in range(2):
                        put(place_up(M, e, hf, up), src(up, x, hf))
            if e:
                x = (r * 2) + (e - 1)
                for n in range(M.nd):
                    put(place_down(M, e - 1, n), src(2, x, n))

        def pass_sp(M, k, src, free):
            def slots_free():
                if M.first and k == M.k0:
                    nc.sync.wait_ge(*released[M.first - 1])

            all_experts(nc.sync, lambda M, k, e, r: load_expert(M, k, e, r, src, free), M, k, slots_free)
            load_expert(M, k, EP, 0, src, free)

        def free_in_pass(M, k, i, r):
            nc.sync.wait_ge(M.done, nth(M.done0 + i + 1 - SLOTS, M.per, r, k - M.k0))

        def src1(half):
            def src(what, x, n):
                if what == 2:
                    return w_down[0, x + EP * half].rearrange("(k p) n -> p k n", p=P)
                return (w_up if what else w_gate)[0, x + EP * half].rearrange("(p k) n -> p k n", p=P)
            return src

        def src2(l):
            def src(what, x, n):
                w = (moe_w_gate, moe_w_up, moe_w_down)[what][l, x][:, n * NC:(n + 1) * NC]
                return w.rearrange("(k p) n -> p k n" if what == 2 else "(p k) n -> p k n", p=P)
            return src

        main = (arrived, item_done)
        M1 = Mixture(kind1, 1, 1, *main, ITEM["moe", 0], done_at[ITEM["moe", 0]] - 1, 0, col("norm_ffn"), None, None)
        MX = Mixture(kind1, 1, 1, [sem(f"more_arrived{i}") for i in range(SLOTS)], sem("more_item_done"), 0, 0, 2, col("norm_ffn"), None, None)
        shifted = sem("slots_shifted")

        def more_passes(eng, one_pass, at_end=None):
            eng.wait_ge(flag_done, 1)
            passes = eng.value_load(flag[0:1, 0:1], min_val=0, max_val=PC)
            with eng.If(passes > 0):
                with eng.Fori(0, passes) as p:
                    for half in range(2):
                        one_pass(p, (p * 2) + (2 + half), half)
                if at_end:
                    eng.wait_ge(MX.y_added, (passes * (2 * 4 * EP)) + 2 * 4 * EP)
                    eng.nop(nofuse=True)

        def more_dve(p, k, half):
            if half == 0:
                nc.vector.tensor_scalar(rankm[:, :, :], rankm[:, :, :], -float(C), None, ALU.add).then_inc(shifted, 1)
                nc.vector.wait_ge(shifted, p + 1)
            pass_dve(MX, k, half)

        def free_more(M, k, i, r):
            if i < SLOTS and isinstance(r, int):
                nc.sync.wait_ge(MX.sel, k + 1)
            else:
                free_in_pass(M, k, i, r)

        M2 = [Mixture(kind2, 2, 2, *main, ITEM["moe", 1 + l], done_at[ITEM["moe", 1 + l]] - 1, l, mod[:, l, 3, :], mod[:, l, 2, :],
                      gate_rows[:, l, 1, :]) for l in range(2)]

        NH2 = 6
        KB = 2 * T
        DV = 2 * HD
        AW = NH2 * DV
        arena_at[0] = 0
        qT2, kT2 = carve(NH2, S), carve(NH2, 2 * S)
        v2 = carve(KB, AW)
        ctx_at = arena_at[0]
        ctxT = carve(KD, S)
        temps2_at = arena_at[0]
        sq2, qn2, tmp2 = carve(2, NC), carve(2, NC), carve(NC)
        ctx_rows = gate_rows[:, 1, :, :]
        fT = carve(2, S, at=ctx_at)
        fCS = carve(T, NC, at=temps2_at)
        pr2 = carve(4, NC, at=ctx_at)
        mixw, mixT = carve(2, NC), carve(2, NC)
        V0 = 2 * AW

        def block(a, t):
            return a[:, :, t * P:(t + 1) * P]

        q_row, k_row = row("q_att"), row("k_att")
        units2 = []
        for n in range(5):
            for t in range(T):
                un = dict(item=ITEM["proj2"] + n, lhs=block(hT, t), cols=(0, NC), kind="qk", rope=rope_of(rope2, t))
                if n == 0:
                    un.update(gains=[(8, q_row)], put=[(0, 4, block(qT2[:, 0:4, :], t))])
                elif n == 1:
                    un.update(gains=[(4, q_row), (4, k_row)],
                              put=[(0, 2, block(qT2[:, 4:6, :], t)), (2, 2, block(kT2[:, 0:2, :], t))])
                elif n == 2:
                    un.update(gains=[(8, k_row)], put=[(0, 4, block(kT2[:, 2:6, :], t))])
                else:
                    w = (NC, AW - NC)[n - 3]
                    un.update(kind="v", cols=(0, w), put=[((0, w), v2[:, t, (n - 3) * NC:(n - 3) * NC + w])])
                units2.append(un)
            for t in range(T):
                un = dict(item=ITEM["proj2"] + n, lhs=block(ctxT, t), cols=(0, NC), kind="qk", rope=None)
                if n == 0:
                    continue
                if n == 1:
                    un.update(cols=(NC // 2, NC // 2), gains=[(4, k_row)], put=[(0, 2, block(kT2[:, 0:2, :], T + t))])
                elif n == 2:
                    un.update(gains=[(8, k_row)], put=[(0, 4, block(kT2[:, 2:6, :], T + t))])
                else:
                    w = (NC, AW - NC)[n - 3]
                    un.update(kind="v", cols=(0, w), put=[((0, w), v2[:, T + t, (n - 3) * NC:(n - 3) * NC + w])])
                units2.append(un)
        units2[2]["ready"] = hT_ready(4)
        h2 = heads("h2", units2, sq2, qn2, tmp2, hT_ready(3))
        NU2 = len(units2)

        ft_c, fa_mm, fa_c, fy_mm, fy_c = sem("ft_c"), sem("fa_mm"), sem("fa_c"), sem("fy_mm"), sem("fy_c")

        def fourier_pe():
            pe = nc.tensor
            i = ITEM["proj2"] + 4
            for b in range(2):
                for k in range(KD):
                    last = nc.tensor.matmul(bank[4][:, b * S:(b + 1) * S], ring[i % SLOTS][:, k, S + b * P:S + (b + 1) * P],
                                            hT[:, k, :], start=(k == 0), stop=(k == KD - 1))
            last.then_inc(item_done, 1)
            pe.wait_ge(ft_c, 1)
            for t in range(T):
                for b in range(2):
                    last = nc.tensor.matmul(bank[4 + t][:, b * S:(b + 1) * S], fT[:, b, t * P:(t + 1) * P], const("chan"),
                                            start=True, stop=True)
            last.then_inc(fa_mm, 1)
            pe.wait_ge(fa_c, 1)
            for t2 in range(T):
                n = 0
                for t in range(T):
                    for c, name in enumerate(("dftc", "dfts")):
                        rhs = fCS[:, t, :].rearrange("p (b c d) -> p c b d", b=2, c=2)[:, c, :, :]
                        last = nc.tensor.matmul(bank[4 + t2][:, 0:S], const(name)[:, t * S + t2 * P:t * S + (t2 + 1) * P], rhs,
                                                start=(n == 0), stop=(n == 3))
                        n += 1
            last.then_inc(fy_mm, 1)

        def fourier_act():
            act = nc.scalar
            act.wait_ge(item_done, done_at[ITEM["proj2"] + 4])
            act.activation(fT[:, :, :], bank[4][:, :].rearrange("p (b s) -> p b s", b=2), ACT.Copy).then_inc(ft_c, 1)
            act.wait_ge(fa_mm, 1)
            for s_, v in h2["done"]:
                act.wait_ge(s_, v)
            for t in range(T):
                last = nc.scalar.activation(fCS[:, t, :], bank[4 + t][:, :], ACT.Copy)
            last.then_inc(fa_c, 1)
            act.wait_ge(fy_mm, 1)
            for t in range(T):
                last = nc.scalar.activation(xn[:, t, AW:D], bank[4 + t][:, 0:S], ACT.Copy)
            last.then_inc(fy_c, 1)

        a2_s, a2_m, a2_e, a2_r, a2_p, a2_w = (sem("a2_" + n) for n in ("scores", "max", "exp", "recip", "first", "mixed"))
        a2_t, a2_c, a2_v, a2_o, a2_b = (sem("a2_" + n) for n in ("turned", "copied", "values", "out", "banks_read"))
        att2 = [(t, hd) for t in range(T) for hd in range(NH2)]
        negm2, lsum2, neglam = small[:, 160:184], small[:, 184:208], small[:, 208:209]
        r2 = small[:, 212:216]

        def lambda_dve():
            v = nc.vector
            lp = small[:, 216:218]
            for n in range(2):
                dve_step(v.tensor_tensor(tmp2[:, 0:HD], row(f"lam_q{n + 1}"), row(f"lam_k{n + 1}"), ALU.mult))
                ins = v.tensor_reduce(lp[:, n:n + 1], tmp2[:, 0:HD], AX.X, ALU.add)
                dve_step(ins) if n == 0 else ins.then_inc(lam_dot, 1)
            v.wait_ge(lam_exp, 1)
            dve_step(v.tensor_tensor(neglam, lp[:, 1:2], lp[:, 0:1], ALU.subtract))
            dve_step(v.tensor_scalar(neglam, neglam, -LAM_INIT, None, ALU.add))
            dve_step(v.tensor_scalar(cols[0:AW // KD, COLS.index("subln"), :], cols[0:AW // KD, COLS.index("subln"), :],
                                     (1.0 - LAM_INIT) * float(DV) ** 0.5, None, ALU.mult))

        lam_dot, lam_exp = sem("lam_dot"), sem("lam_exp")

        def lambda_act():
            nc.scalar.wait_ge(lam_dot, 1)
            nc.scalar.activation(small[:, 216:218], small[:, 216:218], ACT.Exp).then_inc(lam_exp, 1)

        def scores2_pe(u):
            pe = nc.tensor
            t, hd = att2[u]
            if u == 0:
                pe.wait_ge(fy_c, 1)
                for s_, v in h2["done"]:
                    pe.wait_ge(s_, v)
            for m in range(2):
                w = 2 * u + m
                if w >= 3:
                    pe.wait_ge(a2_e, w - 2)
                nc.tensor.matmul(bank[w % 3][:, :], qT2[m * HD:(m + 1) * HD, hd, t * P:(t + 1) * P],
                                 kT2[m * HD:(m + 1) * HD, hd, :], start=True, stop=True).then_inc(a2_s, 1)

        def max2_dve(u):
            for m in range(2):
                w = 2 * u + m
                nc.vector.wait_ge(a2_s, w + 1)
                nc.vector.tensor_reduce(negm2[:, w:w + 1], bank[w % 3][:, :], AX.X, ALU.max, negate=True).then_inc(a2_m, 1)

        def exp2_act(u):
            for m in range(2):
                w = 2 * u + m
                nc.scalar.wait_ge(a2_m, w + 1)
                if u >= 2:
                    nc.scalar.wait_ge(a2_w, u - 1)
                nc.scalar.activation(pr2[:, w % 4, :], bank[w % 3][:, :], ACT.Exp, bias=negm2[:, w:w + 1],
                                     accum_out=lsum2[:, w:w + 1]).then_inc(a2_e, 1)

        def recip2_dve(u):
            v = nc.vector
            r = r2[:, 2 * (u % 2):2 * (u % 2) + 2]
            v.wait_ge(a2_e, 2 * u + 2)
            dve_step(v.reciprocal(r, lsum2[:, 2 * u:2 * u + 2]))
            v.tensor_tensor(r[:, 1:2], r[:, 1:2], neglam, ALU.mult).then_inc(a2_r, 1)

        def first2_act(u):
            act = nc.scalar
            act.wait_ge(a2_r, u + 1)
            if u >= 2:
                act.wait_ge(a2_t, u - 1)
            nc.scalar.activation(mixw[:, u % 2, :], pr2[:, 2 * (u % 2), :], ACT.Copy,
                                 scale=r2[:, 2 * (u % 2):2 * (u % 2) + 1]).then_inc(a2_p, 1)

        def mix2_dve(u):
            v = nc.vector
            v.wait_ge(a2_p, u + 1)
            v.wait_ge(a2_r, u + 1)
            v.scalar_tensor_tensor(mixw[:, u % 2, :], pr2[:, 2 * (u % 2) + 1, :], r2[:, 2 * (u % 2) + 1:2 * (u % 2) + 2],
                                   mixw[:, u % 2, :], ALU.mult, ALU.add).then_inc(a2_w, 1)

        def turn2_pe(u):
            pe = nc.tensor
            pe.wait_ge(a2_w, u + 1)
            if u:
                pe.wait_ge(a2_c, u)
            for b in range(KB):
                last = nc.tensor.transpose(bank[3][:, b * P:(b + 1) * P], mixw[:, u % 2, b * P:(b + 1) * P], ident)
            last.then_inc(a2_t, 1)

        def copy2_act(u):
            nc.scalar.wait_ge(a2_t, u + 1)
            if u >= 2:
                nc.scalar.wait_ge(a2_v, u - 1)
            nc.scalar.activation(mixT[:, u % 2, :], bank[3][:, :], ACT.Copy).then_inc(a2_c, 1)

        def values2_pe(u):
            pe = nc.tensor
            t, hd = att2[u]
            pe.wait_ge(a2_c, u + 1)
            if t and hd % 4 == 0:
                pe.wait_ge(a2_b, 1 + hd // 4)
            for b in range(KB):
                last = nc.tensor.matmul(bank[6 + hd // 4][:, (hd % 4) * DV:(hd % 4 + 1) * DV], mixT[:, u % 2, b * P:(b + 1) * P],
                                        v2[:, b, hd * DV:(hd + 1) * DV], start=(b == 0), stop=(b == KB - 1))
            last.then_inc(a2_v, 1)

        def out2_dve(t, n):
            v = nc.vector
            s6 = small[:, 218:224]
            h0, nh = ((0, 4), (4, 2))[n]
            v.wait_ge(a2_v, NH2 * t + h0 + nh)
            dst = xn[:, t, h0 * DV:(h0 + nh) * DV]
            v.tensor_copy(dst, bank[6 + n][:, 0:nh * DV]).then_inc(a2_b, 1)
            v.wait_ge(a2_b, 2 * t + n + 1)
            dve_step(v.tensor_tensor(out_scaled[:, 0:nh * DV], dst, dst, ALU.mult))
            dve_step(v.tensor_reduce(s6[:, h0:h0 + nh], out_scaled[:, 0:nh * DV].rearrange("p (h d) -> p h d", d=DV), AX.X, ALU.add))
            if n:
                sums_added(s6, DV)

        def out2_norm_dve(t):
            v = nc.vector
            r6 = small[:, 224:230]
            v.wait_ge(roots_done, chain_at["sums"])
            o = xn[:, t, 0:AW].rearrange("p (h d) -> p h d", d=DV)
            v.tensor_tensor(o, o, r6.unsqueeze(2).broadcast_to([P, NH2, DV]), ALU.mult).then_inc(a2_o, 1)

        L2 = len(att2) - 1

        def steps2():
            for u in range(NU2):
                yield "proj", u
                if u >= 2:
                    yield "tr", u - 2
            yield "tr", NU2 - 2
            yield "tr", NU2 - 1
            yield "fourier", 0
            s = 6
            for u in range(L2 + 4):
                if u <= L2:
                    yield "scores", u
                if 1 <= u <= L2 + 1:
                    yield "mix", u - 1
                if 2 <= u <= L2 + 2:
                    yield "turn", u - 2
                if u == L2 + 1:
                    yield "first", 0
                if u >= 3:
                    yield "values", u - 3
                    if (u - 3) % NH2 == 3:
                        yield "out4", (u - 3) // NH2
                    if (u - 3) % NH2 == NH2 - 1:
                        yield "out", (u - 3) // NH2
                    if (u - 3) % NH2 == 0 and u > 3 or u == L2 + 3:
                        yield "normed", (u - 4) // NH2
                if u % 3 == 0 and s < 6 + EARLY:
                    yield "ada_mm", s
                if u % 3 == 1 and s < 6 + EARLY:
                    yield "ada_sum", s
                    s += 1

        def block2_pe():
            for t in range(T):
                tr_pe(3, t, xn_ready(2, t), ZB)
            for what, i in steps2():
                if what == "proj":
                    if i == 1:
                        for t in range(T):
                            tr_pe(4, t, xn_ready(3, t))
                    h2["proj_pe"](i)
                elif what == "tr":
                    h2["tr_pe"](i)
                elif what == "fourier":
                    fourier_pe()
                elif what == "scores":
                    scores2_pe(i)
                elif what == "turn":
                    turn2_pe(i)
                elif what == "values":
                    values2_pe(i)
                elif what == "ada_mm":
                    ada_mm_pe(i)
                elif what == "ada_sum":
                    ada_sum_pe(i)
                elif what == "first":
                    tr_pe(5, 0, [(a2_o, 1), (ada_used, 6 + EARLY)], AB)
            out_pe(1, 0, hT, hT_ready(5, 0), (0,))
            tr_pe(5, 1, [(a2_o, 2)], AB)
            out_pe(1, 0, hT, [], (1,))
            last_out_pe(1, hT, hT_ready(5), 4, 6)

        def block2_act(ready):
            norm_act(2, h, 3, ready)
            both_act(3, hT, mod[:, 0, 1, :], mod[:, 0, 0, :], ZB)
            norm_act(3, ctx_rows, 4, [(ctx_loaded, 16)])
            both_act(4, ctxT, mod_ctx[:, 1, :], mod_ctx[:, 0, :])
            for t in range(T):
                nc.scalar.wait_ge(xn_done[t], 4)
            load_gates_act(1)
            lambda_act()
            for what, i in steps2():
                if what == "proj":
                    h2["post_act"](i)
                elif what == "tr":
                    h2["put_act"](i)
                elif what == "fourier":
                    fourier_act()
                elif what == "scores":
                    exp2_act(i)
                elif what == "mix":
                    first2_act(i)
                elif what == "turn":
                    copy2_act(i)
                elif what == "ada_mm":
                    ada_rows_act(i)
                elif what == "first":
                    tr_act(5, 0, hT, col("subln"), None, AB)
            tr_act(5, 1, hT, col("subln"), None, AB)

        def block2_dve(ready):
            norm_dve(2, h, 3, ready)
            both_dve(3, hT, mod[:, 0, 1, :], mod[:, 0, 0, :], ZB)
            norm_dve(3, ctx_rows, 4, [(ctx_loaded, 16)])
            both_dve(4, ctxT, mod_ctx[:, 1, :], mod_ctx[:, 0, :])
            lambda_dve()
            for what, i in steps2():
                if what == "proj":
                    h2["post_dve"](i)
                elif what == "scores":
                    max2_dve(i)
                    recip2_dve(i)
                elif what == "mix":
                    mix2_dve(i)
                elif what == "out":
                    out2_dve(i, 1)
                elif what == "out4":
                    out2_dve(i, 0)
                elif what == "normed":
                    out2_norm_dve(i)
                elif what == "ada_sum":
                    ada_use_dve(i)
                elif what == "first":
                    tr_dve(5, 0, hT, col("subln"), None, AB)
            tr_dve(5, 1, hT, col("subln"), None, AB)
            out_dve(1, gate_rows[:, 0, 0, :], lambda: tr_dve(6, 0, hT, mod[:, 0, 3, :], mod[:, 0, 2, :]))

        def block2_pool():
            norm_pool(2)
            norm_pool(3)
            for what, i in steps2():
                if what == "proj":
                    h2["rope_pool"](i)
                elif what == "out":
                    root_pool(small[:, 224:230], small[:, 218:224])

        arena_at[0] = 0
        cg = carve(4, S)
        zp = carve(KD, S + 2)
        conv = carve(KD, S)
        mix3 = carve(KD, S)
        c_copied, z_done, cv_done, mix_done = sem("c_copied"), sem("z_done"), sem("conv_done"), sem("mix_done")

        def odd_banks(i):
            return [bank[2 * (i % 3)], bank[2 * (i % 3) + 1]]

        def odd_pe():
            pe = nc.tensor
            for t in range(T):
                tr_pe(7, t, xn_ready(5, t), ZB)
            for s_, v in hT_ready(7):
                pe.wait_ge(s_, v)
            for i in range(6):
                it = ITEM["proj3"] + i
                wait_item(pe, it)
                if i >= 3:
                    if i == 3:
                        pe.wait_ge(c_copied, 1)
                    elif i == 4:
                        pe.wait_ge(z_done, 4)
                    else:
                        pe.wait_ge(mix_done, 4)
                for b in range(4):
                    for k in range(KD):
                        last = nc.tensor.matmul(odd_banks(i)[b // 2][:, (b % 2) * S:(b % 2 + 1) * S],
                                                ring[it % SLOTS][:, k, b * P:(b + 1) * P], hT[:, k, :],
                                                start=(k == 0), stop=(k == KD - 1))
                last.then_inc(item_done, 1)
            out_pe(2, 0, mix3, [(mix_done, 8)])
            last_out_pe(2, mix3, [], 6, 8)

        def odd_act(ready):
            norm_act(5, h, 7, ready)
            both_act(7, hT, mod[:, 1, 1, :], mod[:, 1, 0, :], ZB)
            for n in range(2):
                i = 3 * n
                nc.scalar.wait_ge(item_done, done_at[ITEM["proj3"] + i])
                if n:
                    nc.scalar.wait_ge(z_done, 4)
                for b in range(2):
                    last = nc.scalar.activation(cg[:, 2 * b:2 * b + 2, :], odd_banks(i)[b][:, :].rearrange("p (a s) -> p a s", a=2), ACT.Copy)
                last.then_inc(c_copied, 1)

        def odd_dve(ready):
            v = nc.vector
            norm_dve(5, h, 7, ready)
            both_dve(7, hT, mod[:, 1, 1, :], mod[:, 1, 0, :], ZB)
            dve_step(v.memset(zp[:, :, 0:1], 0.0))
            dve_step(v.memset(zp[:, :, S + 1:S + 2], 0.0))
            for n in range(2):
                i = 3 * n
                v.wait_ge(item_done, done_at[ITEM["proj3"] + i + 1])
                v.wait_ge(c_copied, n + 1)
                for b in range(4):
                    v.tensor_tensor(zp[:, 4 * n + b, 1:S + 1], odd_banks(i + 1)[b // 2][:, (b % 2) * S:(b % 2 + 1) * S],
                                    cg[:, b, :], ALU.mult).then_inc(z_done, 1)
                v.wait_ge(z_done, 4 * (n + 1))
                for j in range(3):
                    for b in range(4):
                        c = 4 * n + b
                        w = col(f"conv{j}")[:, c:c + 1]
                        if j == 0:
                            ins = v.tensor_scalar(conv[:, c, :], zp[:, c, 0:S], w, None, ALU.mult)
                        else:
                            ins = v.scalar_tensor_tensor(conv[:, c, :], zp[:, c, j:j + S], w, conv[:, c, :], ALU.mult, ALU.add)
                        ins.then_inc(cv_done, 1)
                    v.wait_ge(cv_done, 12 * n + 4 * (j + 1))
                v.wait_ge(item_done, done_at[ITEM["proj3"] + i + 2])
                for b in range(4):
                    c = 4 * n + b
                    v.tensor_tensor(mix3[:, c, :], conv[:, c, :], odd_banks(i + 2)[b // 2][:, (b % 2) * S:(b % 2 + 1) * S],
                                    ALU.mult).then_inc(mix_done, 1)
            out_dve(2, gate_rows[:, 1, 0, :], lambda: tr_dve(8, 0, hT, mod[:, 1, 3, :], mod[:, 1, 2, :]))

        stored = sem("stored")
        block = stack.enter_context(nc.Block())

        @block.sync
        def _(sp):
            sp.dma_start(h[:, :, :], x[0].rearrange("(t p) d -> p t d", p=P)).then_inc(x_loaded, 16)
            sp.dma_start(cols[:, :, :], cols_in.rearrange("p (n k) -> p n k", k=KD)).then_inc(first_loaded, 16)
            sp.dma_start(ident, const_in[:, 0:P]).then_inc(first_loaded, 16)
            big = {"w_in": w_in[0], "w_out": w_out[0], "attn_w_in": attn_w_in[0], "attn_w_out": attn_w_out[0],
                   "conv_w_in": conv_w_in[0], "conv_w_out": conv_w_out[0]}

            def load(a, b):
                for i in range(a, b):
                    what = items[i]
                    if i >= SLOTS:
                        sp.wait_ge(*released[i - SLOTS])
                    src, c = (ada_w[what[1]], what[2]) if what[0] == "ada" else (big[what[0]], what[1])
                    order = "(k p) n -> p k n" if what[0] == "conv_w_out" else "(p k) n -> p k n"
                    sp.dma_start(ring[i % SLOTS][:, :, :], src[:, c:c + NC].rearrange(order, p=P)).then_inc(arrived[i % SLOTS], 16)

            def free_main(M, k, i, r):
                j = M.first + i - SLOTS
                if i < SLOTS and isinstance(r, int) and k == M.k0:
                    sp.wait_ge(*released[j])
                else:
                    free_in_pass(M, k, i, r)

            load(0, 1)
            sp.dma_start(router_sb[:, :, :], router.rearrange("(p k) n -> p k n", k=KD)).then_inc(const_loaded, 16)
            sp.dma_start(rows[:, :], rows_in.broadcast_to([P, sum(ROW_W)])).then_inc(const_loaded, 16)
            sp.dma_start(cb[:, P:], const_in[:, P:]).then_inc(const_loaded, 16)
            load(1, ITEM["moe", 0])
            for half in range(2):
                pass_sp(M1, half, src1(half), free_main)
            more_passes(sp, lambda p, k, half: pass_sp(MX, k, src1(half), free_more), at_end=True)
            load(ITEM["proj2"], ITEM["moe", 1])
            pass_sp(M2[0], 0, src2(0), free_main)
            load(ITEM["proj3"], ITEM["moe", 2])
            pass_sp(M2[1], 1, src2(1), free_main)
            sp.wait_ge(M2[1].y_added, 8 * EP)
            sp.dma_start(out[0].rearrange("(t p) d -> p t d", p=P), h[:, :, :]).then_inc(stored, 16)
            sp.wait_ge(stored, 16)

        @block.gpsimd
        def _(pool):
            nc.gpsimd.memset(zero_col[:, :], 0.0)
            nc.gpsimd.memset(minus_half[:, :], -0.5)
            nc.gpsimd.memset(condT[:, :, :], 0.0).then_inc(setup_done, 1)
            block1_pool()
            norm_pool(1)
            for k in range(2):
                pass_pool(M1, k)
            more_passes(pool, lambda p, k, half: pass_pool(MX, k))
            block2_pool()
            norm_pool(4)
            pass_pool(M2[0], 0)
            norm_pool(5)
            norm_pool(6)
            pass_pool(M2[1], 1)

        @block.scalar
        def _(act):
            act.wait_ge(setup_done, 1)
            block1_act()
            norm_act(1, h, 2, out_ready(0, 0))
            tr_act(2, 0, hT, col("norm_ffn"), None)
            tr_act(2, 1, hT, col("norm_ffn"), None)
            ada_rows_act(EARLY)
            route1_act(EARLY)
            for k in range(2):
                pass_act(M1, k)
            more_passes(act, lambda p, k, half: pass_act(MX, k), at_end=True)
            block2_act([(M1.y_added, 8 * EP - 2)])
            norm_act(4, h, 6, out_ready(1, 0))
            tr_act(6, 0, hT, mod[:, 0, 3, :], mod[:, 0, 2, :])
            tr_act(6, 1, hT, mod[:, 0, 3, :], mod[:, 0, 2, :])
            ada_rows_act(6 + EARLY)
            route2_act(0, 6 + EARLY)
            pass_act(M2[0], 0)
            odd_act([(M2[0].y_added, 4 * EP - 2)])
            norm_act(6, h, 8, out_ready(2, 0))
            both_act(8, hT, mod[:, 1, 3, :], mod[:, 1, 2, :])
            route2_act(1)
            pass_act(M2[1], 1)

        @block.vector
        def _(dve):
            dve.wait_ge(setup_done, 1)
            block1_dve()
            norm_dve(1, h, 2, out_ready(0, 1))
            tr_dve(2, 1, hT, col("norm_ffn"), None)
            route1_dve(EARLY)
            for k in range(2):
                pass_dve(M1, k, k, None if k else EARLY + 1)
            more_passes(dve, more_dve, at_end=True)
            block2_dve([(M1.y_added, 8 * EP)])
            norm_dve(4, h, 6, out_ready(1, 1))
            tr_dve(6, 1, hT, mod[:, 0, 3, :], mod[:, 0, 2, :])
            route2_dve(0, 6 + EARLY)
            pass_dve(M2[0], 0, 0, 6 + EARLY + 1)
            odd_dve([(M2[0].y_added, 4 * EP)])
            norm_dve(6, h, 8, out_ready(2, 1))
            tr_dve(8, 1, hT, mod[:, 1, 3, :], mod[:, 1, 2, :])
            route2_dve(1)
            pass_dve(M2[1], 1, 0)

        @block.tensor
        def _(pe):
            block1_pe()
            logits_pe(1, 2, 0, G1 + E1, EARLY)
            rank_pe(EARLY)
            for k in range(2):
                pass_pe(M1, k)
            more_passes(pe, lambda p, k, half: pass_pe(MX, k))
            block2_pe()
            logits_pe(4, 6, G1 + E1, E2, 6 + EARLY)
            route2_pe(0, 6 + EARLY)
            pass_pe(M2[0], 0)
            odd_pe()
            logits_pe(6, 8, G1 + E1 + E2, E2)
            route2_pe(1)
            pass_pe(M2[1], 1)


_BIG = ["x", "ctx_2", "w_in", "w_out", "w_gate", "w_up", "w_down", "ada_w_2", "ada_b_2", "attn_w_in_2", "attn_w_out_2",
        "conv_w_in_2", "conv_w_out_2", "moe_w_gate_2", "moe_w_up_2", "moe_w_down_2"]


def layout(inputs):
    a = {n: np.asarray(v) for n, v in inputs.items()}
    f = np.float32
    pk = lambda v: v.reshape(P, KD)
    bf = np.zeros((P, KD), f)
    bf[:N_HEADS, 0] = a["b_forget"][0]
    b = a["ada_b_2"].reshape(2, 6, D)
    per = {"norm_mix": pk(a["norm_mix"][0]), "norm_ffn": pk(a["norm_ffn"][0]),
           "out_norm": pk(np.concatenate([a["out_norm_fox"][0], a["out_norm_dil"][0]])),
           "norm_mix0": pk(a["norm_mix_2"][0]), "norm_mix1": pk(a["norm_mix_2"][1]),
           "norm_ffn0": pk(a["norm_ffn_2"][0]), "norm_ffn1": pk(a["norm_ffn_2"][1]),
           "subln": pk(np.concatenate([a["attn_subln_2"][0]] * 6 + [np.ones(D - 6 * 2 * HD, f)])),
           "c": pk(a["c_2"][0]), "c_ctx": pk(a["c_ctx_2"]), "b_forget": bf}
    for l in range(2):
        for s in (SH_M, SC_M, SH_F, SC_F):
            per[f"b{l}{s}"] = pk(b[l, s])
    for j in range(3):
        per[f"conv{j}"] = a["conv_w_2"][0, j].reshape(KD, P).T
    every = [a[n][0] for n in ("q_norm_fox", "k_norm_fox", "q_norm_dil", "k_norm_dil", "attn_q_norm_2", "attn_k_norm_2",
                               "lam_q1_2", "lam_k1_2", "lam_q2_2", "lam_k2_2")]
    every += [a["b_router_group"][0], a["b_router_expert"][0].reshape(-1)]
    router = [a["w_router_group"][0], a["w_router_expert"][0].transpose(1, 0, 2).reshape(D, E1),
              a["router_w_2"][0], a["router_w_2"][1], a["w_in"][0][:, 6 * NC:]]
    return {"router": np.concatenate(router, 1), "const": CONST, "cols": np.concatenate([per[n] for n in COLS], 1),
            "rows": np.concatenate(every)[None, :]}


N_HEADS = 8


def kernel(**inputs):
    import concourse.bacc as _bacc
    from concourse.bass_utils import run_bass_kernel_spmd as _run

    nc = _bacc.Bacc("TRN2", target_bir_lowering=False, num_devices=1)
    arrays = {n: np.ascontiguousarray(inputs[n]) for n in _BIG}
    arrays.update({n: np.ascontiguousarray(v) for n, v in layout(inputs).items()})
    args = [nc.dram_tensor(f"in_{n}", a.shape, mybir.dt.from_np(a.dtype), kind="ExternalInput").ap() for n, a in arrays.items()]
    out = nc.dram_tensor("out", (1, S, D), F32, kind="ExternalOutput").ap()
    transformer_blocks(nc, *args, out)
    r = _run(nc, [{f"in_{n}": a for n, a in arrays.items()}], core_ids=[0])
    return r.results[0]["out"]
```
